# Optimizing a Trainium2 kernel written in Bass

```python
import jax, jax.numpy as jnp
from jax import lax
import numpy as np

D_MODEL = 1024
BATCH = 1
SEQ = 512
DEPTH = 1

RMS_EPS = 1e-5
HEAD_DIM = 64
ATT_HEADS = D_MODEL // HEAD_DIM
ATT_KV_HEADS = 4
WINDOW = 128
BLOCK = 128
ROT_DIM = HEAD_DIM // 4
ROPE_THETA = 500000.0
RWKV_HEAD_DIM = 64
RWKV_HEADS = D_MODEL // RWKV_HEAD_DIM
RWKV_WIDTH = RWKV_HEADS * RWKV_HEAD_DIM
DECAY_LORA = 64
AAA_LORA = 64
GATE_LORA = 128
RWKV_GN_EPS = 64e-5
MEM_LEN = 256
CROSS_HEADS = 4
CROSS_HEAD_DIM = 128
PEER_HEADS = 8
N_KEYS = 128
N_EXPERTS = N_KEYS * N_KEYS
PEER_QUERY_DIM = 256
PEER_TOPK = 16
PEER_CHUNK = 128
ATT_Q_WIDTH = ATT_HEADS * HEAD_DIM
ATT_KV_WIDTH = ATT_KV_HEADS * HEAD_DIM
RWKV_IN_WIDTH = 3 * RWKV_WIDTH + DECAY_LORA + AAA_LORA + GATE_LORA
GATE_WIDTH = 2 * D_MODEL
IN_WIDTH = ATT_Q_WIDTH + 2 * ATT_KV_WIDTH + RWKV_IN_WIDTH + GATE_WIDTH

kernel_name = 'hybrid_swa_rwkv7_peer_block'

def rms_norm(x, g):
    xf = x.astype(jnp.float32)
    y = xf * lax.rsqrt(jnp.mean(xf * xf, axis=-1, keepdims=True) + RMS_EPS)
    return (y * g.astype(jnp.float32)).astype(x.dtype)

def partial_rope(x, positions):
    half = ROT_DIM // 2
    inv_freq = 1.0 / (ROPE_THETA ** (jnp.arange(0, ROT_DIM, 2, dtype=jnp.float32) / ROT_DIM))
    ang = positions.astype(jnp.float32)[..., None] * inv_freq
    cos = jnp.cos(ang)[:, :, None, :]
    sin = jnp.sin(ang)[:, :, None, :]
    xr = x[..., :ROT_DIM].astype(jnp.float32)
    x1, x2 = xr[..., :half], xr[..., half:]
    rot = jnp.concatenate([x1 * cos - x2 * sin, x2 * cos + x1 * sin], axis=-1)
    return jnp.concatenate([rot.astype(x.dtype), x[..., ROT_DIM:]], axis=-1)

def sliding_window_attention(q, k, v, sinks):
    B, S = q.shape[0], q.shape[1]
    nb = S // BLOCK
    G = ATT_HEADS // ATT_KV_HEADS
    qb = q.reshape(B, nb, BLOCK, ATT_KV_HEADS, G, HEAD_DIM).transpose(1, 0, 2, 3, 4, 5)

    def band_keys(t):
        tb = t.reshape(B, nb, BLOCK, ATT_KV_HEADS, HEAD_DIM)
        prev = jnp.pad(tb, ((0, 0), (1, 0), (0, 0), (0, 0), (0, 0)))[:, :-1]
        return jnp.concatenate([prev, tb], axis=2).transpose(1, 0, 2, 3, 4)

    kw, vw = band_keys(k), band_keys(v)
    i = jnp.arange(BLOCK)[:, None]
    j = jnp.arange(2 * BLOCK)[None, :]
    band = (j > i) & (j <= i + WINDOW)
    sink = sinks.astype(jnp.float32).reshape(ATT_KV_HEADS, G)[None, :, :, None, None]
    scale = HEAD_DIM ** -0.5

    def one_block(args):
        qn, kn, vn, n = args
        s = jnp.einsum('bqkgd,bskd->bkgqs', qn.astype(jnp.float32), kn.astype(jnp.float32)) * scale
        valid = band & (n * BLOCK - BLOCK + j >= 0)
        s = jnp.where(valid, s, -1e30)
        m = jnp.maximum(jnp.max(s, axis=-1, keepdims=True), sink)
        p = jnp.exp(s - m)
        denom = jnp.sum(p, axis=-1, keepdims=True) + jnp.exp(sink - m)
        o = jnp.einsum('bkgqs,bskd->bqkgd', p / denom, vn.astype(jnp.float32))
        return o.astype(qn.dtype)

    out = lax.map(one_block, (qb, kw, vw, jnp.arange(nb)))
    return out.transpose(1, 0, 2, 3, 4, 5).reshape(B, S, ATT_HEADS * HEAD_DIM)

def rwkv7_time_mix(p, mu, w0, w2, a0, a2, g2, k_k, k_a, r_k, ln_w, ln_b):
    B, S = p.shape[0], p.shape[1]
    H, N, W = RWKV_HEADS, RWKV_HEAD_DIM, RWKV_WIDTH
    prev = jnp.pad(p, ((0, 0), (1, 0), (0, 0)))[:, :-1]
    p = p + (prev - p) * mu
    r = p[..., :W]
    k = p[..., W:2 * W]
    v = p[..., 2 * W:3 * W]
    dw = p[..., 3 * W:3 * W + DECAY_LORA]
    da = p[..., 3 * W + DECAY_LORA:3 * W + DECAY_LORA + AAA_LORA]
    dg = p[..., 3 * W + DECAY_LORA + AAA_LORA:]
    w_log = -jax.nn.softplus(-(w0 + jnp.tanh(dw) @ w2).astype(jnp.float32)) - 0.5
    decay = jnp.exp(-jnp.exp(w_log))
    a = jax.nn.sigmoid((a0 + da @ a2).astype(jnp.float32))
    g = jax.nn.sigmoid(dg) @ g2
    hs = lambda t: t.astype(jnp.float32).reshape(B, S, H, N)
    kk = hs(k * k_k)
    kk = kk / jnp.maximum(jnp.sqrt(jnp.sum(kk * kk, axis=-1, keepdims=True)), 1e-12)
    k = k.astype(jnp.float32) * (1.0 + (a - 1.0) * k_a.astype(jnp.float32))
    rh, kh, vh, wh, ah = hs(r), hs(k), hs(v), hs(decay), hs(a)

    def step(state, inp):
        r_t, w_t, k_t, v_t, kk_t, a_t = inp
        sa = jnp.einsum('bhij,bhj->bhi', state, -kk_t)
        state = (state * w_t[:, :, None, :]
                 + sa[..., :, None] * (kk_t * a_t)[:, :, None, :]
                 + v_t[..., :, None] * k_t[:, :, None, :])
        return state, jnp.einsum('bhij,bhj->bhi', state, r_t)

    tmaj = lambda t: t.transpose(1, 0, 2, 3)
    state0 = jnp.zeros((B, H, N, N), jnp.float32)
    _, o = lax.scan(step, state0, (tmaj(rh), tmaj(wh), tmaj(kh), tmaj(vh), tmaj(kk), tmaj(ah)))
    o = o.transpose(1, 0, 2, 3)
    mean = jnp.mean(o, axis=-1, keepdims=True)
    var = jnp.mean(jnp.square(o - mean), axis=-1, keepdims=True)
    on = ((o - mean) * lax.rsqrt(var + RWKV_GN_EPS)).reshape(B, S, W)
    on = on * ln_w.astype(jnp.float32) + ln_b.astype(jnp.float32)
    bonus = (jnp.sum(rh * kh * r_k.astype(jnp.float32), axis=-1, keepdims=True) * vh).reshape(B, S, W)
    return ((on + bonus) * g.astype(jnp.float32)).astype(p.dtype)

def memory_cross_attention(xn, mem_n, w_q, w_kv, w_o):
    B, S = xn.shape[0], xn.shape[1]
    M = mem_n.shape[1]
    q = (xn @ w_q).reshape(B, S, CROSS_HEADS, CROSS_HEAD_DIM)
    kv = (mem_n @ w_kv).reshape(B, M, 2, CROSS_HEADS, CROSS_HEAD_DIM)
    k, v = kv[:, :, 0], kv[:, :, 1]
    s = jnp.einsum('bshd,bmhd->bhsm', q.astype(jnp.float32), k.astype(jnp.float32)) * (CROSS_HEAD_DIM ** -0.5)
    pr = jax.nn.softmax(s, axis=-1)
    o = jnp.einsum('bhsm,bmhd->bshd', pr, v.astype(jnp.float32)).reshape(B, S, CROSS_HEADS * CROSS_HEAD_DIM)
    return o.astype(xn.dtype) @ w_o

def peer_ffn(xn, w_q, sub_keys_1, sub_keys_2, u, v):
    B, S, D = xn.shape
    half = PEER_QUERY_DIM // 2
    xc = xn.reshape((B * S) // PEER_CHUNK, PEER_CHUNK, D)
    k1 = sub_keys_1.astype(jnp.float32)
    k2 = sub_keys_2.astype(jnp.float32)

    def one_chunk(xt):
        q = (xt @ w_q).reshape(PEER_CHUNK, PEER_HEADS, PEER_QUERY_DIM).astype(jnp.float32)
        s1 = jnp.einsum('chd,nd->chn', q[..., :half], k1)
        s2 = jnp.einsum('chd,nd->chn', q[..., half:], k2)
        v1, i1 = lax.top_k(s1, PEER_TOPK)
        v2, i2 = lax.top_k(s2, PEER_TOPK)
        cand = (v1[..., :, None] + v2[..., None, :]).reshape(PEER_CHUNK, PEER_HEADS, PEER_TOPK * PEER_TOPK)
        sc, ci = lax.top_k(cand, PEER_TOPK)
        e = (jnp.take_along_axis(i1, ci // PEER_TOPK, axis=-1) * N_KEYS
             + jnp.take_along_axis(i2, ci % PEER_TOPK, axis=-1))
        gate = jax.nn.softmax(sc, axis=-1)
        act = jax.nn.gelu(jnp.einsum('cd,chkd->chk', xt, u[e]).astype(jnp.float32), approximate=False)
        return jnp.einsum('chk,chkd->cd', (gate * act).astype(xt.dtype), v[e])

    return lax.map(one_chunk, xc).reshape(B, S, D)

def hybrid_layer(h, mem, positions, g_mix, w_in, attn_sinks, rwkv_mu, rwkv_w0, rwkv_w2, rwkv_a0,
                 rwkv_a2, rwkv_g2, rwkv_k_k, rwkv_k_a, rwkv_r_k, rwkv_ln_w, rwkv_ln_b, w_out,
                 g_cross, g_mem, w_q_cross, w_kv_cross, w_o_cross, g_ffn, peer_w_q,
                 peer_sub_keys_1, peer_sub_keys_2, peer_u, peer_v):
    B, S = h.shape[0], h.shape[1]
    xn = rms_norm(h, g_mix)
    proj = xn @ w_in
    o1 = ATT_Q_WIDTH
    o2 = o1 + ATT_KV_WIDTH
    o3 = o2 + ATT_KV_WIDTH
    o4 = o3 + RWKV_IN_WIDTH
    q = partial_rope(proj[..., :o1].reshape(B, S, ATT_HEADS, HEAD_DIM), positions)
    k = partial_rope(proj[..., o1:o2].reshape(B, S, ATT_KV_HEADS, HEAD_DIM), positions)
    v = proj[..., o2:o3].reshape(B, S, ATT_KV_HEADS, HEAD_DIM)
    attn = sliding_window_attention(q, k, v, attn_sinks)
    rwkv = rwkv7_time_mix(proj[..., o3:o4], rwkv_mu, rwkv_w0, rwkv_w2, rwkv_a0, rwkv_a2, rwkv_g2,
                          rwkv_k_k, rwkv_k_a, rwkv_r_k, rwkv_ln_w, rwkv_ln_b)
    gates = jax.nn.sigmoid(proj[..., o4:])
    mixed = gates[..., :D_MODEL] * attn + gates[..., D_MODEL:] * rwkv
    h = h + mixed @ w_out
    h = h + memory_cross_attention(rms_norm(h, g_cross), rms_norm(mem, g_mem), w_q_cross, w_kv_cross, w_o_cross)
    h = h + peer_ffn(rms_norm(h, g_ffn), peer_w_q, peer_sub_keys_1, peer_sub_keys_2, peer_u, peer_v)
    return h

def setup_inputs(seed: int = 0) -> dict:
    key = jax.random.key(seed)
    ks = jax.random.split(key, 32)
    f32 = jnp.float32
    nrm = lambda i, shape, s: jax.random.normal(ks[i], shape, f32) * s
    L, D = DEPTH, D_MODEL
    half = PEER_QUERY_DIM // 2
    offsets = jax.random.randint(ks[2], (BATCH, 1), 0, 4096, dtype=jnp.int32)
    return {
        'x': nrm(0, (BATCH, SEQ, D), 1.0),
        'mem': nrm(1, (BATCH, MEM_LEN, D), 1.0),
        'positions': offsets + jnp.arange(SEQ, dtype=jnp.int32)[None, :],
        'g_mix': 1.0 + nrm(3, (L, D), 0.02),
        'w_in': nrm(4, (L, D, IN_WIDTH), D ** -0.5),
        'attn_sinks': nrm(5, (L, ATT_HEADS), 0.5),
        'rwkv_mu': jax.random.uniform(ks[6], (L, RWKV_IN_WIDTH), f32),
        'rwkv_w0': -0.5 + nrm(7, (L, RWKV_WIDTH), 0.5),
        'rwkv_w2': nrm(8, (L, DECAY_LORA, RWKV_WIDTH), 0.1),
        'rwkv_a0': nrm(9, (L, RWKV_WIDTH), 0.1),
        'rwkv_a2': nrm(10, (L, AAA_LORA, RWKV_WIDTH), 0.1),
        'rwkv_g2': nrm(11, (L, GATE_LORA, RWKV_WIDTH), GATE_LORA ** -0.5),
        'rwkv_k_k': 0.85 + nrm(12, (L, RWKV_WIDTH), 0.02),
        'rwkv_k_a': 1.0 + nrm(13, (L, RWKV_WIDTH), 0.02),
        'rwkv_r_k': nrm(14, (L, RWKV_HEADS, RWKV_HEAD_DIM), 0.1),
        'rwkv_ln_w': 1.0 + nrm(15, (L, RWKV_WIDTH), 0.02),
        'rwkv_ln_b': nrm(16, (L, RWKV_WIDTH), 0.02),
        'w_out': nrm(17, (L, D, D), D ** -0.5),
        'g_cross': 1.0 + nrm(18, (L, D), 0.02),
        'g_mem': 1.0 + nrm(19, (L, D), 0.02),
        'w_q_cross': nrm(20, (L, D, CROSS_HEADS * CROSS_HEAD_DIM), D ** -0.5),
        'w_kv_cross': nrm(21, (L, D, 2 * CROSS_HEADS * CROSS_HEAD_DIM), D ** -0.5),
        'w_o_cross': nrm(22, (L, CROSS_HEADS * CROSS_HEAD_DIM, D), (CROSS_HEADS * CROSS_HEAD_DIM) ** -0.5),
        'g_ffn': 1.0 + nrm(23, (L, D), 0.02),
        'peer_w_q': nrm(24, (L, D, PEER_HEADS * PEER_QUERY_DIM), D ** -0.5),
        'peer_sub_keys_1': nrm(25, (L, N_KEYS, half), half ** -0.5),
        'peer_sub_keys_2': nrm(26, (L, N_KEYS, half), half ** -0.5),
        'peer_u': nrm(27, (L, N_EXPERTS, D), D ** -0.5),
        'peer_v': nrm(28, (L, N_EXPERTS, D), PEER_HEADS ** -0.5),
        'g_final': 1.0 + nrm(29, (D,), 0.02),
    }

def reference(x, mem, positions, g_mix, w_in, attn_sinks, rwkv_mu, rwkv_w0, rwkv_w2, rwkv_a0,
              rwkv_a2, rwkv_g2, rwkv_k_k, rwkv_k_a, rwkv_r_k, rwkv_ln_w, rwkv_ln_b, w_out,
              g_cross, g_mem, w_q_cross, w_kv_cross, w_o_cross, g_ffn, peer_w_q,
              peer_sub_keys_1, peer_sub_keys_2, peer_u, peer_v, g_final):
    h = x
    for layer in range(DEPTH):
        h = hybrid_layer(h, mem, positions, g_mix[layer], w_in[layer], attn_sinks[layer],
                         rwkv_mu[layer], rwkv_w0[layer], rwkv_w2[layer], rwkv_a0[layer],
                         rwkv_a2[layer], rwkv_g2[layer], rwkv_k_k[layer], rwkv_k_a[layer],
                         rwkv_r_k[layer], rwkv_ln_w[layer], rwkv_ln_b[layer], w_out[layer],
                         g_cross[layer], g_mem[layer], w_q_cross[layer], w_kv_cross[layer],
                         w_o_cross[layer], g_ffn[layer], peer_w_q[layer],
                         peer_sub_keys_1[layer], peer_sub_keys_2[layer], peer_u[layer], peer_v[layer])
    return rms_norm(h, g_final)


_drawn_inputs = setup_inputs


def setup_inputs(seed=0):
    import zlib

    import numpy as np

    out = dict(_drawn_inputs(seed))
    spreads = {}
    factors = {'g_mix': 2.691,
     'attn_sinks': 8.0,
     'rwkv_k_k': 44.916,
     'rwkv_k_a': 3.467,
     'rwkv_ln_w': 3.957,
     'rwkv_ln_b': 4.151,
     'g_cross': 7.198,
     'g_mem': 5.687,
     'g_final': 8.595,
     'g_ffn': 8.0}
    for name, (base, spread) in spreads.items():
        noise = np.random.default_rng([zlib.crc32(name.encode()), seed]).standard_normal(out[name].shape)
        drawn = base * np.exp(spread * noise) if base else spread * noise
        out[name] = __import__('jax').numpy.asarray(drawn.astype(out[name].dtype))
    for name, factor in factors.items():
        out[name] = (out[name] * factor).astype(out[name].dtype)
    return out
```

```python
from contextlib import ExitStack

import numpy as np

import concourse.bass as bass
from concourse import mybir

F32 = mybir.dt.float32
I32 = mybir.dt.int32
U32 = mybir.dt.uint32
ALU = mybir.AluOpType
ACT = mybir.ActivationFunctionType
AX = mybir.AxisListType.X

P = 128
D = 1024
SEQ = 512
TT = SEQ // P
KD = D // P
HEAD = 64
HEADS = 16
KV = 4
CH = 64
NCH = SEQ // CH
MEM = 256
CROSS_W = 512
CROSS_H = 4
PH = 8
TOPK = 16
NKEYS = 128
EPS = 1e-5
GN_EPS = 64e-5
SQE = float(np.exp(-0.5))
TWO_PI = 2.0 * np.pi
OFF_K = 1024
OFF_RWKV = 1536
OFF_LOW = OFF_RWKV + 3 * D
OFF_GATE = OFF_LOW + 256
IN_W = OFF_GATE + 2 * D
NEG = -1e30

C_ID, C_BONES, C_ROT, C_MASK, C_BAND, C_RESET, C_IOTA, C_INVF, C_END = 0, 128, 256, 384, 640, 896, 1408, 1664, 1672

R_MU, R_W0, R_A0, R_KK, R_KA, R_RK, R_LNW, R_LNB, R_GMIX, R_GCROSS, R_GFFN, R_GMEM, R_MULOW = (
    0, 24, 32, 40, 48, 56, 64, 72, 80, 88, 96, 104, 112)
R_END = 114


def constants():
    c = np.zeros((P, C_END), np.float32)
    p = np.arange(P)
    c[:, C_ID:C_ID + P] = np.eye(P)
    c[:, C_BONES:C_BONES + P] = (p[:, None] // HEAD == p[None, :] // HEAD)
    for m in range(P):
        d = m % HEAD
        if d < 8:
            c[m + 8, C_ROT + m] = -1.0
        elif d < 16:
            c[m - 8, C_ROT + m] = 1.0
    s, t = (p % CH)[:, None], np.arange(CH)[None, :]
    for n, m in enumerate([s < t, -1.0 * (s <= t), s < t, s <= t]):
        c[:, C_MASK + n * CH:C_MASK + (n + 1) * CH] = m
    j = np.arange(2 * P)[None, :]
    c[:, C_BAND:C_BAND + 2 * P] = np.where((j > p[:, None]) & (j <= p[:, None] + P), 0.0, NEG)
    c[:, C_RESET:C_RESET + SEQ] = (np.arange(SEQ) % CH != 0)
    c[:, C_IOTA:C_IOTA + 256] = np.arange(256)
    inv = (1.0 / (np.float32(500000.0) ** (np.arange(0, 16, 2, dtype=np.float32) / np.float32(16)))).astype(np.float32)
    d = p % HEAD
    c[:, C_INVF] = np.where(d < 16, inv[d % 8], 0.0)
    return c


def build(nc, x, mem, positions, g_mix, w_in, attn_sinks, rwkv_mu, rwkv_w0, rwkv_w2, rwkv_a0, rwkv_a2, rwkv_g2,
          rwkv_k_k, rwkv_k_a, rwkv_r_k, rwkv_ln_w, rwkv_ln_b, w_out, g_cross, g_mem, w_q_cross, w_kv_cross,
          w_o_cross, g_ffn, peer_w_q, peer_sub_keys_1, peer_sub_keys_2, peer_u, peer_v, g_final, const, out,
          scratch="Internal", last=9):
    ctx = ExitStack()

    stage_sems = []

    def sem(name):
        stage_sems.append(nc.alloc_semaphore(name))
        return stage_sems[-1]

    gone_on = nc.alloc_semaphore("gone_on")

    def end_stage():
        nc.clear_and_free_semaphores(list(stage_sems))
        stage_sems.clear()
        nc.all_engine_barrier()

    def sb(name, shape, dt=F32):
        return nc.alloc_sbuf_tensor(name, shape, dt)

    def dram(name, shape):
        return nc.dram_tensor(name, shape, F32, kind=scratch).ap()

    bank = [nc.alloc_psum_tensor(f"bank{i}", [P, 512], F32) for i in range(8)]

    tok_dram = dram("tok_dram", [KD, P, 4 * SEQ])
    mats_dram = dram("mats_dram", [KD, P, 2 * 4 * 4 * CH])
    rho_dram = dram("rho_dram", [KD, P, SEQ])
    bonus_dram = dram("bonus_dram", [KD, P, SEQ])
    low_dram = dram("low_dram", [HEADS, 4, 2, CH, CH])
    inv_dram = dram("inv_dram", [HEADS, 4, 2, CH, CH])

    cst = sb("cst", [P, C_END])
    prm = sb("prm", [P, P])
    xnT = sb("xnT", [P, KD, SEQ])
    sdg = sb("sdg", [P, SEQ])
    decay_end = sb("decay_end", [P, KD, NCH])
    ident = cst[:, C_ID:C_ID + P]
    bones = cst[:, C_BONES:C_BONES + P]

    def col(row, m):
        if isinstance(m, int):
            return prm[:, row + m:row + m + 1]
        return prm[:, bass.ds(m + row, 1)]

    class Arena:

        def __init__(self):
            self.stack = ExitStack()

        def __call__(self, name, shape, dt=F32):
            return self.stack.enter_context(nc.sbuf_tensor(name, shape, dt))

        def free(self):
            self.stack.close()

    def norm_transpose(block, tag, src, n, width_row, xn, dstT, ready, ready_at, banks):
        ss, ms, rt, rs = (small[:, 8 * i:8 * i + n] for i in range(4))
        squared, scaled, rooted, normed, turned, evac = (sem(f"{tag}_{s}") for s in (
            "squared", "scaled", "rooted", "normed", "turned", "evac"))

        @block.scalar
        def _(act):
            if ready is not None:
                act.wait_ge(ready, ready_at)
            for t in range(n):
                nc.scalar.activation(xn[:, t], src[:, t], ACT.Square, accum_out=ss[:, t:t + 1]).then_inc(squared, 1)
            act.wait_ge(scaled, 1)
            nc.scalar.activation(rt, ms, ACT.Sqrt).then_inc(rooted, 1)

        @block.vector
        def _(dve):
            dve.wait_ge(squared, n)
            nc.vector.tensor_scalar(ms, ss, 1.0 / D, EPS, ALU.mult, ALU.add).then_inc(scaled, 1)
            dve.wait_ge(rooted, 1)
            nc.vector.reciprocal(rs, rt).then_inc(scaled, 1)
            dve.wait_ge(scaled, 2)
            for t in range(n):
                nc.vector.tensor_scalar(xn[:, t], src[:, t], rs[:, t:t + 1], None, ALU.mult).then_inc(normed, 1)

        @block.tensor
        def _(pe):
            pe.wait_ge(normed, n)
            for k in range(KD):
                if k >= 2:
                    pe.wait_ge(evac, k - 1)
                for t in range(n):
                    mm = nc.tensor.transpose(banks[k % 2][:, t * P:(t + 1) * P], xn[:, t, k * P:(k + 1) * P], ident)
                mm.then_inc(turned, 1)

        @block.scalar
        def _(act):
            for k in range(KD):
                act.wait_ge(turned, k + 1)
                nc.scalar.activation(dstT[:, k, 0:n * P], banks[k % 2][:, 0:n * P], ACT.Copy,
                                     scale=col(width_row, k)).then_inc(evac, 1)
        return evac, KD

    small = sb("small", [P, 64])

    def peek(name, t):
        if scratch == "Internal":
            return
        d = nc.dram_tensor("peek_" + name, list(t.shape), F32, kind="ExternalOutput").ap()
        s = sem("peek_" + name)
        with nc.Block() as block:
            @block.sync
            def _(sp):
                sp.dma_start(d, t).then_inc(s, 16)
                sp.wait_ge(s, 16)

    a0 = Arena()
    xt = a0("xt", [P, TT, D])
    xn0 = a0("xn0", [P, TT, D])
    rows = a0("rows", [P, P])
    x_in, params_in, rows_turned, prm_ready = sem("x_in"), sem("params_in"), sem("rows_turned"), sem("prm_ready")
    x_tok = x.rearrange("b (t p) d -> p (b t) d", p=P)
    with nc.Block() as block:
        @block.vector
        def _(dve):
            nc.vector.memset(rows[:, :], 0.0).then_inc(prm_ready, 1)

        @block.sync
        def _(sp):
            sp.dma_start(cst[:, :], const).then_inc(params_in, 16)
            sp.dma_start(xt[:, :, :], x_tok).then_inc(x_in, 16)
            sp.wait_ge(prm_ready, 1)
            params = [(R_MU, rwkv_mu[0, 0:3 * D]), (R_W0, rwkv_w0[0]), (R_A0, rwkv_a0[0]), (R_KK, rwkv_k_k[0]),
                      (R_KA, rwkv_k_a[0]), (R_RK, rwkv_r_k[0].rearrange("h n -> (h n)")), (R_LNW, rwkv_ln_w[0]),
                      (R_LNB, rwkv_ln_b[0]), (R_GMIX, g_mix[0]), (R_GCROSS, g_cross[0]), (R_GFFN, g_ffn[0]),
                      (R_GMEM, g_mem[0]), (R_MULOW, rwkv_mu[0, 3 * D:3 * D + 256])]
            for row, vec in params:
                v = vec.rearrange("(m p) -> m p", p=P)
                sp.dma_start(rows[row:row + v.shape[0], :], v).then_inc(params_in, 16)

        @block.tensor
        def _(pe):
            pe.wait_ge(params_in, 16 * 14)
            nc.tensor.transpose(bank[7][:, 0:P], rows[:, :], ident).then_inc(rows_turned, 1)

        @block.vector
        def _(dve):
            dve.wait_ge(rows_turned, 1)
            nc.vector.tensor_copy(prm[:, :], bank[7][:, 0:P]).then_inc(prm_ready, 1)

        @block.scalar
        def _(act):
            act.wait_ge(prm_ready, 2)
        norm_transpose(block, "nx", xt, TT, R_GMIX, xn0, xnT, x_in, 16, bank[0:2])
    a0.free()
    if last < 1:
        return

    a1 = Arena()
    lowT = a1("lowT", [P, SEQ])
    w_low = a1("w_low", [P, KD, 256])
    w3 = a1("w3", [P, 2, 3, KD, P])
    w_up = a1("w_up", [P, 2, P])
    raw = a1("raw", [P, 2, 3, SEQ + 1])
    sh = a1("sh", [P, 2, 3, SEQ])
    dlt = a1("dlt", [P, 3, SEQ])
    sgw, sga, cum, csub, pe_, pi_, pp_, kk, kk2, nrm, bonin, kap, bet, kh, bh, k2, bv = (
        a1(n, [P, 2, SEQ]) for n in ("sgw", "sga", "cum", "csub", "p_end", "p_inv", "p_prev", "kk", "kk2", "nrm",
                                     "bonin", "kap", "bet", "kh", "bh", "k2", "bv"))
    ar = a1("ar", [P, 2, 2, SEQ])
    tok = a1("tok", [P, 2, 4, SEQ])
    mats = a1("mats", [P, 2, 2, 4, 4 * CH])

    w_cols = w_in[0].rearrange("(k p) c -> p k c", p=P)
    low_w_in, low_mm, low_raw, low_chain, low_done = (sem(s) for s in (
        "low_w_in", "low_mm", "low_raw", "low_chain", "low_done"))
    w3_in = [sem("w3_in0"), sem("w3_in1")]
    (pj_full, pj_free, za_full, za_free, sb_full, sb_free, g_full, g_free, t_full, t_free, raw_zero,
     dve_done, act_done, out_free, cum_ready, exps_ready, kk_ready, kk2_ready, nrm_ready, bon_ready,
     ops_ready, turn_ready, gates_ready, raw_ready, mats_ready, tok_ready, bv_ready, chain) = (sem(s) for s in (
         "pj_full", "pj_free", "za_full", "za_free", "sb_full", "sb_free", "g_full", "g_free", "t_full",
         "t_free", "raw_zero", "dve_done", "act_done", "out_free", "cum_ready", "exps_ready", "kk_ready",
         "kk2_ready", "nrm_ready", "bon_ready", "ops_ready", "turn_ready", "gates_ready", "raw_ready",
         "mats_ready", "tok_ready", "bv_ready", "chain"))
    store = [sem("store0"), sem("store1")]
    with nc.Block() as block:
        @block.sync
        def _(sp):
            sp.dma_start(w_low[:, :, :], w_cols[:, :, OFF_LOW:OFF_LOW + 256]).then_inc(low_w_in, 16)
            with sp.Fori(0, KD // 2) as i:
                for k in range(2):
                    m = i * 2 + k
                    sp.wait_ge(ops_ready, m + 1)
                    sp.dma_start(rho_dram[bass.ds(m, 1)].rearrange("a p s -> (a p) s"), ar[:, k, 1, :]).then_inc(store[k], 16)
                    sp.wait_ge(bv_ready, m + 1)
                    sp.dma_start(bonus_dram[bass.ds(m, 1)].rearrange("a p s -> (a p) s"), bv[:, k, :]).then_inc(store[k], 16)
                    sp.wait_ge(mats_ready, m * 4 + 4)
                    sp.dma_start(mats_dram[bass.ds(m, 1)].rearrange("a p s -> (a p) s"),
                                 mats[:, k, :, :, :].rearrange("p h c n -> p (h c n)")).then_inc(store[k], 16)
                    for par in range(2):
                        sp.dma_start(
                            low_dram[bass.ds(m * 2, 2), :, par].rearrange("h c s t -> s (h c) t"),
                            mats[par * CH:(par + 1) * CH, k, :, :, 0:CH].rearrange("p h c n -> p (h c) n")).then_inc(store[k], 16)
                    sp.wait_ge(tok_ready, m * 4 + 4)
                    sp.dma_start(tok_dram[bass.ds(m, 1)].rearrange("a p s -> (a p) s"),
                                 tok[:, k, :, :].rearrange("p a s -> p (a s)")).then_inc(store[k], 16)
                    sp.wait_ge(store[k], i * 96 + 96)
                    sp.sem_inc(out_free, 1)

        @block.gpsimd
        def _(pool):
            with pool.Fori(0, KD // 2) as i:
                for k in range(2):
                    m = i * 2 + k
                    pool.wait_ge(za_full, m * 2 + 2)
                    for t in range(3):
                        pool.dma_start(w3[:, k, t, :, :], w_cols[:, :, bass.ds(m * P + (OFF_RWKV + t * D), P)]).then_inc(w3_in[k], 16)
                    pool.dma_start(w_up[0:64, k, :], rwkv_w2[0][:, bass.ds(m * P, P)]).then_inc(w3_in[k], 16)
                    pool.dma_start(w_up[64:128, k, :], rwkv_a2[0][:, bass.ds(m * P, P)]).then_inc(w3_in[k], 16)

        @block.tensor
        def _(pe):
            pe.sem_inc(za_full, 4)
            pe.sem_inc(t_full, 8)
            pe.wait_ge(low_w_in, 16)
            for t in range(2):
                for k in range(KD):
                    mm = nc.tensor.matmul(bank[2 + t][:, :], w_low[:, k, t * P:(t + 1) * P], xnT[:, k, :],
                                          start=(k == 0), stop=(k == KD - 1))
                mm.then_inc(low_mm, 1)

            def project(m, i, k, t):
                pe.wait_ge(pj_free, m * 3 + t + 1)
                for d in range(KD):
                    mm = nc.tensor.matmul(bank[(3 * k + t) % 2][:, :], w3[:, k, t, d, :], xnT[:, d, :],
                                          start=(d == 0), stop=(d == KD - 1))
                mm.then_inc(pj_full, 1)

            def up(m, k):
                for t in range(2):
                    pe.wait_ge(za_free, m * 2 + t + 1)
                    r = slice(64 * t, 64 * t + 64)
                    nc.tensor.matmul(bank[2][:, :], w_up[r, k, :], lowT[r, :], start=True, stop=True).then_inc(za_full, 1)

            def head_sums(m, k):
                pe.wait_ge(kk2_ready, m + 1)
                pe.wait_ge(sb_free, m * 2 + 1)
                nc.tensor.matmul(bank[3][:, :], bones, kk2[:, k, :], start=True, stop=True).then_inc(sb_full, 1)
                pe.wait_ge(bon_ready, m + 1)
                pe.wait_ge(sb_free, m * 2 + 2)
                nc.tensor.matmul(bank[3][:, :], bones, bonin[:, k, :], start=True, stop=True).then_inc(sb_full, 1)

            def chunk_products(m, k):
                pe.wait_ge(ops_ready, m + 1)
                for qq in range(2):
                    for h in range(2):
                        pe.wait_ge(g_free, m * 4 + 2 * qq + h + 1)
                        pe.sem_inc(gone_on, 1)
                        hb = slice(64 * h, 64 * h + 64)
                        for c in range(4 * qq, 4 * qq + 4):
                            cb = slice(64 * (c % 2), 64 * (c % 2) + 64)
                            t = slice(c * CH, (c + 1) * CH)
                            for n, left in enumerate((bet, kap)):
                                at = (c // 2 % 2) * 256 + n * 128
                                o = bank[4 + h][cb, at:at + 128]
                                mm = nc.tensor.matmul(o.rearrange("p (a t) -> p a t", a=2), left[hb, k, t],
                                                      ar[hb, k, :, t], start=True, stop=True)
                        mm.then_inc(g_full, 1)

            def turns(m, k):
                pe.wait_ge(turn_ready, m + 1)
                for a, src in enumerate((ar[:, k, 0, :], sh[:, k, 2, :], kh[:, k, :], bh[:, k, :])):
                    pe.wait_ge(t_free, m * 4 + a + 1)
                    for t in range(TT):
                        mm = nc.tensor.transpose(bank[6 + a % 2][:, t * P:(t + 1) * P], src[:, t * P:(t + 1) * P], ident)
                    mm.then_inc(t_full, 1)

            def step(m, i, k, nxt, i2, k2_):
                pe.wait_ge(w3_in[k2_], i2 * 80 + 80)
                project(nxt, i2, k2_, 0)
                head_sums(m, k)
                project(nxt, i2, k2_, 1)
                project(nxt, i2, k2_, 2)
                up(nxt, k2_)
                chunk_products(m, k)
                turns(m, k)

            pe.wait_ge(low_done, 3)
            pe.wait_ge(w3_in[0], 80)
            for t in range(3):
                project(0, 0, 0, t)
            up(0, 0)
            with pe.Fori(0, KD // 2 - 1) as i:
                step(i * 2, i, 0, i * 2 + 1, i, 1)
                step(i * 2 + 1, i, 1, i * 2 + 2, i + 1, 0)
            step(KD - 2, 0, 0, KD - 1, KD // 2 - 1, 1)
            head_sums(KD - 1, 1)
            chunk_products(KD - 1, 1)
            turns(KD - 1, 1)

        @block.scalar
        def _(act):
            act.sem_inc(pj_free, 2)
            act.sem_inc(za_free, 1)
            act.sem_inc(t_free, 2)
            act.sem_inc(act_done, 2)
            act.wait_ge(raw_zero, 1)
            for t in range(2):
                act.wait_ge(low_mm, t + 1)
                nc.scalar.activation(raw[:, 0, t, 1:SEQ + 1], bank[2 + t][:, :], ACT.Copy).then_inc(low_raw, 1)
            act.wait_ge(low_chain, 4)
            nc.scalar.activation(lowT[0:64, :], sh[0:64, 0, 0, :], ACT.Tanh).then_inc(low_done, 1)
            nc.scalar.activation(lowT[64:128, :], sh[64:128, 0, 0, :], ACT.Copy).then_inc(low_done, 1)
            nc.scalar.activation(sdg[:, :], sh[:, 0, 1, :], ACT.Sigmoid).then_inc(low_done, 1)
            act.wait_ge(low_done, 3)
            def evac_raw(m, k, t):
                act.wait_ge(pj_full, m * 3 + t + 1)
                nc.scalar.activation(raw[:, k, t, 1:SEQ + 1], bank[(3 * k + t) % 2][:, :], ACT.Copy).then_inc(raw_ready, 1)
                act.wait_ge(raw_ready, m * 3 + t + 1)
                act.sem_inc(pj_free, 1)

            def gates(m, k):
                for t, (dst, bias) in enumerate(((sgw, R_W0), (sga, R_A0))):
                    act.wait_ge(za_full, m * 2 + t + 5)
                    nc.scalar.activation(dst[:, k, :], bank[2][:, :], ACT.Sigmoid, bias=col(bias, m)).then_inc(gates_ready, 1)
                    act.wait_ge(gates_ready, m * 2 + t + 1)
                    act.sem_inc(za_free, 1)

            def exps(m, k):
                act.wait_ge(kk_ready, m + 1)
                nc.scalar.activation(kk2[:, k, :], kk[:, k, :], ACT.Square).then_inc(kk2_ready, 1)
                act.wait_ge(cum_ready, m + 1)
                nc.scalar.activation(pe_[:, k, :], cum[:, k, :], ACT.Exp, scale=-SQE).then_inc(exps_ready, 1)
                nc.scalar.activation(pi_[:, k, :], cum[:, k, :], ACT.Exp, scale=SQE).then_inc(exps_ready, 1)
                nc.scalar.activation(pp_[:, k, :], csub[:, k, :], ACT.Exp, scale=-SQE).then_inc(exps_ready, 1)

            def norm_root(m, k):
                act.wait_ge(sb_full, m * 2 + 1)
                nc.scalar.activation(nrm[:, k, :], bank[3][:, :], ACT.Sqrt).then_inc(nrm_ready, 1)

            def evac_turns(m, k):
                act.wait_ge(out_free, m + 1)
                for a in range(4):
                    act.wait_ge(t_full, m * 4 + a + 9)
                    nc.scalar.activation(tok[:, k, a, :], bank[6 + a % 2][:, :], ACT.Copy).then_inc(tok_ready, 1)
                    act.wait_ge(tok_ready, m * 4 + a + 1)
                    act.sem_inc(t_free, 1)
                act.sem_inc(act_done, 1)

            def front(m, k, m_before=None, k_before=None):
                act.wait_ge(dve_done, m + 1)
                evac_raw(m, k, 0)
                if m_before is not None:
                    norm_root(m_before, k_before)
                evac_raw(m, k, 1)
                evac_raw(m, k, 2)
                gates(m, k)
                if m_before is not None:
                    evac_turns(m_before, k_before)
                act.wait_ge(t_full, m * 4 + 4)
                exps(m, k)

            front(0, 0)
            with act.Fori(0, KD // 2 - 1) as i:
                front(i * 2 + 1, 1, i * 2, 0)
                front(i * 2 + 2, 0, i * 2 + 1, 1)
            front(KD - 1, 1, KD - 2, 0)
            norm_root(KD - 1, 1)
            evac_turns(KD - 1, 1)

        LINKS = 19

        @block.vector
        def _(dve):
            dve.sem_inc(dve_done, 2)
            dve.sem_inc(sb_free, 1)
            dve.sem_inc(g_free, 2)
            dve.sem_inc(out_free, 2)
            nc.vector.memset(raw[:, :, :, 0:1], 0.0).then_inc(raw_zero, 1)
            dve.wait_ge(raw_zero, 1)
            for t in range(2):
                dve.wait_ge(low_raw, t + 1)
                nc.vector.tensor_tensor(dlt[:, t, :], raw[:, 0, t, 0:SEQ], raw[:, 0, t, 1:SEQ + 1], ALU.subtract).then_inc(low_chain, 1)
                dve.wait_ge(low_chain, 2 * t + 1)
                nc.vector.scalar_tensor_tensor(out=sh[:, 0, t, :], in0=dlt[:, t, :], scalar=col(R_MULOW, t),
                                               in1=raw[:, 0, t, 1:SEQ + 1], op0=ALU.mult, op1=ALU.add).then_inc(low_chain, 1)
            dve.wait_ge(low_done, 3)
            with dve.Fori(0, KD // 2) as i:
                for k in range(2):
                    m = i * 2 + k
                    count = [0]

                    def link(ins):
                        count[0] += 1
                        ins.then_inc(chain, 1)
                        dve.wait_ge(chain, m * LINKS + count[0])

                    dve.wait_ge(t_full, m * 4 + 4)
                    dve.wait_ge(act_done, m + 1)
                    dve.wait_ge(out_free, m + 1)
                    r_, k_, v_ = (sh[:, k, t, :] for t in range(3))
                    alpha, rho = ar[:, k, 0, :], ar[:, k, 1, :]
                    for t in (1, 0, 2):
                        dve.wait_ge(raw_ready, m * 3 + t + 1)
                        link(nc.vector.tensor_tensor(dlt[:, t, :], raw[:, k, t, 0:SEQ], raw[:, k, t, 1:SEQ + 1], ALU.subtract))
                        link(nc.vector.scalar_tensor_tensor(out=sh[:, k, t, :], in0=dlt[:, t, :], scalar=col(R_MU + 8 * t, m),
                                                            in1=raw[:, k, t, 1:SEQ + 1], op0=ALU.mult, op1=ALU.add))
                        if t == 1:
                            link(nc.vector.tensor_scalar(kk[:, k, :], k_, col(R_KK, m), None, ALU.mult))
                            dve.sem_inc(kk_ready, 1)
                    dve.wait_ge(gates_ready, m * 2 + 1)
                    link(nc.vector.tensor_tensor_scan(cum[:, k, :], cst[:, C_RESET:C_RESET + SEQ], sgw[:, k, :], 0.0, ALU.mult, ALU.add))
                    link(nc.vector.tensor_tensor(csub[:, k, :], cum[:, k, :], sgw[:, k, :], ALU.subtract))
                    dve.sem_inc(cum_ready, 1)
                    dve.wait_ge(gates_ready, m * 2 + 2)
                    link(nc.vector.tensor_scalar(k2[:, k, :], sga[:, k, :], 1.0, col(R_KA, m), ALU.subtract, ALU.mult))
                    link(nc.vector.scalar_tensor_tensor(out=k2[:, k, :], in0=k2[:, k, :], scalar=1.0, in1=k_, op0=ALU.add, op1=ALU.mult))
                    link(nc.vector.scalar_tensor_tensor(out=bonin[:, k, :], in0=r_, scalar=col(R_RK, m), in1=k2[:, k, :],
                                                        op0=ALU.mult, op1=ALU.mult))
                    dve.sem_inc(bon_ready, 1)
                    dve.wait_ge(nrm_ready, m + 1)
                    dve.sem_inc(sb_free, 1)
                    link(nc.vector.tensor_scalar(nrm[:, k, :], nrm[:, k, :], 1e-12, None, ALU.max))
                    link(nc.vector.reciprocal(nrm[:, k, :], nrm[:, k, :]))
                    link(nc.vector.tensor_tensor(kk[:, k, :], kk[:, k, :], nrm[:, k, :], ALU.mult))
                    dve.wait_ge(exps_ready, m * 3 + 3)
                    nc.vector.tensor_copy(decay_end[:, bass.ds(m, 1), :].rearrange("p a c -> p (a c)"), pe_[:, k, CH - 1::CH])
                    nc.vector.tensor_tensor(alpha, kk[:, k, :], pp_[:, k, :], ALU.mult)
                    nc.vector.tensor_tensor(rho, r_, pe_[:, k, :], ALU.mult)
                    link(nc.vector.tensor_tensor(bet[:, k, :], kk[:, k, :], sga[:, k, :], ALU.mult))
                    nc.vector.tensor_tensor(kap[:, k, :], k2[:, k, :], pi_[:, k, :], ALU.mult)
                    link(nc.vector.tensor_tensor(bet[:, k, :], bet[:, k, :], pi_[:, k, :], ALU.mult))
                    dve.sem_inc(ops_ready, 1)
                    chunks = lambda t: t[:, k, :].rearrange("p (c t) -> p c t", t=CH)
                    last_decay = chunks(pe_)[:, :, CH - 1:CH].broadcast_to([P, NCH, CH])
                    nc.vector.tensor_tensor(chunks(kh), chunks(kap), last_decay, ALU.mult)
                    link(nc.vector.scalar_tensor_tensor(out=chunks(bh), in0=chunks(bet), scalar=-1.0, in1=last_decay,
                                                        op0=ALU.mult, op1=ALU.mult))
                    dve.sem_inc(turn_ready, 1)
                    dve.wait_ge(sb_full, m * 2 + 2)
                    link(nc.vector.tensor_tensor(bv[:, k, :], bank[3][:, :], v_, ALU.mult))
                    dve.sem_inc(sb_free, 1)
                    dve.sem_inc(bv_ready, 1)
                    mask = cst[:, C_MASK:C_MASK + 256]
                    for f in range(4):
                        dve.wait_ge(g_full, m * 4 + f + 1)
                        for q in range(2):
                            ins = nc.vector.tensor_tensor(mats[:, k, f % 2, f // 2 * 2 + q, :],
                                                          bank[4 + f % 2][:, q * 256:q * 256 + 256], mask, ALU.mult)
                        ins.then_inc(mats_ready, 1)
                        dve.wait_ge(mats_ready, m * 4 + f + 1)
                        dve.sem_inc(g_free, 1)
                    dve.sem_inc(dve_done, 1)
                    assert count[0] == LINKS, count
    a1.free()
    end_stage()
    if last < 2:
        return

    mix = sb("mix", [P, KD, SEQ])
    gate_b = sb("gate_b", [P, KD, SEQ])
    a2 = Arena()
    lo = a2("lo", [P, CH, CH])
    ti = a2("ti", [P, CH, CH])
    upd = a2("upd", [P, CH * CH // 4])
    wr = a2("wr", [P, 3, KD, 512])
    qk = a2("qk", [P, 10, SEQ])
    vt = a2("vt", [P, TT, KV * HEAD])
    rope_tmp = a2("rope_tmp", [P, 2, SEQ])
    rope_sin_x = a2("rope_sin_x", [P, 2, SEQ])
    cos_t, sin_t, ang, turn = (a2(n, [P, SEQ]) for n in ("cos_t", "sin_t", "ang", "turn"))
    pos_i = a2("pos_i", [P, SEQ], positions.tensor.dtype)
    sink = a2("sink", [P, HEADS])
    sm = a2("sm", [P, 2, 2, 2 * P])
    pr = a2("pr", [P, 2, 2, 2 * P])
    prT = a2("prT", [P, 2, 512])
    mx, nmx, sums, es, sd, rec = (a2(n, [P, 2, 2]) for n in ("mx", "nmx", "sums", "es", "sd", "rec"))
    half_pi = a2("half_pi", [P, 2])

    lo_in, tab_in, sink_in, lo_chain, ti_ready, ti_stored, pos_ready = (sem(n) for n in (
        "lo_in", "tab_in", "sink_in", "lo_chain", "ti_ready", "ti_stored", "pos_ready"))
    wr_in = [sem(f"wr_in{n}") for n in range(3)]
    f_full, f_evac, tab_done, rot_full, rope_x, rope_s, roped = (sem(n) for n in (
        "f_full", "f_evac", "tab_done", "rot_full", "rope_x", "rope_s", "roped"))
    s_full, sm_ready, p_ready, pn_ready, pt_full, pt_ready, o_full, o_used, att_chain = (sem(n) for n in (
        "s_full", "sm_ready", "p_ready", "pn_ready", "pt_full", "pt_ready", "o_full", "o_used", "att_chain"))
    w_blocks = [0, 512, 1024] + [OFF_GATE + 512 * n for n in range(4)]
    fills = ([("q", b, g) for b in range(2) for g in range(4)] + [("k", 2, g) for g in range(2)]
             + [("v", 2, t) for t in range(TT)] + [("a", 3 + b, g) for b in range(2) for g in range(4)]
             + [("b", 5 + b, g) for b in range(2) for g in range(4)])
    units = [(pp, n, g) for pp in range(2) for n in range(TT) for g in range(4)]
    NU = len(units)
    with nc.Block() as block:
        @block.sync
        def _(sp):
            sp.dma_start(lo[:, :, :], low_dram.rearrange("h q c s t -> (h q c) s t")).then_inc(lo_in, 16)
            sp.dma_start(pos_i[:, :], positions.partition_broadcast(P)).then_inc(tab_in, 16)
            sp.dma_start(sink[:, :], attn_sinks.partition_broadcast(P)).then_inc(sink_in, 16)
            for n, c in enumerate(w_blocks):
                if n >= 3:
                    sp.wait_ge(f_full, 1 + max(i for i, f in enumerate(fills) if f[1] == n - 3))
                if n < 2:
                    for d in range(KD):
                        for a in range(2):
                            sp.dma_start(wr[:, n, d, :].rearrange("p (g a j) -> p g a j", a=2, g=4)[:, :, a, :],
                                         w_cols[:, d, c + 256 * a:c + 256 * a + 256].rearrange("p (g j) -> p g j", g=4))\
                                .then_inc(wr_in[n], 16)
                else:
                    sp.dma_start(wr[:, n % 3, :, :], w_cols[:, :, c:c + 512]).then_inc(wr_in[n % 3], 16)
            sp.wait_ge(ti_ready, 1)
            sp.dma_start(inv_dram.rearrange("h q c s t -> (h q c) s t"), ti[:, :, :]).then_inc(ti_stored, 16)
            sp.wait_ge(ti_stored, 16)

        @block.vector
        def _(dve):
            n = [0]

            def link(ins):
                n[0] += 1
                ins.then_inc(pos_ready, 1)
                dve.wait_ge(pos_ready, n[0])

            dve.wait_ge(tab_in, 16)
            link(nc.vector.tensor_copy(ang[:, :], pos_i[:, :]))
            link(nc.vector.tensor_scalar(ang[:, :], ang[:, :], cst[:, C_INVF:C_INVF + 1], None, ALU.mult))
            magic = 1.5 * 2 ** 23
            for dst, quarter in ((sin_t, 0.0), (cos_t, 0.25)):
                link(nc.vector.tensor_scalar(turn[:, :], ang[:, :], 1.0 / TWO_PI, quarter, ALU.mult, ALU.add))
                link(nc.vector.tensor_scalar(turn[:, :], turn[:, :], magic, magic, ALU.add, ALU.subtract))
                hi = 6.28125
                mid = float(np.float32(TWO_PI - hi).view(np.uint32) & np.uint32(0xFFFFF000))
                mid = float(np.uint32(np.float32(TWO_PI - hi).view(np.uint32) & np.uint32(0xFFFFF000)).view(np.float32))
                low = float(TWO_PI - hi - mid)
                link(nc.vector.scalar_tensor_tensor(out=dst[:, :], in0=turn[:, :], scalar=-hi, in1=ang[:, :], op0=ALU.mult, op1=ALU.add))
                link(nc.vector.scalar_tensor_tensor(out=dst[:, :], in0=turn[:, :], scalar=-mid, in1=dst[:, :], op0=ALU.mult, op1=ALU.add))
                link(nc.vector.scalar_tensor_tensor(out=dst[:, :], in0=turn[:, :], scalar=-low, in1=dst[:, :], op0=ALU.mult, op1=ALU.add))
                if quarter:
                    link(nc.vector.tensor_scalar(dst[:, :], dst[:, :], float(np.pi / 2), None, ALU.add))
                link(nc.vector.tensor_scalar(dst[:, :], dst[:, :], 3.1415925, -3.1415925, ALU.min, ALU.max))
            dve.sem_inc(tab_done, 1)

            n[0] = 0

            def follow(ins):
                n[0] += 1
                ins.then_inc(lo_chain, 1)
                dve.wait_ge(lo_chain, n[0])

            follow(nc.vector.memset(ti[:, :, :], 0.0))
            follow(nc.vector.memset(ti[:, :, :].rearrange("p s t -> p (s t)")[:, ::CH + 1], 1.0))
            dve.wait_ge(lo_in, 16)
            for j in range(CH - 1):
                r, c = j + 1, CH - 1 - j
                u = upd[:, 0:r * c].rearrange("p (r c) -> p r c", c=c)
                follow(nc.vector.tensor_tensor(u, ti[:, 0:r, j:j + 1].broadcast_to([P, r, c]),
                                               lo[:, j:j + 1, j + 1:].broadcast_to([P, r, c]), ALU.mult))
                follow(nc.vector.tensor_tensor(ti[:, 0:r, j + 1:], ti[:, 0:r, j + 1:], u, ALU.subtract))
            dve.sem_inc(ti_ready, 1)

        @block.tensor
        def _(pe):
            for i, (kind, b, g) in enumerate(fills):
                pe.wait_ge(wr_in[b % 3], 16 * (b // 3 + 1) + (240 if b % 3 < 2 else 0))
                if i >= 2:
                    pe.wait_ge(f_evac, i - 1)
                w = wr[:, b % 3, :, :]
                for d in range(KD):
                    st = dict(start=(d == 0), stop=(d == KD - 1))
                    if kind == "v":
                        mm = nc.tensor.matmul(bank[i % 2][:, 0:256], xnT[:, d, g * P:(g + 1) * P], w[:, d, 256:512], **st)
                    else:
                        mm = nc.tensor.matmul(bank[i % 2][:, :], w[:, d, g * P:(g + 1) * P], xnT[:, d, :], **st)
                mm.then_inc(f_full, 1)
            for i in range(10):
                if i < 2:
                    pe.wait_ge(f_evac, len(fills) - 1 + i)
                else:
                    pe.wait_ge(rope_s, i - 1)
                nc.tensor.matmul(bank[i % 2][:, :], cst[:, C_ROT:C_ROT + P], qk[:, i, :], start=True, stop=True).then_inc(rot_full, 1)

            def scores(u):
                pp, n, g = units[u]
                if u >= 2:
                    pe.wait_ge(sm_ready, u - 1)
                k0, width = (0, P) if n == 0 else ((n - 1) * P, 2 * P)
                for h in range(2):
                    hb = slice(64 * h, 64 * h + 64)
                    mm = nc.tensor.matmul(bank[2 * (u % 2) + h][:, 0:width], qk[hb, 4 * pp + g, n * P:(n + 1) * P],
                                          qk[hb, 8 + pp, k0:k0 + width], start=True, stop=True)
                mm.then_inc(s_full, 1)

            def turn_p(u):
                n = units[u][1]
                pe.wait_ge(pn_ready, u + 1)
                if u >= 2:
                    pe.wait_ge(pt_ready, u - 1)
                for h in range(2):
                    for s in range(1 if n == 0 else 2):
                        mm = nc.tensor.transpose(bank[4 + u % 2][:, (2 * h + s) * P:(2 * h + s + 1) * P],
                                                 pr[:, u % 2, h, s * P:(s + 1) * P], ident)
                mm.then_inc(pt_full, 1)

            def weigh(u):
                pp, n, g = units[u]
                pe.wait_ge(pt_ready, u + 1)
                if u >= 2:
                    pe.wait_ge(o_used, u - 1)
                ob = slice(64 * (g % 2), 64 * (g % 2) + 64)
                tiles = [0] if n == 0 else [n - 1, n]
                for h in range(2):
                    kv = 2 * pp + h
                    for s, t in enumerate(tiles):
                        mm = nc.tensor.matmul(bank[6 + u % 2][ob, h * P:(h + 1) * P], vt[:, t, kv * HEAD:(kv + 1) * HEAD],
                                              prT[:, u % 2, (2 * h + s) * P:(2 * h + s + 1) * P],
                                              start=(s == 0), stop=(s == len(tiles) - 1))
                mm.then_inc(o_full, 1)

            pe.wait_ge(roped, 10)
            for u in range(NU + 2):
                if u < NU:
                    scores(u)
                if 1 <= u <= NU:
                    turn_p(u - 1)
                if u >= 2:
                    weigh(u - 2)

        @block.scalar
        def _(act):
            act.wait_ge(tab_done, 1)
            nc.scalar.activation(sin_t[:, :], sin_t[:, :], ACT.Sin).then_inc(tab_done, 1)
            nc.scalar.activation(cos_t[:, :], cos_t[:, :], ACT.Sin).then_inc(tab_done, 1)
            for i, (kind, b, g) in enumerate(fills):
                act.wait_ge(f_full, i + 1)
                src = bank[i % 2][:, :]
                if kind == "q":
                    nc.scalar.activation(qk[:, 4 * b + g, :], src, ACT.Copy).then_inc(f_evac, 1)
                elif kind == "k":
                    nc.scalar.activation(qk[:, 8 + g, :], src, ACT.Copy).then_inc(f_evac, 1)
                elif kind == "v":
                    nc.scalar.activation(vt[:, g, :], src[:, 0:256], ACT.Copy).then_inc(f_evac, 1)
                elif kind == "a":
                    nc.scalar.activation(mix[:, 4 * (b - 3) + g, :], src, ACT.Sigmoid).then_inc(f_evac, 1)
                else:
                    nc.scalar.activation(gate_b[:, 4 * (b - 5) + g, :], src, ACT.Sigmoid).then_inc(f_evac, 1)

            def exps(u):
                width = P if units[u][1] == 0 else 2 * P
                act.wait_ge(sm_ready, u + 1)
                for h in range(2):
                    nc.scalar.activation(pr[:, u % 2, h, 0:width], sm[:, u % 2, h, 0:width], ACT.Exp,
                                         bias=nmx[:, u % 2, h:h + 1], accum_out=sums[:, u % 2, h:h + 1])
                nc.scalar.activation(es[:, u % 2, :], sd[:, u % 2, :], ACT.Exp).then_inc(p_ready, 1)

            def evac_p(u):
                act.wait_ge(pt_full, u + 1)
                if u >= 2:
                    act.wait_ge(o_full, u - 1)
                n = units[u][1]
                if n == 0:
                    v = prT[:, u % 2, :].rearrange("p (h s q) -> p h s q", h=2, s=2)[:, :, 0, :]
                    w = bank[4 + u % 2][:, :].rearrange("p (h s q) -> p h s q", h=2, s=2)[:, :, 0, :]
                else:
                    v, w = prT[:, u % 2, :], bank[4 + u % 2][:, :]
                nc.scalar.activation(v, w, ACT.Copy).then_inc(pt_ready, 1)

            for u in range(NU + 1):
                if u < NU:
                    exps(u)
                if u >= 1:
                    evac_p(u - 1)

        @block.gpsimd
        def _(pool):
            pool.wait_ge(tab_done, 3)
            for i in range(10):
                pool.wait_ge(f_evac, i + 1)
                if i >= 2:
                    pool.wait_ge(roped, i - 1)
                nc.gpsimd.tensor_tensor(rope_tmp[:, i % 2, :], qk[:, i, :], cos_t[:, :], ALU.mult).then_inc(rope_x, 1)

        @block.vector
        def _(dve):
            dve.wait_ge(tab_done, 3)
            for i in range(10):
                dve.wait_ge(rot_full, i + 1)
                nc.vector.tensor_tensor(rope_sin_x[:, i % 2, :], bank[i % 2][:, :], sin_t[:, :], ALU.mult).then_inc(rope_s, 1)
                dve.wait_ge(rope_s, i + 1)
                dve.wait_ge(rope_x, i + 1)
                nc.vector.tensor_tensor(qk[:, i, :], rope_tmp[:, i % 2, :], rope_sin_x[:, i % 2, :], ALU.add).then_inc(roped, 1)

            dve.wait_ge(sink_in, 16)
            dve.wait_ge(f_evac, len(fills))
            n_links = [0]

            def link(ins):
                n_links[0] += 1
                ins.then_inc(att_chain, 1)
                dve.wait_ge(att_chain, n_links[0])

            def mask_max(u):
                pp, n, g = units[u]
                i, width = u % 2, (P if n == 0 else 2 * P)
                first = P if n == 0 else 0
                dve.wait_ge(s_full, u + 1)
                if u >= 2:
                    dve.wait_ge(p_ready, u - 1)
                for h in range(2):
                    ins = nc.vector.scalar_tensor_tensor(
                        out=sm[:, i, h, 0:width], in0=bank[2 * i + h][:, 0:width], scalar=HEAD ** -0.5,
                        in1=cst[:, C_BAND + first:C_BAND + 2 * P], op0=ALU.mult, op1=ALU.add)
                link(ins)
                link(nc.vector.tensor_reduce(mx[:, i, :], sm[:, i, :, 0:width], AX, ALU.max))
                sinks = sink[:, 8 * pp + g:8 * pp + g + 5:4]
                link(nc.vector.tensor_tensor(nmx[:, i, :], mx[:, i, :], sinks, ALU.max))
                link(nc.vector.tensor_scalar(nmx[:, i, :], nmx[:, i, :], -1.0, None, ALU.mult))
                nc.vector.tensor_tensor(sd[:, i, :], sinks, nmx[:, i, :], ALU.add).then_inc(sm_ready, 1)

            def normalise(u):
                i, width = u % 2, (P if units[u][1] == 0 else 2 * P)
                dve.wait_ge(p_ready, u + 1)
                link(nc.vector.tensor_tensor(rec[:, i, :], sums[:, i, :], es[:, i, :], ALU.add))
                link(nc.vector.reciprocal(rec[:, i, :], rec[:, i, :]))
                for h in range(2):
                    ins = nc.vector.tensor_scalar(pr[:, i, h, 0:width], pr[:, i, h, 0:width], rec[:, i, h:h + 1], None, ALU.mult)
                ins.then_inc(pn_ready, 1)

            def gated(u):
                pp, n, g = units[u]
                dve.wait_ge(o_full, u + 1)
                ob = slice(64 * (g % 2), 64 * (g % 2) + 64)
                m0 = 4 * pp + g // 2
                for h in range(2):
                    v = mix[ob, m0 + 2 * h, n * P:(n + 1) * P]
                    ins = nc.vector.tensor_tensor(v, bank[6 + u % 2][ob, h * P:(h + 1) * P], v, ALU.mult)
                ins.then_inc(o_used, 1)

            for u in range(NU + 2):
                if u < NU:
                    mask_max(u)
                if 1 <= u <= NU:
                    normalise(u - 1)
                if u >= 2:
                    gated(u - 2)
    a2.free()
    end_stage()
    peek("mix", mix[:, :, :])
    peek("gate_b", gate_b[:, :, :])
    if last < 3:
        return

    a3 = Arena()
    tok_s = a3("tok_s", [P, 2, 4, SEQ])
    mats_s = a3("mats_s", [P, 2, 2, 4, 4 * CH])
    ti_s = a3("ti_s", [P, 2, 2, 4, CH])
    rho_s = a3("rho_s", [P, 2, SEQ])
    y_s = a3("y_s", [P, 2, SEQ])
    ta_s = a3("ta_s", [P, 2, SEQ])
    w1_s = a3("w1_s", [P, 2, SEQ])
    diag = a3("diag", [P, 2, NCH, CH])
    two_id = a3("two_id", [P, CH])
    phi = a3("phi", [P, KD, NCH, CH])
    psi = a3("psi", [P, KD, NCH, CH])
    rhop = a3("rhop", [P, KD, NCH, CH])
    o_all = a3("o_all", [P, KD, NCH, CH])
    state = a3("state", [P, 2, KD, CH])
    g2_s = a3("g2_s", [P, D])

    in_s = [sem("chunk_in0"), sem("chunk_in1")]
    (y_full, y_ready, tw_full, ta_ready, w1_ready, xz_full, x_used, z_used, id_ready, diag_ready, state_ready, st_full,
     os_full, o_ready, g2_in) = (sem(n) for n in (
         "y_full", "y_ready", "tw_full", "ta_ready", "w1_ready", "xz_full", "x_used", "z_used", "id_ready",
         "diag_ready", "state_ready", "st_full", "os_full", "o_ready", "g2_in"))

    def halves(c):
        return slice(64 * (c % 2), 64 * (c % 2) + 64)

    def one(t, m):
        return t[:, bass.ds(m, 1)] if not isinstance(m, int) else t[:, m:m + 1]

    with nc.Block() as block:
        @block.sync
        def _(sp):
            sp.dma_start(g2_s[:, :], rwkv_g2[0]).then_inc(g2_in, 16)
            with sp.Fori(0, KD // 2) as i:
                for k in range(2):
                    m = i * 2 + k
                    sp.wait_ge(xz_full, m * 2 + 2)
                    sp.wait_ge(x_used, m * 2 + 2)
                    sp.dma_start(tok_s[:, k, :, :].rearrange("p a s -> p (a s)"),
                                 tok_dram[bass.ds(m, 1)].rearrange("a p s -> (a p) s")).then_inc(in_s[k], 16)
                    sp.dma_start(mats_s[:, k, :, :, :].rearrange("p h c n -> p (h c n)"),
                                 mats_dram[bass.ds(m, 1)].rearrange("a p s -> (a p) s")).then_inc(in_s[k], 16)
                    sp.dma_start(rho_s[:, k, :], rho_dram[bass.ds(m, 1)].rearrange("a p s -> (a p) s")).then_inc(in_s[k], 16)
                    for par in range(2):
                        sp.dma_start(ti_s[par * CH:(par + 1) * CH, k, :, :, :].rearrange("p h c t -> p (h c) t"),
                                     inv_dram[bass.ds(m * 2, 2), :, par].rearrange("h c s t -> s (h c) t")).then_inc(in_s[k], 16)

        @block.tensor
        def _(pe):
            pe.sem_inc(xz_full, 4)

            def y_part(m, i, k):
                pe.wait_ge(in_s[k], i * 80 + 80)
                pe.wait_ge(y_ready, m + 1)
                pe.sem_inc(gone_on, 1)
                for c in range(NCH):
                    cb = halves(c)
                    for h in range(2):
                        at = (h * 4 + c // 2) * CH
                        mm = nc.tensor.matmul(bank[0][cb, at:at + CH], mats_s[cb, k, h, c // 2, 2 * CH:3 * CH],
                                              tok_s[cb, k, 1, c // 2 * P + h * 64:c // 2 * P + h * 64 + 64], start=True, stop=True)
                mm.then_inc(y_full, 1)

            def solve_part(m, k):
                pe.wait_ge(ta_ready, m + 1)
                pe.sem_inc(gone_on, 1)
                for c in range(NCH):
                    cb = halves(c)
                    for h in range(2):
                        at = (h * 4 + c // 2) * CH
                        mm = nc.tensor.matmul(bank[1][cb, at:at + CH], ti_s[cb, k, h, c // 2, :],
                                              tok_s[cb, k, 0, c // 2 * P + h * 64:c // 2 * P + h * 64 + 64], start=True, stop=True)
                mm.then_inc(tw_full, 1)
                pe.wait_ge(y_ready, m + 2)
                pe.wait_ge(w1_ready, m + 1)
                pe.sem_inc(gone_on, 1)
                for c in range(NCH):
                    cb = halves(c)
                    for h in range(2):
                        at = (h * 4 + c // 2) * CH
                        mm = nc.tensor.matmul(bank[2][cb, at:at + CH], ti_s[cb, k, h, c // 2, :],
                                              y_s[cb, k, at:at + CH], start=True, stop=True)
                mm.then_inc(tw_full, 1)

            def xz_part(m, k):
                pe.wait_ge(ta_ready, m + 2)
                pe.wait_ge(x_used, m * 2 + 4)
                pe.sem_inc(gone_on, 1)
                for c in range(NCH):
                    cb = halves(c)
                    q = c // 2
                    x = bank[3 + c % 2]
                    for h in range(2):
                        hb = slice(64 * h, 64 * h + 64)
                        at = (h * 4 + q) * CH
                        ch = slice(q * P + h * 64, q * P + h * 64 + 64)
                        ta = ta_s[cb, k, at:at + CH]
                        nc.tensor.matmul(x[hb, q * CH:(q + 1) * CH], ta, mats_s[cb, k, h, q, CH:2 * CH], start=True, stop=True)
                        mm = nc.tensor.matmul(x[hb, 256 + q * CH:256 + (q + 1) * CH], ta, tok_s[cb, k, 3, ch], start=True, stop=True)
                mm.then_inc(xz_full, 1)
                pe.wait_ge(w1_ready, m + 2)
                pe.wait_ge(z_used, m * 2 + 2)
                pe.sem_inc(gone_on, 1)
                for c in range(NCH):
                    cb = halves(c)
                    q = c // 2
                    z = bank[5 + c % 2]
                    for h in range(2):
                        hb = slice(64 * h, 64 * h + 64)
                        at = (h * 4 + q) * CH
                        ch = slice(q * P + h * 64, q * P + h * 64 + 64)
                        w1 = w1_s[cb, k, at:at + CH]
                        v = tok_s[cb, k, 1, ch]
                        o = z[hb, q * CH:(q + 1) * CH]
                        nc.tensor.matmul(o, tok_s[cb, k, 2, ch], v, start=True, stop=False)
                        nc.tensor.matmul(o, tok_s[cb, k, 3, ch], w1, start=False, stop=True)
                        o = z[hb, 256 + q * CH:256 + (q + 1) * CH]
                        nc.tensor.matmul(o, v, mats_s[cb, k, h, q, 3 * CH:4 * CH], start=True, stop=False)
                        mm = nc.tensor.matmul(o, w1, mats_s[cb, k, h, q, CH:2 * CH], start=False, stop=True)
                mm.then_inc(xz_full, 1)

            y_part(0, 0, 0)
            with pe.Fori(0, KD // 2 - 1) as i:
                solve_part(i * 2, 0)
                y_part(i * 2 + 1, i, 1)
                xz_part(i * 2, 0)
                solve_part(i * 2 + 1, 1)
                y_part(i * 2 + 2, i + 1, 0)
                xz_part(i * 2 + 1, 1)
            solve_part(KD - 2, 0)
            y_part(KD - 1, KD // 2 - 1, 1)
            xz_part(KD - 2, 0)
            solve_part(KD - 1, 1)
            xz_part(KD - 1, 1)

            for c in range(NCH):
                if c > 0:
                    pe.wait_ge(state_ready, c)
                    if c < NCH - 1:
                        for m in range(KD):
                            for h in range(2):
                                hb = slice(64 * h, 64 * h + 64)
                                mm = nc.tensor.matmul(bank[0][hb, m * CH:(m + 1) * CH], phi[hb, m, c, :],
                                                      state[hb, c % 2, m, :], start=True, stop=True)
                        mm.then_inc(st_full, 1)
                    if c > 2:
                        pe.wait_ge(o_ready, c - 2)
                    if c == 1:
                        pe.wait_ge(x_used, 2 * KD + 4)
                        pe.wait_ge(z_used, 2 * KD + 2)
                    for m in range(KD):
                        for h in range(2):
                            hb = slice(64 * h, 64 * h + 64)
                            mm = nc.tensor.matmul(bank[1 + c % 2][hb, m * CH:(m + 1) * CH], state[hb, c % 2, m, :],
                                                  rhop[hb, m, c, :], start=True, stop=True)
                    mm.then_inc(os_full, 1)

        @block.scalar
        def _(act):
            act.sem_inc(y_ready, 1)
            act.sem_inc(ta_ready, 1)
            act.sem_inc(z_used, 2)
            with act.Fori(0, KD // 2) as i:
                for k in range(2):
                    m = i * 2 + k
                    act.wait_ge(y_full, m + 1)
                    act.wait_ge(xz_full, m * 2 + 2)
                    nc.scalar.activation(y_s[:, k, :], bank[0][:, :], ACT.Copy).then_inc(y_ready, 1)
                    act.wait_ge(tw_full, m * 2 + 1)
                    nc.scalar.activation(ta_s[:, k, :], bank[1][:, :], ACT.Copy).then_inc(ta_ready, 1)
                    act.wait_ge(xz_full, m * 2 + 6)
                    for par in range(2):
                        src = bank[5 + par][:, :].rearrange("p (n q t) -> p n q t", n=2, t=CH)
                        for n, dst in enumerate((psi, o_all)):
                            v = one(dst, m).rearrange("p m (q par) t -> p (m q) par t", par=2)[:, :, par, :]
                            ins = nc.scalar.activation(v, src[:, n], ACT.Copy)
                        ins.then_inc(z_used, 1)

        @block.vector
        def _(dve):
            dve.sem_inc(w1_ready, 1)
            dve.sem_inc(x_used, 4)
            nc.vector.tensor_tensor(two_id[:, :], ident[:, 0:CH], ident[:, CH:2 * CH], ALU.add).then_inc(id_ready, 1)
            dve.wait_ge(id_ready, 1)
            with dve.Fori(0, KD // 2) as i:
                for k in range(2):
                    m = i * 2 + k
                    nc.vector.tensor_tensor(diag[:, k, :, :], two_id[:, :].rearrange("p (a t) -> p a t", a=1).broadcast_to([P, NCH, CH]),
                                            one(decay_end, m).rearrange("p a (c t) -> p (a c) t", t=1).broadcast_to([P, NCH, CH]),
                                            ALU.mult).then_inc(diag_ready, 1)
                    dve.wait_ge(diag_ready, m + 1)
                    dve.wait_ge(tw_full, m * 2 + 2)
                    nc.vector.tensor_copy(w1_s[:, k, :], bank[2][:, :]).then_inc(w1_ready, 1)
                    dve.wait_ge(xz_full, m * 2 + 5)
                    for par in range(2):
                        src = bank[3 + par][:, :].rearrange("p (n q t) -> p n q t", n=2, t=CH)

                        def mine(t):
                            return t.rearrange("p (q par) t -> p q par t", par=2)[:, :, par, :]

                        nc.vector.tensor_tensor(mine(one(rhop, m).rearrange("p m c t -> p (m c) t")), src[:, 0],
                                                mine(rho_s[:, k, :].rearrange("p (c t) -> p c t", t=CH)), ALU.add)
                        nc.vector.tensor_tensor(mine(one(phi, m).rearrange("p m c t -> p (m c) t")), src[:, 1],
                                                mine(diag[:, k, :, :]), ALU.add).then_inc(x_used, 1)

            dve.wait_ge(z_used, 2 * KD + 2)
            nc.vector.tensor_copy(state[:, 1, :, :], psi[:, :, 0, :]).then_inc(state_ready, 1)
            for c in range(1, NCH):
                if c < NCH - 1:
                    dve.wait_ge(st_full, c)
                    if c > 1:
                        dve.wait_ge(os_full, c - 1)
                    nc.vector.tensor_tensor(state[:, (c + 1) % 2, :, :], bank[0][:, :].rearrange("p (m t) -> p m t", t=CH),
                                            psi[:, :, c, :], ALU.add).then_inc(state_ready, 1)
                dve.wait_ge(os_full, c)
                nc.vector.tensor_tensor(o_all[:, :, c, :], bank[1 + c % 2][:, :].rearrange("p (m t) -> p m t", t=CH),
                                        o_all[:, :, c, :], ALU.add).then_inc(o_ready, 1)

    (gn_mean, gn_cen, gn_sq, gn_var, gn_std, gn_g, gn_used, gn_chain, gn_on, gn_done) = (sem(n) for n in (
        "gn_mean", "gn_cen", "gn_sq", "gn_var", "gn_std", "gn_g", "gn_used", "gn_chain", "gn_on", "gn_done"))
    bonus_in = [sem("bonus_in0"), sem("bonus_in1")]
    cen, sq, std, on, bns = rho_s, y_s, ta_s, w1_s, tok_s[:, 0, 0:2, :]
    eps_gn = a3("eps_gn", [P, 1])
    with nc.Block() as block:
        @block.sync
        def _(sp):
            for m in range(KD):
                if m >= 2:
                    sp.wait_ge(gn_done, m - 1)
                sp.dma_start(bns[:, m % 2, :], bonus_dram[m]).then_inc(bonus_in[m % 2], 16)

        @block.tensor
        def _(pe):
            def mean(m):
                if m >= 2:
                    pe.wait_ge(gn_cen, m - 1)
                nc.tensor.matmul(bank[m % 2][:, :], bones, o_all[:, m].rearrange("p c t -> p (c t)"), start=True, stop=True).then_inc(gn_mean, 1)
            mean(0)
            for m in range(KD):
                if m + 1 < KD:
                    mean(m + 1)
                if m >= 2:
                    pe.wait_ge(gn_used, m - 1)
                nc.tensor.matmul(bank[4 + m % 2][:, :], g2_s[:, m * P:(m + 1) * P], sdg[:, :], start=True, stop=True).then_inc(gn_g, 1)
                pe.wait_ge(gn_sq, m + 1)
                if m >= 2:
                    pe.wait_ge(gn_std, m - 1)
                nc.tensor.matmul(bank[2 + m % 2][:, :], bones, sq[:, m % 2, :], start=True, stop=True).then_inc(gn_var, 1)

        @block.scalar
        def _(act):
            for m in range(KD):
                i = m % 2
                act.wait_ge(gn_cen, m + 1)
                if m >= 2:
                    act.wait_ge(gn_var, m - 1)
                nc.scalar.activation(sq[:, i, :], cen[:, i, :], ACT.Square).then_inc(gn_sq, 1)
                act.wait_ge(gn_var, m + 1)
                if m >= 2:
                    act.wait_ge(gn_on, m - 1)
                nc.scalar.activation(std[:, i, :], bank[2 + i][:, :], ACT.Sqrt, scale=1.0 / HEAD, bias=eps_gn[:, :]).then_inc(gn_std, 1)

        @block.vector
        def _(dve):
            n = [0]

            def link(ins):
                n[0] += 1
                ins.then_inc(gn_chain, 1)
                dve.wait_ge(gn_chain, n[0])

            link(nc.vector.memset(eps_gn[:, :], GN_EPS))

            def centre(m):
                i = m % 2
                dve.wait_ge(gn_mean, m + 1)
                if m >= 2:
                    dve.wait_ge(gn_sq, m - 1)
                nc.vector.scalar_tensor_tensor(out=cen[:, i, :], in0=bank[i][:, :], scalar=-1.0 / HEAD,
                                               in1=o_all[:, m].rearrange("p c t -> p (c t)"), op0=ALU.mult, op1=ALU.add).then_inc(gn_cen, 1)
                dve.wait_ge(gn_cen, m + 1)
            centre(0)
            for m in range(KD):
                i = m % 2
                if m + 1 < KD:
                    centre(m + 1)
                dve.wait_ge(gn_std, m + 1)
                link(nc.vector.reciprocal(std[:, i, :], std[:, i, :]))
                link(nc.vector.tensor_tensor(on[:, i, :], cen[:, i, :], std[:, i, :], ALU.mult))
                dve.sem_inc(gn_on, 1)
                link(nc.vector.tensor_scalar(on[:, i, :], on[:, i, :], col(R_LNW, m), col(R_LNB, m), ALU.mult, ALU.add))
                dve.wait_ge(bonus_in[i], 16 * (m // 2 + 1))
                link(nc.vector.tensor_tensor(on[:, i, :], on[:, i, :], bns[:, i, :], ALU.add))
                dve.sem_inc(gn_done, 1)
                dve.wait_ge(gn_g, m + 1)
                link(nc.vector.tensor_tensor(on[:, i, :], bank[4 + i][:, :], on[:, i, :], ALU.mult))
                dve.sem_inc(gn_used, 1)
                link(nc.vector.tensor_tensor(on[:, i, :], on[:, i, :], gate_b[:, m], ALU.mult))
                link(nc.vector.tensor_tensor(mix[:, m], mix[:, m], on[:, i, :], ALU.add))
    a3.free()
    end_stage()
    peek("mixed", mix[:, :, :])
    if last < 4:
        return

    hres = sb("hres", [P, TT, D])
    kc = sb("kc", [P, CROSS_H, MEM])
    vc = sb("vc", [P, MEM // P, CROSS_W])
    a4 = Arena()
    mem_s = a4("mem_s", [P, MEM // P, D])
    mem_n = a4("mem_n", [P, MEM // P, D])
    memT = a4("memT", [P, KD, MEM])
    w_kv = a4("w_kv", [P, KD, 2 * CROSS_W])
    mem_in, hres_in, kv_in, kv_full, kv_evac = (sem(n) for n in ("mem_in", "hres_in", "kv_in", "kv_full", "kv_evac"))
    with nc.Block() as block:
        @block.sync
        def _(sp):
            sp.dma_start(mem_s[:, :, :], mem.rearrange("b (t p) d -> p (b t) d", p=P)).then_inc(mem_in, 16)
            sp.dma_start(w_kv[:, :, :], w_kv_cross[0].rearrange("(k p) c -> p k c", p=P)).then_inc(kv_in, 16)
            sp.dma_start(hres[:, :, :], x_tok).then_inc(hres_in, 16)
        memT_ready, memT_at = norm_transpose(block, "nm", mem_s, MEM // P, R_GMEM, mem_n, memT, mem_in, 16, bank[0:2])

        @block.tensor
        def _(pe):
            pe.wait_ge(kv_in, 16)
            pe.wait_ge(memT_ready, memT_at)
            for n in range(CROSS_H + MEM // P):
                if n >= 2:
                    pe.wait_ge(kv_evac, n - 1)
                b = bank[2 + n % 2]
                for d in range(KD):
                    st = dict(start=(d == 0), stop=(d == KD - 1))
                    if n < CROSS_H:
                        mm = nc.tensor.matmul(b[:, 0:MEM], w_kv[:, d, n * P:(n + 1) * P], memT[:, d, :], **st)
                    else:
                        t = n - CROSS_H
                        mm = nc.tensor.matmul(b[:, :], memT[:, d, t * P:(t + 1) * P], w_kv[:, d, CROSS_W:], **st)
                mm.then_inc(kv_full, 1)

        @block.scalar
        def _(act):
            for n in range(CROSS_H + MEM // P):
                act.wait_ge(kv_full, n + 1)
                b = bank[2 + n % 2]
                if n < CROSS_H:
                    ins = nc.scalar.activation(kc[:, n, :], b[:, 0:MEM], ACT.Copy)
                else:
                    ins = nc.scalar.activation(vc[:, n - CROSS_H, :], b[:, :], ACT.Copy)
                ins.then_inc(kv_evac, 1)
    a4.free()

    a5 = Arena()
    w_o1 = a5("w_o1", [P, KD, D])
    w_qc = a5("w_qc", [P, KD, CROSS_W])
    w_oc = a5("w_oc", [P, CROSS_H, D])
    xn5 = a5("xn5", [P, TT, D])
    cpr = a5("cpr", [P, 2, 2, MEM])
    cprT = a5("cprT", [P, 2, 512])
    cmx, csum, crec = (a5(n, [P, 2, 2]) for n in ("cmx", "csum", "crec"))
    qc = gate_b[:, 0:CROSS_H, :]
    oc = gate_b[:, CROSS_H:2 * CROSS_H, :]
    (wo1_in, wqc_in, woc_in, op_full, h_ready, qc_full, qc_evac, cs_full, cmx_ready, cp_ready, cpn_ready, ct_full,
     ct_evac, co_full, co_evac, c_chain, oo_full) = (sem(n) for n in (
         "wo1_in", "wqc_in", "woc_in", "op_full", "h_ready", "qc_full", "qc_evac", "cs_full", "cmx_ready", "cp_ready",
         "cpn_ready", "ct_full", "ct_evac", "co_full", "co_evac", "c_chain", "oo_full"))
    SC = P ** -0.5
    cunits = [(t, hp) for t in range(TT) for hp in range(2)]
    NC_ = len(cunits)
    with nc.Block() as block:
        @block.sync
        def _(sp):
            sp.dma_start(w_o1[:, :, :], w_out[0].rearrange("(k p) c -> p k c", p=P)).then_inc(wo1_in, 16)
            sp.dma_start(w_qc[:, :, :], w_q_cross[0].rearrange("(k p) c -> p k c", p=P)).then_inc(wqc_in, 16)
            sp.dma_start(w_oc[:, :, :], w_o_cross[0].rearrange("(k p) c -> p k c", p=P)).then_inc(woc_in, 16)

        @block.tensor
        def _(pe):
            pe.wait_ge(wo1_in, 16)
            for n in range(2 * TT):
                if n >= 2:
                    pe.wait_ge(h_ready, n - 1)
                t, f = n // 2, n % 2
                for d in range(KD):
                    mm = nc.tensor.matmul(bank[2 + n % 2][:, :], mix[:, d, t * P:(t + 1) * P], w_o1[:, d, f * 512:(f + 1) * 512],
                                          start=(d == 0), stop=(d == KD - 1))
                mm.then_inc(op_full, 1)

        @block.vector
        def _(dve):
            dve.wait_ge(hres_in, 16)
            for n in range(2 * TT):
                dve.wait_ge(op_full, n + 1)
                v = hres[:, n // 2, n % 2 * 512:n % 2 * 512 + 512]
                nc.vector.tensor_tensor(v, bank[2 + n % 2][:, :], v, ALU.add).then_inc(h_ready, 1)
        xc_ready, xc_at = norm_transpose(block, "nc", hres, TT, R_GCROSS, xn5, xnT, h_ready, 2 * TT, bank[0:2])

        @block.tensor
        def _(pe):
            pe.wait_ge(wqc_in, 16)
            pe.wait_ge(xc_ready, xc_at)
            for n in range(CROSS_H):
                if n >= 2:
                    pe.wait_ge(qc_evac, n - 1)
                for d in range(KD):
                    mm = nc.tensor.matmul(bank[4 + n % 2][:, :], w_qc[:, d, n * P:(n + 1) * P], xnT[:, d, :],
                                          start=(d == 0), stop=(d == KD - 1))
                mm.then_inc(qc_full, 1)

            def scores(u):
                t, hp = cunits[u]
                if u >= 2:
                    pe.wait_ge(cp_ready, u - 1)
                for h in range(2):
                    mm = nc.tensor.matmul(bank[u % 2][:, h * MEM:(h + 1) * MEM], qc[:, 2 * hp + h, t * P:(t + 1) * P],
                                          kc[:, 2 * hp + h, :], start=True, stop=True)
                mm.then_inc(cs_full, 1)

            def turn(u):
                pe.wait_ge(cpn_ready, u + 1)
                if u >= 2:
                    pe.wait_ge(ct_evac, u - 1)
                for h in range(2):
                    for s in range(2):
                        mm = nc.tensor.transpose(bank[2 + u % 2][:, (2 * h + s) * P:(2 * h + s + 1) * P],
                                                 cpr[:, u % 2, h, s * P:(s + 1) * P], ident)
                mm.then_inc(ct_full, 1)

            def weigh(u):
                t, hp = cunits[u]
                pe.wait_ge(ct_evac, u + 1)
                if u >= 2:
                    pe.wait_ge(co_evac, u - 1)
                for h in range(2):
                    for s in range(2):
                        mm = nc.tensor.matmul(bank[4 + u % 2][:, h * P:(h + 1) * P], vc[:, s, (2 * hp + h) * P:(2 * hp + h + 1) * P],
                                              cprT[:, u % 2, (2 * h + s) * P:(2 * h + s + 1) * P], start=(s == 0), stop=(s == 1))
                mm.then_inc(co_full, 1)

            pe.wait_ge(qc_evac, CROSS_H)
            for u in range(NC_ + 2):
                if u < NC_:
                    scores(u)
                if 1 <= u <= NC_:
                    turn(u - 1)
                if u >= 2:
                    weigh(u - 2)
            pe.wait_ge(woc_in, 16)
            pe.wait_ge(co_evac, NC_)
            for n in range(2 * TT):
                if n >= 2:
                    pe.wait_ge(h_ready, 2 * TT + n - 1)
                t, f = n // 2, n % 2
                for d in range(CROSS_H):
                    mm = nc.tensor.matmul(bank[6 + n % 2][:, :], oc[:, d, t * P:(t + 1) * P], w_oc[:, d, f * 512:(f + 1) * 512],
                                          start=(d == 0), stop=(d == CROSS_H - 1))
                mm.then_inc(oo_full, 1)

        @block.scalar
        def _(act):
            for n in range(CROSS_H):
                act.wait_ge(qc_full, n + 1)
                nc.scalar.activation(qc[:, n, :], bank[4 + n % 2][:, :], ACT.Copy).then_inc(qc_evac, 1)

            def exps(u):
                act.wait_ge(cmx_ready, u + 1)
                for h in range(2):
                    ins = nc.scalar.activation(cpr[:, u % 2, h, :], bank[u % 2][:, h * MEM:(h + 1) * MEM], ACT.Exp, scale=SC,
                                               bias=cmx[:, u % 2, h:h + 1], accum_out=csum[:, u % 2, h:h + 1])
                ins.then_inc(cp_ready, 1)

            def evac(u):
                act.wait_ge(ct_full, u + 1)
                if u >= 2:
                    act.wait_ge(co_full, u - 1)
                nc.scalar.activation(cprT[:, u % 2, :], bank[2 + u % 2][:, :], ACT.Copy).then_inc(ct_evac, 1)

            for u in range(NC_ + 1):
                if u < NC_:
                    exps(u)
                if u >= 1:
                    evac(u - 1)

        @block.vector
        def _(dve):
            n_links = [0]

            def link(ins):
                n_links[0] += 1
                ins.then_inc(c_chain, 1)
                dve.wait_ge(c_chain, n_links[0])

            def maxes(u):
                dve.wait_ge(cs_full, u + 1)
                if u >= 2:
                    dve.wait_ge(cp_ready, u - 1)
                link(nc.vector.tensor_reduce(cmx[:, u % 2, :], bank[u % 2][:, :].rearrange("p (h m) -> p h m", h=2), AX, ALU.max))
                nc.vector.tensor_scalar(cmx[:, u % 2, :], cmx[:, u % 2, :], -SC, None, ALU.mult).then_inc(cmx_ready, 1)

            def normalise(u):
                dve.wait_ge(cp_ready, u + 1)
                link(nc.vector.reciprocal(crec[:, u % 2, :], csum[:, u % 2, :]))
                for h in range(2):
                    ins = nc.vector.tensor_scalar(cpr[:, u % 2, h, :], cpr[:, u % 2, h, :], crec[:, u % 2, h:h + 1], None, ALU.mult)
                ins.then_inc(cpn_ready, 1)

            def collect(u):
                t, hp = cunits[u]
                dve.wait_ge(co_full, u + 1)
                nc.vector.tensor_copy(oc[:, 2 * hp:2 * hp + 2, t * P:(t + 1) * P],
                                      bank[4 + u % 2][:, 0:256].rearrange("p (h q) -> p h q", h=2)).then_inc(co_evac, 1)

            for u in range(NC_ + 2):
                if u < NC_:
                    maxes(u)
                if 1 <= u <= NC_:
                    normalise(u - 1)
                if u >= 2:
                    collect(u - 2)
            for n in range(2 * TT):
                dve.wait_ge(oo_full, n + 1)
                v = hres[:, n // 2, n % 2 * 512:n % 2 * 512 + 512]
                nc.vector.tensor_tensor(v, bank[6 + n % 2][:, :], v, ALU.add).then_inc(h_ready, 1)
    a5.free()
    end_stage()
    peek("h2", hres[:, :, :])
    if last < 5:
        return

    xf = mix[:, :, :].rearrange("p k s -> p (k s)").rearrange("p (t d) -> p t d", d=D)
    HK = PH * TOPK
    expert = sb("expert", [P, TT * HK], U32)
    gate = sb("gate", [P, TT, HK])
    a6 = Arena()
    scores_s = a6("scores_s", [P, TT, 2 * PH, NKEYS])
    sc_in = a6("sc_in", [P, 2, NKEYS])
    rest = a6("rest", [P, 2, NKEYS])
    top = a6("top", [P, 2, TOPK])
    topi = a6("topi", [P, 2, TOPK], U32)
    topf = a6("topf", [P, 2, TOPK])
    cand = a6("cand", [P, TOPK * TOPK])
    cand2 = a6("cand2", [P, TOPK * TOPK])
    ctop = a6("ctop", [P, TOPK])
    ci = a6("ci", [P, TOPK], U32)
    cj = a6("cj", [P, 2, TOPK], U32)
    cf = a6("cf", [P, 2, TOPK])
    pick = a6("pick", [P, 2, TOPK, TOPK])
    pick2 = a6("pick2", [P, 2, TOPK, TOPK])
    ef = a6("ef", [P, 2, TOPK])
    en = a6("en", [P, TOPK])
    shifted, expd = a6("shifted", [P, TOPK]), a6("expd", [P, TOPK])
    gsum = a6("gsum", [P, 1])
    TOP_LINKS = 23

    def top_head(dve, t, h, before, chain, shift, exped):
        n_links = [0]

        def link(ins, apart=False):
            n_links[0] += 1
            ins.then_inc(chain, 1)
            dve.wait_ge(chain, before * TOP_LINKS + n_links[0])
            if apart:
                dve.sem_inc(gone_on, 1)

        def top16(src, spare, vals, idx):
            link(nc.vector.max(vals[:, 0:8], src), apart=True)
            nc.vector.max_index(idx[:, 0:8], vals[:, 0:8], src)
            link(nc.vector.match_replace(spare, vals[:, 0:8], src, -3.0e38), apart=True)
            link(nc.vector.max(vals[:, 8:16], spare), apart=True)
            link(nc.vector.max_index(idx[:, 8:16], vals[:, 8:16], spare), apart=True)

        link(nc.vector.tensor_copy(sc_in[:, :, :], scores_s[:, t, bass.ds(h * 2, 2), :]), apart=True)
        for s in range(2):
            top16(sc_in[:, s, :], rest[:, s, :], top[:, s, :], topi[:, s, :])
        link(nc.vector.tensor_tensor(cand[:, :].rearrange("p (a b) -> p a b", a=TOPK),
                                     top[:, 0, :].rearrange("p (a b) -> p a b", b=1).broadcast_to([P, TOPK, TOPK]),
                                     top[:, 1:2, :].broadcast_to([P, TOPK, TOPK]), ALU.add), apart=True)
        top16(cand[:, :], cand2[:, :], ctop[:, :], ci[:, :])
        nc.vector.tensor_scalar(shifted[:, :], ctop[:, :], ctop[:, 0:1], None, ALU.subtract).then_inc(shift, 1)
        nc.vector.tensor_copy(topf[:, :, :], topi[:, :, :])
        nc.vector.tensor_scalar(cj[:, 0, :], ci[:, :], 4, None, ALU.logical_shift_right)
        link(nc.vector.tensor_scalar(cj[:, 1, :], ci[:, :], 15, None, ALU.bitwise_and))
        link(nc.vector.tensor_copy(cf[:, :, :], cj[:, :, :]))
        places = cst[:, C_IOTA:C_IOTA + TOPK].rearrange("p (a j) -> p a j", a=1).broadcast_to([P, 2 * TOPK, TOPK])
        link(nc.vector.tensor_tensor(pick[:, :, :, :].rearrange("p s k j -> p (s k) j"),
                                     cf[:, :, :].rearrange("p s (k j) -> p (s k) j", j=1).broadcast_to([P, 2 * TOPK, TOPK]),
                                     places, ALU.is_equal))
        for s in range(2):
            ins = nc.vector.tensor_tensor(pick2[:, s, :, :], pick[:, s, :, :], topf[:, s:s + 1, :].broadcast_to([P, TOPK, TOPK]), ALU.mult)
        link(ins)
        link(nc.vector.tensor_reduce(ef[:, :, :], pick2[:, :, :, :], AX, ALU.add))
        link(nc.vector.scalar_tensor_tensor(out=en[:, :], in0=ef[:, 0, :], scalar=float(NKEYS), in1=ef[:, 1, :],
                                            op0=ALU.mult, op1=ALU.add))
        link(nc.vector.tensor_copy(expert[:, bass.ds(h * TOPK + t * HK, TOPK)], en[:, :]))
        dve.wait_ge(exped, before + 1)
        link(nc.vector.reciprocal(gsum[:, :], gsum[:, :]))
        link(nc.vector.tensor_scalar(gate[:, t, bass.ds(h * TOPK, TOPK)], expd[:, :], gsum[:, 0:1], None, ALU.mult))
        assert n_links[0] == TOP_LINKS, n_links

    def top_exp(act, before, shift, exped):
        act.wait_ge(shift, before + 1)
        nc.scalar.activation(expd[:, :], shifted[:, :], ACT.Exp, accum_out=gsum[:, 0:1]).then_inc(exped, 1)

    k_chain, k_shift, k_exp = (sem(n) for n in ("k_chain", "k_shift", "k_exp"))
    a7 = Arena()
    xn7 = a7("xn7", [P, TT, D])
    gf = a7("gf", [P, D])
    w_pq = a7("w_pq", [P, 2, KD, 512])
    qp = a7("qp", [P, 2, SEQ])
    keys = a7("keys", [P, 2, P])
    keysT = a7("keysT", [P, 2, P])
    (gf_in, keys_in, keys_full, keys_ready, pq_full, pq_evac, ps_full, ps_evac, xf_ready) = (sem(n) for n in (
        "gf_in", "keys_in", "keys_full", "keys_ready", "pq_full", "pq_evac", "ps_full", "ps_evac", "xf_ready"))
    wpq_in = [sem("wpq_in0"), sem("wpq_in1")]
    with nc.Block() as block:
        @block.sync
        def _(sp):
            sp.dma_start(keys[:, 0, :], peer_sub_keys_1[0]).then_inc(keys_in, 16)
            sp.dma_start(keys[:, 1, :], peer_sub_keys_2[0]).then_inc(keys_in, 16)
            sp.dma_start(gf[:, :], g_ffn.partition_broadcast(P)).then_inc(gf_in, 16)
            for b in range(4):
                if b >= 2:
                    sp.wait_ge(pq_full, 4 * (b - 1))
                sp.dma_start(w_pq[:, b % 2, :, :], peer_w_q[0].rearrange("(k p) c -> p k c", p=P)[:, :, b * 512:(b + 1) * 512]).then_inc(wpq_in[b % 2], 16)
        xp_ready, xp_at = norm_transpose(block, "np", hres, TT, R_GFFN, xn7, xnT, None, 0, bank[0:2])

        @block.vector
        def _(dve):
            dve.wait_ge(gf_in, 16)
            dve.wait_ge(xp_ready, xp_at)
            for t in range(TT):
                nc.vector.tensor_tensor(xf[:, t], xn7[:, t], gf[:, :], ALU.mult).then_inc(xf_ready, 1)
            with dve.Fori(0, PH) as h:
                dve.wait_ge(ps_evac, h * 2 + 2)
                top_head(dve, 0, h, h, k_chain, k_shift, k_exp)

        @block.tensor
        def _(pe):
            pe.wait_ge(keys_in, 32)
            for s in range(2):
                mm = nc.tensor.transpose(bank[2][:, s * P:(s + 1) * P], keys[:, s, :], ident)
            mm.then_inc(keys_full, 1)
            pe.wait_ge(xp_ready, xp_at)

            def score(n):
                pe.wait_ge(pq_evac, n + 1)
                if n >= 2:
                    pe.wait_ge(ps_evac, n - 1)
                for t in range(TT):
                    mm = nc.tensor.matmul(bank[4 + n % 2][:, t * P:(t + 1) * P], qp[:, n % 2, t * P:(t + 1) * P],
                                          keysT[:, n % 2, :], start=True, stop=True)
                mm.then_inc(ps_full, 1)

            pe.wait_ge(keys_ready, 1)
            for n in range(2 * PH):
                pe.wait_ge(wpq_in[n // 4 % 2], 16 * (n // 8 + 1))
                if n >= 2:
                    pe.wait_ge(pq_evac, n - 1)
                for d in range(KD):
                    mm = nc.tensor.matmul(bank[2 + n % 2][:, :], w_pq[:, n // 4 % 2, d, n % 4 * P:(n % 4 + 1) * P], xnT[:, d, :],
                                          start=(d == 0), stop=(d == KD - 1))
                mm.then_inc(pq_full, 1)
                if n >= 1:
                    score(n - 1)
            score(2 * PH - 1)

        @block.scalar
        def _(act):
            act.wait_ge(keys_full, 1)
            nc.scalar.activation(keysT[:, :, :], bank[2][:, 0:2 * P].rearrange("p (s n) -> p s n", s=2), ACT.Copy).then_inc(keys_ready, 1)

            def evac_scores(n):
                act.wait_ge(ps_full, n + 1)
                nc.scalar.activation(scores_s[:, :, n, :], bank[4 + n % 2][:, :].rearrange("p (t n) -> p t n", t=TT), ACT.Copy).then_inc(ps_evac, 1)

            for n in range(2 * PH):
                act.wait_ge(pq_full, n + 1)
                if n >= 2:
                    act.wait_ge(ps_full, n - 1)
                nc.scalar.activation(qp[:, n % 2, :], bank[2 + n % 2][:, :], ACT.Copy).then_inc(pq_evac, 1)
                if n >= 1:
                    evac_scores(n - 1)
                if n >= 6 and n % 2 == 0:
                    top_exp(act, n // 2 - 3, k_shift, k_exp)
            evac_scores(2 * PH - 1)
            for h in range(PH - 3, PH):
                top_exp(act, h, k_shift, k_exp)
    a7.free()
    end_stage()

    G = 8
    a9 = Arena()
    stage_i = a9("stage_i", [P, 2, G], U32)
    u_rows = a9("u_rows", [P, G, D])
    v_rows = a9("v_rows", [P, G, D])
    dots = a9("dots", [P, 2, G])
    gel = a9("gel", [P, 2, G])
    wgt = a9("wgt", [P, 2, G])
    wdiag = gate_b[:, 0:4, :].rearrange("p a s -> p (a s)").rearrange("p (k j q) -> p k j q", k=2, j=G)
    zeros = a9("zeros", [P, P])
    gfin = a9("gfin", [P, D])
    out_s = gate_b[:, 4:8, :].rearrange("p a s -> p (a s)").rearrange("p (k d) -> p k d", k=2)
    sq9 = xnT[:, 0:2, :].rearrange("p a s -> p (a s)")
    fs = a9("fs", [P, TT, 4])
    eps_col = a9("eps_col", [P, 1])
    u_in = [sem(f"u_in{j}") for j in range(G)]
    v_in = [sem(f"v_in{j}") for j in range(G)]
    (staged, dot_done, gel_done, w_done, diag_done, acc_done, fin_full, z_ready, gfin_in, f_sq, f_ms, f_rt, f_chain,
     f_out, v_used) = (sem(n) for n in (
         "staged", "dot_done", "gel_done", "w_done", "diag_done", "acc_done", "fin_full", "z_ready", "gfin_in", "f_sq",
         "f_ms", "f_rt", "f_chain", "f_out", "v_used"))
    top_link, top_shift, top_exped = (sem(n) for n in ("top_link", "top_shift", "top_exped"))
    out_stored = [sem("out_stored0"), sem("out_stored1")]
    NG = HK // G
    with nc.Block() as block:
        @block.sync
        def _(sp):
            sp.dma_start(gfin[:, :], g_final.rearrange("(a d) -> a d", a=1).partition_broadcast(P)).then_inc(gfin_in, 16)
            for t in range(TT):
                sp.wait_ge(f_out, t + 1)
                sp.dma_start(out[0, t * P:(t + 1) * P, :], out_s[:, t % 2, :]).then_inc(out_stored[t % 2], 16)
            for s in out_stored:
                sp.wait_ge(s, 16 * TT // 2)

        @block.gpsimd
        def _(pool):
            for t in range(TT):
                if t >= 1:
                    pool.wait_ge(top_link, t * PH * TOP_LINKS)
                with pool.Fori(0, NG // 2) as i:
                    for k in range(2):
                        g = i * 2 + (k + t * NG)
                        nc.gpsimd.tensor_copy(stage_i[:, k, :], expert[:, bass.ds(g * G, G)]).then_inc(staged, 1)
                        pool.wait_ge(staged, g + 1)
                        for rows_, table, done, used, ahead in ((u_rows, peer_u, u_in, dot_done, 1), (v_rows, peer_v, v_in, v_used, G + 1)):
                            for j in range(G):
                                pool.wait_ge(used, g * G + j + ahead)
                                pool.sem_inc(gone_on, 1)
                                pool.indirect_dma_start(rows_[:, j, :], None, table[0],
                                                        bass.IndirectOffsetOnAxis(ap=stage_i[:, k, j:j + 1], axis=0)).then_inc(done[j], 16)

        @block.vector
        def _(dve):
            dve.sem_inc(dot_done, G)
            nc.vector.memset(zeros[:, :], 0.0).then_inc(z_ready, 1)
            nc.vector.memset(eps_col[:, :], EPS).then_inc(z_ready, 1)
            dve.wait_ge(gfin_in, 16)

            def finish(t):
                dve.wait_ge(f_rt, t + 1)
                nc.vector.reciprocal(fs[:, t, 2:3], fs[:, t, 3:4]).then_inc(f_chain, 1)
                dve.wait_ge(f_chain, t + 1)
                if t >= 2:
                    dve.wait_ge(out_stored[t % 2], 16 * (t // 2))
                for f in range(2):
                    half = slice(f * 512, (f + 1) * 512)
                    ins = nc.vector.scalar_tensor_tensor(out=out_s[:, t % 2, half], in0=bank[2 * t + f][:, :], scalar=fs[:, t, 2:3],
                                                         in1=gfin[:, half], op0=ALU.mult, op1=ALU.mult)
                ins.then_inc(f_out, 1)

            for t in range(TT):
                with dve.Fori(0, NG // 2) as i:
                    if t + 1 < TT:
                        top_head(dve, t + 1, i, i + t * PH, top_link, top_shift, top_exped)
                    for k in range(2):
                        g = i * 2 + (k + t * NG)
                        for j in range(G):
                            dve.wait_ge(u_in[j], g * 16 + 16)
                            nc.vector.tensor_tensor_reduce(u_rows[:, j, :], u_rows[:, j, :], xf[:, t, :], 1.0, 0.0, ALU.mult,
                                                           ALU.add, dots[:, k, j:j + 1]).then_inc(dot_done, 1)
                        dve.wait_ge(gel_done, g + 1)
                        nc.vector.tensor_tensor(wgt[:, k, :], gel[:, k, :], gate[:, t, bass.ds(i * 2 * G + k * G, G)], ALU.mult).then_inc(w_done, 1)
                        dve.wait_ge(w_done, g + 1)
                        dve.wait_ge(v_used, g * G + G)
                        nc.vector.tensor_tensor(wdiag[:, k, :, :], ident.rearrange("p (a q) -> p a q", a=1).broadcast_to([P, G, P]),
                                                wgt[:, k, :].rearrange("p (j a) -> p j a", a=1).broadcast_to([P, G, P]), ALU.mult).then_inc(diag_done, 1)
                if t >= 1:
                    finish(t - 1)
            finish(TT - 1)

        @block.scalar
        def _(act):
            def gelu(g, k):
                act.wait_ge(dot_done, g * G + 2 * G)
                nc.scalar.activation(gel[:, k, :], dots[:, k, :], ACT.Gelu).then_inc(gel_done, 1)
            def finish(t):
                act.wait_ge(fin_full, t + 1)
                for f in range(2):
                    nc.scalar.activation(sq9[:, f * 512:(f + 1) * 512], bank[2 * t + f][:, :], ACT.Square,
                                         accum_out=fs[:, t, f:f + 1]).then_inc(f_sq, 1)
                act.wait_ge(f_sq, 2 * t + 2)
                nc.scalar.activation(fs[:, t, 2:3], fs[:, t, 0:1], ACT.Identity, bias=fs[:, t, 1:2]).then_inc(f_ms, 1)
                act.wait_ge(f_ms, t + 1)
                nc.scalar.activation(fs[:, t, 3:4], fs[:, t, 2:3], ACT.Sqrt, scale=1.0 / D, bias=eps_col[:, :]).then_inc(f_rt, 1)

            act.wait_ge(z_ready, 2)
            for t in range(TT):
                with act.Fori(0, NG // 2) as i:
                    if t + 1 < TT:
                        top_exp(act, i + t * PH, top_shift, top_exped)
                    for k in range(2):
                        gelu(i * 2 + (k + t * NG), k)
                if t >= 1:
                    finish(t - 1)
            finish(TT - 1)

        @block.tensor
        def _(pe):
            pe.sem_inc(v_used, 2 * G)
            pe.wait_ge(z_ready, 1)
            for t in range(TT):
                for f in range(2):
                    nc.tensor.matmul(bank[2 * t + f][:, :], ident, hres[:, t, f * 512:(f + 1) * 512], start=True, stop=False,
                                     skip_group_check=True)
                with pe.Fori(0, NG // 2) as i:
                    for k in range(2):
                        g = i * 2 + (k + t * NG)
                        pe.wait_ge(diag_done, g + 1)
                        for j in range(G):
                            pe.wait_ge(v_in[j], g * 16 + 16)
                            for f in range(2):
                                mm = nc.tensor.matmul(bank[2 * t + f][:, :], wdiag[:, k, j, :], v_rows[:, j, f * 512:(f + 1) * 512],
                                                      start=False, stop=False, skip_group_check=True)
                            mm.then_inc(v_used, 1)
                for f in range(2):
                    mm = nc.tensor.matmul(bank[2 * t + f][:, :], zeros[:, :], hres[:, t, f * 512:(f + 1) * 512], start=False, stop=True,
                                          skip_group_check=True)
                mm.then_inc(fin_full, 1)


NAMES = ["x", "mem", "positions", "g_mix", "w_in", "attn_sinks", "rwkv_mu", "rwkv_w0", "rwkv_w2", "rwkv_a0", "rwkv_a2",
         "rwkv_g2", "rwkv_k_k", "rwkv_k_a", "rwkv_r_k", "rwkv_ln_w", "rwkv_ln_b", "w_out", "g_cross", "g_mem",
         "w_q_cross", "w_kv_cross", "w_o_cross", "g_ffn", "peer_w_q", "peer_sub_keys_1", "peer_sub_keys_2", "peer_u",
         "peer_v", "g_final"]



def kernel(**inputs):
    import numpy as _np
    import concourse.bacc as _bacc
    from concourse import mybir as _mybir
    from concourse.bass_utils import run_bass_kernel_spmd as _run

    nc = _bacc.Bacc("TRN2", target_bir_lowering=False, num_devices=1)
    arrays, args = {}, []
    for name in NAMES:
        a = _np.ascontiguousarray(inputs[name])
        arrays[f"in_{name}"] = a
        args.append(nc.dram_tensor(f"in_{name}", a.shape, _mybir.dt.from_np(a.dtype), kind="ExternalInput").ap())
    c = constants()
    arrays["const"] = c
    args.append(nc.dram_tensor("const", c.shape, F32, kind="ExternalInput").ap())
    args.append(nc.dram_tensor("out", (1, SEQ, D), F32, kind="ExternalOutput").ap())
    build(nc, *args)
    r = _run(nc, [arrays], core_ids=[0])
    return r.results[0]["out"]
```

```python
from contextlib import ExitStack

import numpy as np

import concourse.bass as bass
from concourse import mybir

F32 = mybir.dt.float32
BF16 = mybir.dt.bfloat16
I32 = mybir.dt.int32
U32 = mybir.dt.uint32
ALU = mybir.AluOpType
ACT = mybir.ActivationFunctionType
AX = mybir.AxisListType.X

P = 128
D = 1024
SEQ = 512
TT = SEQ // P
KD = D // P
HEAD = 64
HEADS = 16
KV = 4
CH = 64
NCH = SEQ // CH
MEM = 256
CROSS_W = 512
CROSS_H = 4
PH = 8
TOPK = 16
NKEYS = 128
EPS = 1e-5
GN_EPS = 64e-5
SQE = float(np.exp(-0.5))
TWO_PI = 2.0 * np.pi
OFF_K = 1024
OFF_RWKV = 1536
OFF_LOW = OFF_RWKV + 3 * D
OFF_GATE = OFF_LOW + 256
IN_W = OFF_GATE + 2 * D
NEG = -1e30

C_ID, C_BONES, C_ROT, C_MASK, C_BAND, C_RESET, C_IOTA, C_INVF, C_END = 0, 128, 256, 384, 640, 896, 1408, 1664, 1672

R_MU, R_W0, R_A0, R_KK, R_KA, R_RK, R_LNW, R_LNB, R_GMIX, R_GCROSS, R_GFFN, R_GMEM, R_MULOW = (
    0, 24, 32, 40, 48, 56, 64, 72, 80, 88, 96, 104, 112)
R_END = 114


def constants():
    c = np.zeros((P, C_END), np.float32)
    p = np.arange(P)
    c[:, C_ID:C_ID + P] = np.eye(P)
    c[:, C_BONES:C_BONES + P] = (p[:, None] // HEAD == p[None, :] // HEAD)
    for m in range(P):
        d = m % HEAD
        if d < 8:
            c[m + 8, C_ROT + m] = -1.0
        elif d < 16:
            c[m - 8, C_ROT + m] = 1.0
    s, t = (p % CH)[:, None], np.arange(CH)[None, :]
    for n, m in enumerate([s < t, -1.0 * (s <= t), s < t, s <= t]):
        c[:, C_MASK + n * CH:C_MASK + (n + 1) * CH] = m
    j = np.arange(2 * P)[None, :]
    c[:, C_BAND:C_BAND + 2 * P] = np.where((j > p[:, None]) & (j <= p[:, None] + P), 0.0, NEG)
    c[:, C_RESET:C_RESET + SEQ] = (np.arange(SEQ) % CH != 0)
    c[:, C_IOTA:C_IOTA + 256] = np.arange(256)
    inv = (1.0 / (np.float32(500000.0) ** (np.arange(0, 16, 2, dtype=np.float32) / np.float32(16)))).astype(np.float32)
    d = p % HEAD
    c[:, C_INVF] = np.where(d < 16, inv[d % 8], 0.0)
    return c


def build(nc, x, mem, positions, g_mix, w_in, attn_sinks, rwkv_mu, rwkv_w0, rwkv_w2, rwkv_a0, rwkv_a2, rwkv_g2,
          rwkv_k_k, rwkv_k_a, rwkv_r_k, rwkv_ln_w, rwkv_ln_b, w_out, g_cross, g_mem, w_q_cross, w_kv_cross,
          w_o_cross, g_ffn, peer_w_q, peer_sub_keys_1, peer_sub_keys_2, peer_u, peer_v, g_final, const, out,
          scratch="Internal", last=9):
    ctx = ExitStack()

    stage_sems = []

    def sem(name):
        stage_sems.append(nc.alloc_semaphore(name))
        return stage_sems[-1]

    gone_on = nc.alloc_semaphore("gone_on")

    def end_stage():
        nc.clear_and_free_semaphores(list(stage_sems))
        stage_sems.clear()
        nc.all_engine_barrier()

    def sb(name, shape, dt=F32):
        return nc.alloc_sbuf_tensor(name, shape, dt)

    def dram(name, shape):
        return nc.dram_tensor(name, shape, F32, kind=scratch).ap()

    bank = [nc.alloc_psum_tensor(f"bank{i}", [P, 512], F32) for i in range(8)]

    tok_dram = dram("tok_dram", [KD, P, 4 * SEQ])
    mats_dram = dram("mats_dram", [KD, P, 2 * 4 * 4 * CH])
    rho_dram = dram("rho_dram", [KD, P, SEQ])
    bonus_dram = dram("bonus_dram", [KD, P, SEQ])
    low_dram = dram("low_dram", [HEADS, 4, 2, CH, CH])
    inv_dram = dram("inv_dram", [HEADS, 4, 2, CH, CH])

    cst = sb("cst", [P, C_END])
    prm = sb("prm", [P, P])
    xnT = sb("xnT", [P, KD, SEQ])
    sdg = sb("sdg", [P, SEQ])
    decay_end = sb("decay_end", [P, KD, NCH])
    ident = cst[:, C_ID:C_ID + P]
    bones = cst[:, C_BONES:C_BONES + P]

    def col(row, m):
        if isinstance(m, int):
            return prm[:, row + m:row + m + 1]
        return prm[:, bass.ds(m + row, 1)]

    class Arena:

        def __init__(self):
            self.stack = ExitStack()

        def __call__(self, name, shape, dt=F32):
            return self.stack.enter_context(nc.sbuf_tensor(name, shape, dt))

        def free(self):
            self.stack.close()

    def norm_transpose(block, tag, src, n, width_row, xn, dstT, ready, ready_at, banks):
        ss, ms, rt, rs = (small[:, 8 * i:8 * i + n] for i in range(4))
        squared, scaled, rooted, normed, turned, evac = (sem(f"{tag}_{s}") for s in (
            "squared", "scaled", "rooted", "normed", "turned", "evac"))

        @block.scalar
        def _(act):
            if ready is not None:
                act.wait_ge(ready, ready_at)
            for t in range(n):
                nc.scalar.activation(xn[:, t], src[:, t], ACT.Square, accum_out=ss[:, t:t + 1]).then_inc(squared, 1)
            act.wait_ge(scaled, 1)
            nc.scalar.activation(rt, ms, ACT.Sqrt).then_inc(rooted, 1)

        @block.vector
        def _(dve):
            dve.wait_ge(squared, n)
            nc.vector.tensor_scalar(ms, ss, 1.0 / D, EPS, ALU.mult, ALU.add).then_inc(scaled, 1)
            dve.wait_ge(rooted, 1)
            nc.vector.reciprocal(rs, rt).then_inc(scaled, 1)
            dve.wait_ge(scaled, 2)
            for t in range(n):
                nc.vector.tensor_scalar(xn[:, t], src[:, t], rs[:, t:t + 1], None, ALU.mult).then_inc(normed, 1)

        @block.tensor
        def _(pe):
            pe.wait_ge(normed, n)
            for k in range(KD):
                if k >= 2:
                    pe.wait_ge(evac, k - 1)
                for t in range(n):
                    mm = nc.tensor.transpose(banks[k % 2][:, t * P:(t + 1) * P], xn[:, t, k * P:(k + 1) * P], ident)
                mm.then_inc(turned, 1)

        @block.scalar
        def _(act):
            for k in range(KD):
                act.wait_ge(turned, k + 1)
                nc.scalar.activation(dstT[:, k, 0:n * P], banks[k % 2][:, 0:n * P], ACT.Copy,
                                     scale=col(width_row, k)).then_inc(evac, 1)
        return evac, KD

    small = sb("small", [P, 64])

    def peek(name, t):
        if scratch == "Internal":
            return
        d = nc.dram_tensor("peek_" + name, list(t.shape), F32, kind="ExternalOutput").ap()
        s = sem("peek_" + name)
        with nc.Block() as block:
            @block.sync
            def _(sp):
                sp.dma_start(d, t).then_inc(s, 16)
                sp.wait_ge(s, 16)

    a0 = Arena()
    xt = a0("xt", [P, TT, D])
    xn0 = a0("xn0", [P, TT, D])
    rows = a0("rows", [P, P])
    x_in, params_in, rows_turned, prm_ready = sem("x_in"), sem("params_in"), sem("rows_turned"), sem("prm_ready")
    x_tok = x.rearrange("b (t p) d -> p (b t) d", p=P)
    with nc.Block() as block:
        @block.vector
        def _(dve):
            nc.vector.memset(rows[:, :], 0.0).then_inc(prm_ready, 1)

        @block.sync
        def _(sp):
            sp.dma_start(cst[:, :], const).then_inc(params_in, 16)
            sp.dma_start(xt[:, :, :], x_tok).then_inc(x_in, 16)
            sp.wait_ge(prm_ready, 1)
            params = [(R_MU, rwkv_mu[0, 0:3 * D]), (R_W0, rwkv_w0[0]), (R_A0, rwkv_a0[0]), (R_KK, rwkv_k_k[0]),
                      (R_KA, rwkv_k_a[0]), (R_RK, rwkv_r_k[0].rearrange("h n -> (h n)")), (R_LNW, rwkv_ln_w[0]),
                      (R_LNB, rwkv_ln_b[0]), (R_GMIX, g_mix[0]), (R_GCROSS, g_cross[0]), (R_GFFN, g_ffn[0]),
                      (R_GMEM, g_mem[0]), (R_MULOW, rwkv_mu[0, 3 * D:3 * D + 256])]
            for row, vec in params:
                v = vec.rearrange("(m p) -> m p", p=P)
                sp.dma_start(rows[row:row + v.shape[0], :], v).then_inc(params_in, 16)

        @block.tensor
        def _(pe):
            pe.wait_ge(params_in, 16 * 14)
            nc.tensor.transpose(bank[7][:, 0:P], rows[:, :], ident).then_inc(rows_turned, 1)

        @block.vector
        def _(dve):
            dve.wait_ge(rows_turned, 1)
            nc.vector.tensor_copy(prm[:, :], bank[7][:, 0:P]).then_inc(prm_ready, 1)

        @block.scalar
        def _(act):
            act.wait_ge(prm_ready, 2)
        norm_transpose(block, "nx", xt, TT, R_GMIX, xn0, xnT, x_in, 16, bank[0:2])
    a0.free()
    if last < 1:
        return

    a1 = Arena()
    lowT = a1("lowT", [P, SEQ])
    w_low = a1("w_low", [P, KD, 256])
    w3 = a1("w3", [P, 2, 3, KD, P])
    w_up = a1("w_up", [P, 2, P])
    raw = a1("raw", [P, 2, 3, SEQ + 1])
    sh = a1("sh", [P, 2, 3, SEQ])
    dlt = a1("dlt", [P, 3, SEQ])
    sgw, sga, cum, csub, pe_, pi_, pp_, kk, kk2, nrm, bonin, kap, bet, kh, bh, k2, bv = (
        a1(n, [P, 2, SEQ]) for n in ("sgw", "sga", "cum", "csub", "p_end", "p_inv", "p_prev", "kk", "kk2", "nrm",
                                     "bonin", "kap", "bet", "kh", "bh", "k2", "bv"))
    ar = a1("ar", [P, 2, 2, SEQ])
    ar_b = a1("ar_b", [P, 2, 2, SEQ])
    tok = a1("tok", [P, 2, 4, SEQ])
    mats = a1("mats", [P, 2, 2, 4, 4 * CH])

    w_cols = w_in[0].rearrange("(k p) c -> p k c", p=P)
    low_w_in, low_mm, low_raw, low_chain, low_done = (sem(s) for s in (
        "low_w_in", "low_mm", "low_raw", "low_chain", "low_done"))
    w3_in = [sem("w3_in0"), sem("w3_in1")]
    (pj_full, pj_free, za_full, za_free, sb_full, sb_free, g_full, g_free, t_full, t_free, raw_zero,
     dve_done, act_done, out_free, cum_ready, exps_ready, kk_ready, kk2_ready, nrm_ready, bon_ready,
     ops_ready, turn_ready, gates_ready, raw_ready, mats_ready, tok_ready, bv_ready, chain) = (sem(s) for s in (
         "pj_full", "pj_free", "za_full", "za_free", "sb_full", "sb_free", "g_full", "g_free", "t_full",
         "t_free", "raw_zero", "dve_done", "act_done", "out_free", "cum_ready", "exps_ready", "kk_ready",
         "kk2_ready", "nrm_ready", "bon_ready", "ops_ready", "turn_ready", "gates_ready", "raw_ready",
         "mats_ready", "tok_ready", "bv_ready", "chain"))
    ar_ready, arb_zero, arb_ready = (sem(s) for s in ("ar_ready", "arb_zero", "arb_ready"))
    store = [sem("store0"), sem("store1")]
    with nc.Block() as block:
        @block.sync
        def _(sp):
            sp.dma_start(w_low[:, :, :], w_cols[:, :, OFF_LOW:OFF_LOW + 256]).then_inc(low_w_in, 16)
            with sp.Fori(0, KD // 2) as i:
                for k in range(2):
                    m = i * 2 + k
                    sp.wait_ge(ops_ready, m + 1)
                    sp.dma_start(rho_dram[bass.ds(m, 1)].rearrange("a p s -> (a p) s"), ar[:, k, 1, :]).then_inc(store[k], 16)
                    sp.wait_ge(bv_ready, m + 1)
                    sp.dma_start(bonus_dram[bass.ds(m, 1)].rearrange("a p s -> (a p) s"), bv[:, k, :]).then_inc(store[k], 16)
                    sp.wait_ge(mats_ready, m * 4 + 4)
                    sp.dma_start(mats_dram[bass.ds(m, 1)].rearrange("a p s -> (a p) s"),
                                 mats[:, k, :, :, :].rearrange("p h c n -> p (h c n)")).then_inc(store[k], 16)
                    for par in range(2):
                        sp.dma_start(
                            low_dram[bass.ds(m * 2, 2), :, par].rearrange("h c s t -> s (h c) t"),
                            mats[par * CH:(par + 1) * CH, k, :, :, 0:CH].rearrange("p h c n -> p (h c) n")).then_inc(store[k], 16)
                    sp.wait_ge(tok_ready, m * 4 + 4)
                    sp.dma_start(tok_dram[bass.ds(m, 1)].rearrange("a p s -> (a p) s"),
                                 tok[:, k, :, :].rearrange("p a s -> p (a s)")).then_inc(store[k], 16)
                    sp.wait_ge(store[k], i * 96 + 96)
                    sp.sem_inc(out_free, 1)

        @block.gpsimd
        def _(pool):
            def loads(m, k):
                for t in range(3):
                    pool.wait_ge(pj_full, m * 3 + t + 1)
                    pool.sem_inc(gone_on, 1)
                    pool.dma_start(w3[:, k, t, :, :], w_cols[:, :, bass.ds(m * P + (OFF_RWKV + t * D), P)]).then_inc(w3_in[k], 16)
                pool.wait_ge(za_full, m * 2 + 2)
                pool.sem_inc(gone_on, 1)
                pool.dma_start(w_up[0:64, k, :], rwkv_w2[0][:, bass.ds(m * P, P)]).then_inc(w3_in[k], 16)
                pool.dma_start(w_up[64:128, k, :], rwkv_a2[0][:, bass.ds(m * P, P)]).then_inc(w3_in[k], 16)

            with pool.Fori(0, KD // 2) as i:
                for k in range(2):
                    loads(i * 2 + k, k)

        @block.tensor
        def _(pe):
            pe.sem_inc(pj_full, 6)
            pe.sem_inc(za_full, 4)
            pe.sem_inc(t_full, 8)
            pe.wait_ge(low_w_in, 16)
            for t in range(2):
                for k in range(KD):
                    mm = nc.tensor.matmul(bank[2 + t][:, :], w_low[:, k, t * P:(t + 1) * P], xnT[:, k, :],
                                          start=(k == 0), stop=(k == KD - 1))
                mm.then_inc(low_mm, 1)

            def project(m, i, k, t):
                pe.wait_ge(pj_free, m * 3 + t + 1)
                for d in range(KD):
                    mm = nc.tensor.matmul(bank[(3 * k + t) % 2][:, :], w3[:, k, t, d, :], xnT[:, d, :],
                                          start=(d == 0), stop=(d == KD - 1))
                mm.then_inc(pj_full, 1)

            def up(m, k, which=(0, 1)):
                for t in which:
                    pe.wait_ge(za_free, m * 2 + t + 1)
                    r = slice(64 * t, 64 * t + 64)
                    nc.tensor.matmul(bank[2][:, :], w_up[r, k, :], lowT[r, :], start=True, stop=True).then_inc(za_full, 1)

            def head_sums(m, k):
                pe.wait_ge(kk2_ready, m + 1)
                pe.wait_ge(sb_free, m * 2 + 1)
                nc.tensor.matmul(bank[3][:, :], bones, kk2[:, k, :], start=True, stop=True).then_inc(sb_full, 1)
                pe.wait_ge(bon_ready, m + 1)
                pe.wait_ge(sb_free, m * 2 + 2)
                nc.tensor.matmul(bank[3][:, :], bones, bonin[:, k, :], start=True, stop=True).then_inc(sb_full, 1)

            def chunk_products(m, k):
                pe.wait_ge(arb_ready, m + 1)
                for qq in range(2):
                    for j in range(2):
                        pe.wait_ge(g_free, m * 4 + 2 * qq + j + 1)
                        pe.sem_inc(gone_on, 1)
                        for c in range(4 * qq + 2 * j, 4 * qq + 2 * j + 2):
                            cb = slice(64 * (c % 2), 64 * (c % 2) + 64)
                            t = slice(c * CH, (c + 1) * CH)
                            dst = bank[4 + j][cb, :].rearrange("p (h n a t) -> p h n a t", h=2, n=2, a=2)
                            for n, left in enumerate((bet, kap)):
                                mm = nc.tensor.matmul(dst[:, :, n], left[:, k, t], ar_b[:, :, :, t].rearrange("p a h t -> p h a t"),
                                                      start=True, stop=True)
                        mm.then_inc(g_full, 1)

            def turns(m, k):
                pe.wait_ge(turn_ready, m + 1)
                for a, src in enumerate((ar[:, k, 0, :], sh[:, k, 2, :], kh[:, k, :], bh[:, k, :])):
                    pe.wait_ge(t_free, m * 4 + a + 1)
                    for t in range(TT):
                        mm = nc.tensor.transpose(bank[6 + a % 2][:, t * P:(t + 1) * P], src[:, t * P:(t + 1) * P], ident)
                    mm.then_inc(t_full, 1)

            def step(m, i, k, nxt, i2, k2_):
                pe.wait_ge(w3_in[k2_], i2 * 80 + 80)
                project(nxt, i2, k2_, 0)
                head_sums(m, k)
                project(nxt, i2, k2_, 1)
                project(nxt, i2, k2_, 2)
                turns(m, k)
                up(nxt, k2_, (0,))
                chunk_products(m, k)
                up(nxt, k2_, (1,))

            pe.wait_ge(low_done, 3)
            pe.wait_ge(w3_in[0], 80)
            for t in range(3):
                project(0, 0, 0, t)
            up(0, 0)
            with pe.Fori(0, KD // 2 - 1) as i:
                step(i * 2, i, 0, i * 2 + 1, i, 1)
                step(i * 2 + 1, i, 1, i * 2 + 2, i + 1, 0)
            step(KD - 2, 0, 0, KD - 1, KD // 2 - 1, 1)
            head_sums(KD - 1, 1)
            turns(KD - 1, 1)
            chunk_products(KD - 1, 1)

        @block.scalar
        def _(act):
            act.sem_inc(pj_free, 2)
            act.sem_inc(za_free, 1)
            act.sem_inc(t_free, 2)
            act.sem_inc(act_done, 2)
            act.wait_ge(raw_zero, 1)
            for t in range(2):
                act.wait_ge(low_mm, t + 1)
                nc.scalar.activation(raw[:, 0, t, 1:SEQ + 1], bank[2 + t][:, :], ACT.Copy).then_inc(low_raw, 1)
            act.wait_ge(low_chain, 4)
            nc.scalar.activation(lowT[0:64, :], sh[0:64, 0, 0, :], ACT.Tanh).then_inc(low_done, 1)
            nc.scalar.activation(lowT[64:128, :], sh[64:128, 0, 0, :], ACT.Copy).then_inc(low_done, 1)
            nc.scalar.activation(sdg[:, :], sh[:, 0, 1, :], ACT.Sigmoid).then_inc(low_done, 1)
            act.wait_ge(low_done, 3)
            def evac_raw(m, k, t):
                act.wait_ge(pj_full, m * 3 + t + 7)
                nc.scalar.activation(raw[:, k, t, 1:SEQ + 1], bank[(3 * k + t) % 2][:, :], ACT.Copy).then_inc(raw_ready, 1)
                act.wait_ge(raw_ready, m * 3 + t + 1)
                act.sem_inc(pj_free, 1)

            def gates(m, k):
                for t, (dst, bias) in enumerate(((sgw, R_W0), (sga, R_A0))):
                    act.wait_ge(za_full, m * 2 + t + 5)
                    nc.scalar.activation(dst[:, k, :], bank[2][:, :], ACT.Sigmoid, bias=col(bias, m)).then_inc(gates_ready, 1)
                    act.wait_ge(gates_ready, m * 2 + t + 1)
                    act.sem_inc(za_free, 1)

            def exps(m, k):
                act.wait_ge(kk_ready, m + 1)
                nc.scalar.activation(kk2[:, k, :], kk[:, k, :], ACT.Square).then_inc(kk2_ready, 1)
                act.wait_ge(cum_ready, m + 1)
                nc.scalar.activation(pe_[:, k, :], cum[:, k, :], ACT.Exp, scale=-SQE).then_inc(exps_ready, 1)
                nc.scalar.activation(pi_[:, k, :], cum[:, k, :], ACT.Exp, scale=SQE).then_inc(exps_ready, 1)
                nc.scalar.activation(pp_[:, k, :], csub[:, k, :], ACT.Exp, scale=-SQE).then_inc(exps_ready, 1)

            def norm_root(m, k):
                act.wait_ge(sb_full, m * 2 + 1)
                nc.scalar.activation(nrm[:, k, :], bank[3][:, :], ACT.Sqrt).then_inc(nrm_ready, 1)

            def evac_turns(m, k):
                act.wait_ge(out_free, m + 1)
                for a in range(4):
                    act.wait_ge(t_full, m * 4 + a + 9)
                    nc.scalar.activation(tok[:, k, a, :], bank[6 + a % 2][:, :], ACT.Copy).then_inc(tok_ready, 1)
                    act.wait_ge(tok_ready, m * 4 + a + 1)
                    act.sem_inc(t_free, 1)
                act.sem_inc(act_done, 1)

            def blocks(m, k):
                act.wait_ge(ar_ready, m + 1)
                act.wait_ge(g_free, m * 4 + 2)
                for n in range(2):
                    for h in range(2):
                        hb = slice(64 * h, 64 * h + 64)
                        ins = nc.scalar.activation(ar_b[hb, n, h, :], ar[hb, k, n, :], ACT.Copy)
                ins.then_inc(arb_ready, 1)

            act.wait_ge(arb_zero, 1)

            def front(m, k, m_before=None, k_before=None):
                act.wait_ge(dve_done, m + 1)
                evac_raw(m, k, 0)
                if m_before is not None:
                    norm_root(m_before, k_before)
                evac_raw(m, k, 1)
                if m_before is not None:
                    blocks(m_before, k_before)
                evac_raw(m, k, 2)
                if m_before is not None:
                    evac_turns(m_before, k_before)
                gates(m, k)
                act.wait_ge(t_full, m * 4 + 4)
                exps(m, k)

            front(0, 0)
            with act.Fori(0, KD // 2 - 1) as i:
                front(i * 2 + 1, 1, i * 2, 0)
                front(i * 2 + 2, 0, i * 2 + 1, 1)
            front(KD - 1, 1, KD - 2, 0)
            norm_root(KD - 1, 1)
            blocks(KD - 1, 1)
            evac_turns(KD - 1, 1)

        LINKS = 19

        @block.vector
        def _(dve):
            dve.sem_inc(dve_done, 2)
            dve.sem_inc(sb_free, 1)
            dve.sem_inc(g_free, 2)
            dve.sem_inc(out_free, 2)
            nc.vector.memset(raw[:, :, :, 0:1], 0.0).then_inc(raw_zero, 1)
            dve.wait_ge(raw_zero, 1)
            nc.vector.memset(ar_b[:, :, :, :], 0.0).then_inc(arb_zero, 1)
            for t in range(2):
                dve.wait_ge(low_raw, t + 1)
                nc.vector.tensor_tensor(dlt[:, t, :], raw[:, 0, t, 0:SEQ], raw[:, 0, t, 1:SEQ + 1], ALU.subtract).then_inc(low_chain, 1)
                dve.wait_ge(low_chain, 2 * t + 1)
                nc.vector.scalar_tensor_tensor(out=sh[:, 0, t, :], in0=dlt[:, t, :], scalar=col(R_MULOW, t),
                                               in1=raw[:, 0, t, 1:SEQ + 1], op0=ALU.mult, op1=ALU.add).then_inc(low_chain, 1)
            dve.wait_ge(low_done, 3)
            with dve.Fori(0, KD // 2) as i:
                for k in range(2):
                    m = i * 2 + k
                    count = [0]

                    def link(ins):
                        count[0] += 1
                        ins.then_inc(chain, 1)
                        dve.wait_ge(chain, m * LINKS + count[0])

                    dve.wait_ge(t_full, m * 4 + 4)
                    dve.wait_ge(act_done, m + 1)
                    dve.wait_ge(out_free, m + 1)
                    r_, k_, v_ = (sh[:, k, t, :] for t in range(3))
                    alpha, rho = ar[:, k, 0, :], ar[:, k, 1, :]
                    for t in (1, 0, 2):
                        dve.wait_ge(raw_ready, m * 3 + t + 1)
                        link(nc.vector.tensor_tensor(dlt[:, t, :], raw[:, k, t, 0:SEQ], raw[:, k, t, 1:SEQ + 1], ALU.subtract))
                        link(nc.vector.scalar_tensor_tensor(out=sh[:, k, t, :], in0=dlt[:, t, :], scalar=col(R_MU + 8 * t, m),
                                                            in1=raw[:, k, t, 1:SEQ + 1], op0=ALU.mult, op1=ALU.add))
                        if t == 1:
                            link(nc.vector.tensor_scalar(kk[:, k, :], k_, col(R_KK, m), None, ALU.mult))
                            dve.sem_inc(kk_ready, 1)
                    dve.wait_ge(gates_ready, m * 2 + 1)
                    link(nc.vector.tensor_tensor_scan(cum[:, k, :], cst[:, C_RESET:C_RESET + SEQ], sgw[:, k, :], 0.0, ALU.mult, ALU.add))
                    link(nc.vector.tensor_tensor(csub[:, k, :], cum[:, k, :], sgw[:, k, :], ALU.subtract))
                    dve.sem_inc(cum_ready, 1)
                    dve.wait_ge(gates_ready, m * 2 + 2)
                    link(nc.vector.tensor_scalar(k2[:, k, :], sga[:, k, :], 1.0, col(R_KA, m), ALU.subtract, ALU.mult))
                    link(nc.vector.scalar_tensor_tensor(out=k2[:, k, :], in0=k2[:, k, :], scalar=1.0, in1=k_, op0=ALU.add, op1=ALU.mult))
                    link(nc.vector.scalar_tensor_tensor(out=bonin[:, k, :], in0=r_, scalar=col(R_RK, m), in1=k2[:, k, :],
                                                        op0=ALU.mult, op1=ALU.mult))
                    dve.sem_inc(bon_ready, 1)
                    dve.wait_ge(nrm_ready, m + 1)
                    dve.sem_inc(sb_free, 1)
                    link(nc.vector.tensor_scalar(nrm[:, k, :], nrm[:, k, :], 1e-12, None, ALU.max))
                    link(nc.vector.reciprocal(nrm[:, k, :], nrm[:, k, :]))
                    link(nc.vector.tensor_tensor(kk[:, k, :], kk[:, k, :], nrm[:, k, :], ALU.mult))
                    dve.wait_ge(exps_ready, m * 3 + 3)
                    nc.vector.tensor_copy(decay_end[:, bass.ds(m, 1), :].rearrange("p a c -> p (a c)"), pe_[:, k, CH - 1::CH])
                    nc.vector.tensor_tensor(alpha, kk[:, k, :], pp_[:, k, :], ALU.mult)
                    nc.vector.tensor_tensor(rho, r_, pe_[:, k, :], ALU.mult)
                    link(nc.vector.tensor_tensor(bet[:, k, :], kk[:, k, :], sga[:, k, :], ALU.mult))
                    dve.sem_inc(ar_ready, 1)
                    nc.vector.tensor_tensor(kap[:, k, :], k2[:, k, :], pi_[:, k, :], ALU.mult)
                    link(nc.vector.tensor_tensor(bet[:, k, :], bet[:, k, :], pi_[:, k, :], ALU.mult))
                    dve.sem_inc(ops_ready, 1)
                    chunks = lambda t: t[:, k, :].rearrange("p (c t) -> p c t", t=CH)
                    last_decay = chunks(pe_)[:, :, CH - 1:CH].broadcast_to([P, NCH, CH])
                    nc.vector.tensor_tensor(chunks(kh), chunks(kap), last_decay, ALU.mult)
                    link(nc.vector.scalar_tensor_tensor(out=chunks(bh), in0=chunks(bet), scalar=-1.0, in1=last_decay,
                                                        op0=ALU.mult, op1=ALU.mult))
                    dve.sem_inc(turn_ready, 1)
                    dve.wait_ge(sb_full, m * 2 + 2)
                    link(nc.vector.tensor_tensor(bv[:, k, :], bank[3][:, :], v_, ALU.mult))
                    dve.sem_inc(sb_free, 1)
                    dve.sem_inc(bv_ready, 1)
                    mask = cst[:, C_MASK:C_MASK + 256].rearrange("p (a n) -> p a n", a=1).broadcast_to([P, 2, 256])
                    for f in range(4):
                        dve.wait_ge(g_full, m * 4 + f + 1)
                        nc.vector.tensor_tensor(mats[:, k, :, f, :], bank[4 + f % 2][:, :].rearrange("p (h n) -> p h n", h=2),
                                                mask, ALU.mult).then_inc(mats_ready, 1)
                        dve.wait_ge(mats_ready, m * 4 + f + 1)
                        dve.sem_inc(g_free, 1)
                    dve.sem_inc(dve_done, 1)
                    assert count[0] == LINKS, count
    a1.free()
    end_stage()
    if last < 2:
        return

    mix = sb("mix", [P, KD, SEQ])
    gate_b = sb("gate_b", [P, KD, SEQ])
    a2 = Arena()
    lo = a2("lo", [P, CH, CH])
    ti = a2("ti", [P, CH, CH])
    upd = a2("upd", [P, CH * CH // 4])
    wr = a2("wr", [P, 3, KD, 512])
    qk = a2("qk", [P, 10, SEQ])
    vt = a2("vt", [P, TT, KV * HEAD])
    rope_tmp = a2("rope_tmp", [P, 2, SEQ])
    rope_sin_x = a2("rope_sin_x", [P, 2, SEQ])
    cos_t, sin_t, ang, turn = (a2(n, [P, SEQ]) for n in ("cos_t", "sin_t", "ang", "turn"))
    pos_i = a2("pos_i", [P, SEQ], positions.tensor.dtype)
    sink = a2("sink", [P, HEADS])
    kp = a2("kp", [P, 2, 2, SEQ])
    nsink = a2("nsink", [P, HEADS])
    band = a2("band", [P, 2, 2 * P], BF16)
    ident_b = a2("ident_b", [P, P], BF16)
    pr = a2("pr", [P, 4, 2, 2 * P])
    prT = a2("prT", [P, 2, 512])
    inv_sum = upd[:, :].rearrange("p (i h q) -> p i h q", i=4, h=2)
    mx, nmx, sums, es, sd, rec = (a2(n, [P, 4, 2]) for n in ("mx", "nmx", "sums", "es", "sd", "rec"))

    lo_in, tab_in, sink_in, lo_chain, ti_ready, ti_stored, pos_ready = (sem(n) for n in (
        "lo_in", "tab_in", "sink_in", "lo_chain", "ti_ready", "ti_stored", "pos_ready"))
    wr_in = [sem(f"wr_in{n}") for n in range(3)]
    f_full, f_evac, tab_done, rot_full, rope_x, rope_s, roped = (sem(n) for n in (
        "f_full", "f_evac", "tab_done", "rot_full", "rope_x", "rope_s", "roped"))
    s_full, mx_ready, p_ready, rec_ready, inv_ready, pt_full, pt_ready, o_full, o_used, att_chain, kp_zero, band_ready = (
        sem(n) for n in ("s_full", "mx_ready", "p_ready", "rec_ready", "inv_ready", "pt_full", "pt_ready", "o_full",
                         "o_used", "att_chain", "kp_zero", "band_ready"))
    w_blocks = [0, 512, 1024] + [OFF_GATE + 512 * n for n in range(4)]
    fills = ([("q", b, g) for b in range(2) for g in range(4)] + [("k", 2, g) for g in range(2)]
             + [("v", 2, t) for t in range(TT)] + [("a", 3 + b, g) for b in range(2) for g in range(4)]
             + [("b", 5 + b, g) for b in range(2) for g in range(4)])
    units = [(pp, n, g) for pp in range(2) for n in range(TT) for g in range(4)]
    NU = len(units)
    with nc.Block() as block:
        @block.sync
        def _(sp):
            sp.dma_start(pos_i[:, :], positions.partition_broadcast(P)).then_inc(tab_in, 16)
            sp.dma_start(sink[:, :], attn_sinks.partition_broadcast(P)).then_inc(sink_in, 16)
            for n, c in enumerate(w_blocks):
                if n >= 3:
                    sp.wait_ge(f_full, 1 + max(i for i, f in enumerate(fills) if f[1] == n - 3))
                if n < 2:
                    for d in range(KD):
                        for a in range(2):
                            sp.dma_start(wr[:, n, d, :].rearrange("p (g a j) -> p g a j", a=2, g=4)[:, :, a, :],
                                         w_cols[:, d, c + 256 * a:c + 256 * a + 256].rearrange("p (g j) -> p g j", g=4))\
                                .then_inc(wr_in[n], 16)
                    if n == 0:
                        sp.dma_start(lo[:, :, :], low_dram.rearrange("h q c s t -> (h q c) s t")).then_inc(lo_in, 16)
                else:
                    sp.dma_start(wr[:, n % 3, :, :], w_cols[:, :, c:c + 512]).then_inc(wr_in[n % 3], 16)
            sp.wait_ge(ti_ready, 1)
            sp.dma_start(inv_dram.rearrange("h q c s t -> (h q c) s t"), ti[:, :, :]).then_inc(ti_stored, 16)
            sp.wait_ge(ti_stored, 16)

        @block.vector
        def _(dve):
            n = [0]

            def link(ins):
                n[0] += 1
                ins.then_inc(pos_ready, 1)
                dve.wait_ge(pos_ready, n[0])

            dve.wait_ge(tab_in, 16)
            link(nc.vector.tensor_copy(ang[:, :], pos_i[:, :]))
            link(nc.vector.tensor_scalar(ang[:, :], ang[:, :], cst[:, C_INVF:C_INVF + 1], None, ALU.mult))
            magic = 1.5 * 2 ** 23
            for dst, quarter in ((sin_t, 0.0), (cos_t, 0.25)):
                link(nc.vector.tensor_scalar(turn[:, :], ang[:, :], 1.0 / TWO_PI, quarter, ALU.mult, ALU.add))
                link(nc.vector.tensor_scalar(turn[:, :], turn[:, :], magic, magic, ALU.add, ALU.subtract))
                hi = 6.28125
                mid = float(np.float32(TWO_PI - hi).view(np.uint32) & np.uint32(0xFFFFF000))
                mid = float(np.uint32(np.float32(TWO_PI - hi).view(np.uint32) & np.uint32(0xFFFFF000)).view(np.float32))
                low = float(TWO_PI - hi - mid)
                link(nc.vector.scalar_tensor_tensor(out=dst[:, :], in0=turn[:, :], scalar=-hi, in1=ang[:, :], op0=ALU.mult, op1=ALU.add))
                link(nc.vector.scalar_tensor_tensor(out=dst[:, :], in0=turn[:, :], scalar=-mid, in1=dst[:, :], op0=ALU.mult, op1=ALU.add))
                link(nc.vector.scalar_tensor_tensor(out=dst[:, :], in0=turn[:, :], scalar=-low, in1=dst[:, :], op0=ALU.mult, op1=ALU.add))
                if quarter:
                    link(nc.vector.tensor_scalar(dst[:, :], dst[:, :], float(np.pi / 2), None, ALU.add))
                link(nc.vector.tensor_scalar(dst[:, :], dst[:, :], 3.1415925, -3.1415925, ALU.min, ALU.max))
            dve.sem_inc(tab_done, 1)
            nc.vector.tensor_copy(ident_b[:, :], ident).then_inc(band_ready, 1)
            for h in range(2):
                nc.vector.tensor_copy(band[:, h, :], cst[:, C_BAND:C_BAND + 2 * P]).then_inc(band_ready, 1)
            dve.wait_ge(sink_in, 16)
            nc.vector.tensor_scalar(nsink[:, :], sink[:, :], -1.0, None, ALU.mult).then_inc(band_ready, 1)

            def rope(i):
                if i == 0:
                    dve.wait_ge(tab_done, 3)
                dve.wait_ge(rot_full, i + 1)
                nc.vector.tensor_tensor(rope_sin_x[:, i % 2, :], bank[2 + i % 6][:, :], sin_t[:, :], ALU.mult).then_inc(rope_s, 1)
                dve.wait_ge(rope_s, i + 1)
                dve.wait_ge(rope_x, i + 1)
                if i < 8:
                    ins = nc.vector.tensor_tensor(qk[:, i, :], rope_tmp[:, i % 2, :], rope_sin_x[:, i % 2, :], ALU.add)
                else:
                    dve.wait_ge(kp_zero, 1)
                    for h in range(2):
                        hb = slice(64 * h, 64 * h + 64)
                        ins = nc.vector.tensor_tensor(kp[hb, i - 8, h, :], rope_tmp[hb, i % 2, :], rope_sin_x[hb, i % 2, :], ALU.add)
                ins.then_inc(roped, 1)

            n[0] = 0

            def follow(ins):
                n[0] += 1
                ins.then_inc(lo_chain, 1)
                dve.wait_ge(lo_chain, n[0])

            follow(nc.vector.memset(ti[:, :, :], 0.0))
            follow(nc.vector.memset(ti[:, :, :].rearrange("p s t -> p (s t)")[:, ::CH + 1], 1.0))
            dve.wait_ge(lo_in, 16)
            for j in range(CH - 1):
                r, c = j + 1, CH - 1 - j
                u = upd[:, 0:r * c].rearrange("p (r c) -> p r c", c=c)
                follow(nc.vector.tensor_tensor(u, ti[:, 0:r, j:j + 1].broadcast_to([P, r, c]),
                                               lo[:, j:j + 1, j + 1:].broadcast_to([P, r, c]), ALU.mult))
                follow(nc.vector.tensor_tensor(ti[:, 0:r, j + 1:], ti[:, 0:r, j + 1:], u, ALU.subtract))
                if j % 5 == 4 and j // 5 < 10 + 2 and j // 5 >= 2:
                    rope(j // 5 - 2)
            dve.sem_inc(ti_ready, 1)

        @block.tensor
        def _(pe):
            def rot(i):
                pe.wait_ge(f_evac, i + 1)
                if i >= 6:
                    pe.wait_ge(rope_s, i - 5)
                nc.tensor.matmul(bank[2 + i % 6][:, :], cst[:, C_ROT:C_ROT + P], qk[:, i, :], start=True, stop=True).then_inc(rot_full, 1)

            for i, (kind, b, g) in enumerate(fills):
                pe.wait_ge(wr_in[b % 3], 16 * (b // 3 + 1) + (240 if b % 3 < 2 else 0))
                if i >= 2:
                    pe.wait_ge(f_evac, i - 1)
                w = wr[:, b % 3, :, :]
                for d in range(KD):
                    st = dict(start=(d == 0), stop=(d == KD - 1))
                    if kind == "v":
                        mm = nc.tensor.matmul(bank[i % 2][:, 0:256], xnT[:, d, g * P:(g + 1) * P], w[:, d, 256:512], **st)
                    else:
                        mm = nc.tensor.matmul(bank[i % 2][:, :], w[:, d, g * P:(g + 1) * P], xnT[:, d, :], **st)
                mm.then_inc(f_full, 1)
                if 2 <= i <= 20 and i % 2 == 0:
                    rot(i // 2 - 1)

            def scores(u):
                pp, n, g = units[u]
                if u >= 4:
                    pe.wait_ge(p_ready, u - 3)
                k0, width = (0, P) if n == 0 else ((n - 1) * P, 2 * P)
                first = P if n == 0 else 0
                dst = bank[u % 4][:, :].rearrange("p (h k) -> p h k", h=2)[:, :, 0:width]
                nc.tensor.matmul(dst, qk[:, 4 * pp + g, n * P:(n + 1) * P], kp[:, pp, :, k0:k0 + width], start=True, stop=False)
                nc.tensor.matmul(dst, ident_b[:, :], band[:, :, first:2 * P], start=False, stop=True).then_inc(s_full, 1)

            def turn_p(u):
                n = units[u][1]
                pe.wait_ge(inv_ready, u + 1)
                if u >= 2:
                    pe.wait_ge(pt_ready, u - 1)
                for h in range(2):
                    for s in range(1 if n == 0 else 2):
                        mm = nc.tensor.matmul(bank[4 + u % 2][:, (2 * h + s) * P:(2 * h + s + 1) * P],
                                              pr[:, u % 4, h, s * P:(s + 1) * P], inv_sum[:, u % 4, h, :], start=True, stop=True)
                mm.then_inc(pt_full, 1)

            def weigh(u):
                pp, n, g = units[u]
                pe.wait_ge(pt_ready, u + 1)
                if u >= 2:
                    pe.wait_ge(o_used, u - 1)
                ob = slice(64 * (g % 2), 64 * (g % 2) + 64)
                tiles = [0] if n == 0 else [n - 1, n]
                for h in range(2):
                    kv = 2 * pp + h
                    for s, t in enumerate(tiles):
                        mm = nc.tensor.matmul(bank[6 + u % 2][ob, h * P:(h + 1) * P], vt[:, t, kv * HEAD:(kv + 1) * HEAD],
                                              prT[:, u % 2, (2 * h + s) * P:(2 * h + s + 1) * P],
                                              start=(s == 0), stop=(s == len(tiles) - 1))
                mm.then_inc(o_full, 1)

            pe.wait_ge(roped, 10)
            pe.wait_ge(band_ready, 4)
            pe.wait_ge(f_evac, len(fills))
            for u in range(NU + 4):
                if u < NU:
                    scores(u)
                if 3 <= u < NU + 3:
                    turn_p(u - 3)
                if u >= 4:
                    weigh(u - 4)

        @block.scalar
        def _(act):
            act.wait_ge(tab_done, 1)
            nc.scalar.activation(sin_t[:, :], sin_t[:, :], ACT.Sin).then_inc(tab_done, 1)
            nc.scalar.activation(cos_t[:, :], cos_t[:, :], ACT.Sin).then_inc(tab_done, 1)
            for i, (kind, b, g) in enumerate(fills):
                act.wait_ge(f_full, i + 1)
                src = bank[i % 2][:, :]
                if kind == "q":
                    nc.scalar.activation(qk[:, 4 * b + g, :], src, ACT.Copy, scale=HEAD ** -0.5).then_inc(f_evac, 1)
                elif kind == "k":
                    nc.scalar.activation(qk[:, 8 + g, :], src, ACT.Copy).then_inc(f_evac, 1)
                elif kind == "v":
                    nc.scalar.activation(vt[:, g, :], src[:, 0:256], ACT.Copy).then_inc(f_evac, 1)
                elif kind == "a":
                    nc.scalar.activation(mix[:, 4 * (b - 3) + g, :], src, ACT.Sigmoid).then_inc(f_evac, 1)
                else:
                    nc.scalar.activation(gate_b[:, 4 * (b - 5) + g, :], src, ACT.Sigmoid).then_inc(f_evac, 1)

            def exps(u):
                width = P if units[u][1] == 0 else 2 * P
                act.wait_ge(mx_ready, u + 1)
                if u >= 4:
                    act.wait_ge(pt_full, u - 3)
                for h in range(2):
                    nc.scalar.activation(pr[:, u % 4, h, 0:width], bank[u % 4][:, h * 2 * P:h * 2 * P + width], ACT.Exp,
                                         bias=nmx[:, u % 4, h:h + 1], accum_out=sums[:, u % 4, h:h + 1])
                nc.scalar.activation(es[:, u % 4, :], sd[:, u % 4, :], ACT.Exp).then_inc(p_ready, 1)

            def evac_p(u):
                act.wait_ge(pt_full, u + 1)
                if u >= 2:
                    act.wait_ge(o_full, u - 1)
                n = units[u][1]
                if n == 0:
                    v = prT[:, u % 2, :].rearrange("p (h s q) -> p h s q", h=2, s=2)[:, :, 0, :]
                    w = bank[4 + u % 2][:, :].rearrange("p (h s q) -> p h s q", h=2, s=2)[:, :, 0, :]
                else:
                    v, w = prT[:, u % 2, :], bank[4 + u % 2][:, :]
                nc.scalar.activation(v, w, ACT.Copy).then_inc(pt_ready, 1)

            for u in range(NU + 3):
                if u < NU:
                    exps(u)
                if u >= 3:
                    evac_p(u - 3)

        @block.gpsimd
        def _(pool):
            nc.gpsimd.memset(kp[:, :, :, :], 0.0).then_inc(kp_zero, 1)
            pool.wait_ge(tab_done, 3)
            for i in range(10):
                pool.wait_ge(f_evac, i + 1)
                if i >= 2:
                    pool.wait_ge(roped, i - 1)
                nc.gpsimd.tensor_tensor(rope_tmp[:, i % 2, :], qk[:, i, :], cos_t[:, :], ALU.mult).then_inc(rope_x, 1)
            for u in range(NU):
                pool.wait_ge(rec_ready, u + 1)
                if u >= 4:
                    pool.wait_ge(pt_full, u - 3)
                nc.gpsimd.tensor_tensor(inv_sum[:, u % 4, :, :], ident.rearrange("p (a q) -> p a q", a=1).broadcast_to([P, 2, P]),
                                        rec[:, u % 4, :].rearrange("p (h a) -> p h a", a=1).broadcast_to([P, 2, P]), ALU.mult)\
                    .then_inc(inv_ready, 1)

        @block.vector
        def _(dve):
            n_links = [0]

            def link(ins):
                n_links[0] += 1
                ins.then_inc(att_chain, 1)
                dve.wait_ge(att_chain, n_links[0])

            def maxes(u):
                pp, n, g = units[u]
                i, width = u % 4, (P if n == 0 else 2 * P)
                dve.wait_ge(s_full, u + 1)
                link(nc.vector.tensor_reduce(mx[:, i, :], bank[i][:, :].rearrange("p (h k) -> p h k", h=2)[:, :, 0:width], AX, ALU.max))
                of_pair = slice(8 * pp + g, 8 * pp + g + 5, 4)
                link(nc.vector.scalar_tensor_tensor(out=nmx[:, i, :], in0=mx[:, i, :], scalar=-1.0, in1=nsink[:, of_pair],
                                                    op0=ALU.mult, op1=ALU.min))
                nc.vector.tensor_tensor(sd[:, i, :], sink[:, of_pair], nmx[:, i, :], ALU.add).then_inc(mx_ready, 1)

            def over_sum(u):
                i = u % 4
                dve.wait_ge(p_ready, u + 1)
                link(nc.vector.tensor_tensor(rec[:, i, :], sums[:, i, :], es[:, i, :], ALU.add))
                nc.vector.reciprocal(rec[:, i, :], rec[:, i, :]).then_inc(rec_ready, 1)

            def gated(u):
                pp, n, g = units[u]
                dve.wait_ge(o_full, u + 1)
                ob = slice(64 * (g % 2), 64 * (g % 2) + 64)
                m0 = 4 * pp + g // 2
                for h in range(2):
                    v = mix[ob, m0 + 2 * h, n * P:(n + 1) * P]
                    ins = nc.vector.tensor_tensor(v, bank[6 + u % 2][ob, h * P:(h + 1) * P], v, ALU.mult)
                ins.then_inc(o_used, 1)

            for u in range(NU + 5):
                if u < NU:
                    maxes(u)
                if 1 <= u <= NU:
                    over_sum(u - 1)
                if u >= 5:
                    gated(u - 5)
    a2.free()
    end_stage()
    peek("mix", mix[:, :, :])
    peek("gate_b", gate_b[:, :, :])
    if last < 3:
        return

    hres = sb("hres", [P, TT, D])
    kv_keep = sb("kv_keep", [P, 2 * CROSS_H * MEM])
    kc = kv_keep[:, 0:CROSS_H * MEM].rearrange("p (n s) -> p n s", n=CROSS_H)
    vc = kv_keep[:, CROSS_H * MEM:].rearrange("p (t c) -> p t c", t=MEM // P)
    w_big = sb("w_big", [P, KD * D])
    w_o1 = w_big[:, :].rearrange("p (k c) -> p k c", k=KD)
    w_pq = w_big[:, :].rearrange("p (i k c) -> p i k c", i=2, k=KD)
    a3 = Arena()
    tok_s = a3("tok_s", [P, 2, 5, SEQ])
    for_kv = a3("for_kv", [P, 2 * CROSS_W * KD])
    w_kv = for_kv[:, :].rearrange("p (d c) -> p d c", d=KD)
    mats_s = for_kv[:, 0:8 * SEQ].rearrange("p (k n h q a t) -> p k n h q a t", k=2, n=2, h=2, q=4, a=2)
    y_in = for_kv[:, 8 * SEQ:12 * SEQ].rearrange("p (k n s) -> p k n s", k=2, n=2)
    rho_s = a3("rho_s", [P, 2, SEQ])
    vb_s = a3("vb_s", [P, 2, 2, NCH, 2, CH])
    ta_s = a3("ta_s", [P, 2, 2, 4, CH])
    w1_s = a3("w1_s", [P, 2, 2, 4, CH])
    w1_b = a3("w1_b", [P, 2, 2, 4, 2, CH])
    diag = a3("diag", [P, 2, NCH, CH])
    two_id = a3("two_id", [P, CH])
    ti_s = kv_keep[:, :].rearrange("p (k h q a t) -> p k h q a t", k=2, h=2, q=4, a=2)
    phi = w_big[:, 0:KD * SEQ].rearrange("p (m c t) -> p m c t", m=KD, t=CH)
    psi = w_big[:, KD * SEQ:].rearrange("p (m c t) -> p m c t", m=KD, t=CH)
    rhop = hres[:, :, :].rearrange("p a (b c t) -> p (a b) c t", b=2, t=CH)
    o_all = xnT[:, :, :].rearrange("p m (c t) -> p m c t", t=CH)
    state = rho_s[:, :, :].rearrange("p i (m t) -> p i m t", t=CH)

    in_s = [sem("chunk_in0"), sem("chunk_in1")]
    IN_ALL = 16 * 8
    y_loaded = [sem("y_loaded0"), sem("y_loaded1")]
    (y_full, y_ready, tw_full, tw_act, tw_dve, vb_ready, zeroed, xz_full, x_used, z_used, id_ready, diag_ready, state_ready, st_full,
     os_full, o_ready) = (sem(n) for n in (
         "y_full", "y_ready", "tw_full", "tw_act", "tw_dve", "vb_ready", "zeroed", "xz_full", "x_used", "z_used", "id_ready",
         "diag_ready", "state_ready", "st_full", "os_full", "o_ready"))

    vb_flat = vb_s[:, :, :, :, :, :].rearrange("p k n u a t -> p (k n u a t)")
    mem_s, mem_n = (vb_flat[:, i * 2 * D:(i + 1) * 2 * D].rearrange("p (t d) -> p t d", d=D) for i in range(2))
    memT = w1_b[:, :, :, :, :, :].rearrange("p k h q a t -> p (k h q a t)").rearrange("p (d s) -> p d s", s=MEM)
    mem_in, kv_in = sem("mem_in"), sem("kv_in")

    def halves(c):
        return slice(64 * (c % 2), 64 * (c % 2) + 64)

    def one(t, m):
        return t[:, bass.ds(m, 1)] if not isinstance(m, int) else t[:, m:m + 1]

    with nc.Block() as block:
        @block.sync
        def _(sp):
            def y_loads(m, k):
                sp.dma_start(y_in[:, k, 0, :].rearrange("p (n t) -> p n t", t=CH),
                             mats_dram[bass.ds(m, 1)].rearrange("a p (n j t) -> (a p) n j t", j=4, t=CH)[:, :, 2, :]).then_inc(y_loaded[k], 16)
                sp.dma_start(y_in[:, k, 1, :], tok_dram[bass.ds(m, 1)].rearrange("a p s -> (a p) s")[:, SEQ:2 * SEQ]).then_inc(y_loaded[k], 16)

            def loads(m, k):
                sp.wait_ge(xz_full, m * 2 + 2)
                sp.sem_inc(gone_on, 1)
                sp.wait_ge(x_used, m + 1)
                sp.sem_inc(gone_on, 1)
                sp.dma_start(tok_s[:, k, 0:4, :].rearrange("p a s -> p (a s)"),
                             tok_dram[bass.ds(m, 1)].rearrange("a p s -> (a p) s")).then_inc(in_s[k], 16)
                sp.wait_ge(zeroed, 4)
                sp.sem_inc(gone_on, 1)
                for par in range(2):
                    rows = slice(par * CH, (par + 1) * CH)
                    sp.dma_start(ti_s[rows, k, :, :, par, :].rearrange("p h c t -> p (h c) t"),
                                 inv_dram[bass.ds(m * 2, 2), :, par].rearrange("h c s t -> s (h c) t")).then_inc(in_s[k], 16)
                    for n, kind in enumerate((1, 3)):
                        sp.dma_start(mats_s[rows, k, n, :, :, par, :].rearrange("p h c t -> p (h c) t"),
                                     mats_dram[bass.ds(m, 1), rows].rearrange("a p (u j t) -> (a p) u j t", j=4, t=CH)[:, :, kind, :])\
                            .then_inc(in_s[k], 16)
                sp.dma_start(rho_s[:, k, :], rho_dram[bass.ds(m, 1)].rearrange("a p s -> (a p) s")).then_inc(in_s[k], 16)

            y_loads(0, 0)
            with sp.Fori(0, KD // 2 - 1) as i:
                for k in range(2):
                    m = i * 2 + k
                    sp.wait_ge(y_full, m + 1)
                    sp.sem_inc(gone_on, 1)
                    y_loads(m + 1, 1 - k)
                    loads(m, k)
            sp.wait_ge(y_full, KD - 1)
            y_loads(KD - 1, 1)
            loads(KD - 2, 0)
            loads(KD - 1, 1)
            sp.wait_ge(xz_full, 2 * KD + 4)
            sp.dma_start(mem_s, mem.rearrange("b (t p) d -> p (b t) d", p=P)).then_inc(mem_in, 16)
            sp.dma_start(w_kv, w_kv_cross[0].rearrange("(k p) c -> p k c", p=P)).then_inc(kv_in, 16)

        @block.gpsimd
        def _(pool):
            nc.gpsimd.memset(kv_keep[:, :], 0.0).then_inc(zeroed, 1)
            nc.gpsimd.memset(w1_b[:, :], 0.0).then_inc(zeroed, 1)
            nc.gpsimd.memset(vb_s[:, :, :, :, :, :], 0.0).then_inc(vb_ready, 1)
            pool.wait_ge(vb_ready, 1)
            with pool.Fori(0, KD // 2) as i:
                for k in range(2):
                    pool.wait_ge(in_s[k], i * IN_ALL + IN_ALL)
                    pool.sem_inc(gone_on, 1)
                    for n, kind in enumerate((1, 3)):
                        for par in range(2):
                            rows = slice(par * CH, (par + 1) * CH)
                            ins = nc.gpsimd.tensor_copy(vb_s[rows, k, n, :, par, :], tok_s[rows, k, kind, :].rearrange("p (u t) -> p u t", t=CH))
                    ins.then_inc(vb_ready, 1)

        @block.tensor
        def _(pe):
            pe.sem_inc(xz_full, 4)
            pe.sem_inc(y_full, 1)

            def y_part(m, i, k):
                pe.wait_ge(y_loaded[k], i * 32 + 32)
                pe.wait_ge(y_ready, m + 1)
                pe.sem_inc(gone_on, 1)
                for c in range(NCH):
                    cb = halves(c)
                    for h in range(2):
                        ch = slice(c // 2 * P + h * 64, c // 2 * P + h * 64 + 64)
                        at = (h * 4 + c // 2) * CH
                        mm = nc.tensor.matmul(bank[0][cb, ch], y_in[cb, k, 0, at:at + CH], y_in[cb, k, 1, ch], start=True, stop=True)
                mm.then_inc(y_full, 1)

            def solve_part(m, i, k):
                pe.wait_ge(in_s[k], i * IN_ALL + IN_ALL)
                pe.wait_ge(y_ready, m + 2)
                pe.wait_ge(tw_act, m + 1)
                pe.wait_ge(tw_dve, m + 1)
                pe.sem_inc(gone_on, 1)
                for h in range(2):
                    for q in range(4):
                        mm = nc.tensor.matmul(bank[1 + h][:, q * P:(q + 1) * P], ti_s[:, k, h, q, :, :].rearrange("p a t -> p (a t)"),
                                              tok_s[:, k, 0:5:4, q * P + h * 64:q * P + h * 64 + 64], start=True, stop=True)
                mm.then_inc(tw_full, 1)

            def xz_part(m, k):
                pe.wait_ge(tw_act, m + 2)
                pe.wait_ge(tw_dve, m + 2)
                pe.wait_ge(vb_ready, m + 2)
                pe.wait_ge(x_used, m + 2)
                pe.sem_inc(gone_on, 1)

                def blocks(t):
                    return t.rearrange("p a t -> p (a t)")

                for q in range(4):
                    to = slice(q * P, (q + 1) * P)
                    for h in range(2):
                        hb = slice(64 * h, 64 * h + 64)
                        nc.tensor.matmul(bank[3][hb, to], ta_s[:, k, h, q, :], blocks(mats_s[:, k, 0, h, q]), start=True, stop=True)
                        mm = nc.tensor.matmul(bank[4][hb, to], ta_s[:, k, h, q, :], blocks(vb_s[:, k, 1, 2 * q + h]), start=True, stop=True)
                mm.then_inc(xz_full, 1)
                pe.wait_ge(z_used, m + 1)
                pe.sem_inc(gone_on, 1)
                for q in range(4):
                    to = slice(q * P, (q + 1) * P)
                    for h in range(2):
                        hb = slice(64 * h, 64 * h + 64)
                        ch = slice(q * P + h * 64, q * P + h * 64 + 64)
                        nc.tensor.matmul(bank[6][hb, to], tok_s[:, k, 1, ch], blocks(mats_s[:, k, 1, h, q]), start=True, stop=False)
                        nc.tensor.matmul(bank[6][hb, to], w1_s[:, k, h, q, :], blocks(mats_s[:, k, 0, h, q]), start=False, stop=True)
                        nc.tensor.matmul(bank[5][hb, to], tok_s[:, k, 2, ch], blocks(vb_s[:, k, 0, 2 * q + h]), start=True, stop=False)
                        mm = nc.tensor.matmul(bank[5][hb, to], tok_s[:, k, 3, ch], blocks(w1_b[:, k, h, q]), start=False, stop=True)
                mm.then_inc(xz_full, 1)

            y_part(0, 0, 0)
            with pe.Fori(0, KD // 2 - 1) as i:
                solve_part(i * 2, i, 0)
                y_part(i * 2 + 1, i, 1)
                xz_part(i * 2, 0)
                solve_part(i * 2 + 1, i, 1)
                y_part(i * 2 + 2, i + 1, 0)
                xz_part(i * 2 + 1, 1)
            solve_part(KD - 2, KD // 2 - 1, 0)
            y_part(KD - 1, KD // 2 - 1, 1)
            xz_part(KD - 2, 0)
            solve_part(KD - 1, KD // 2 - 1, 1)
            xz_part(KD - 1, 1)

            for c in range(NCH):
                if c > 0:
                    pe.wait_ge(state_ready, c)
                    if c < NCH - 1:
                        for m in range(KD):
                            for h in range(2):
                                hb = slice(64 * h, 64 * h + 64)
                                mm = nc.tensor.matmul(bank[0][hb, m * CH:(m + 1) * CH], phi[hb, m, c, :],
                                                      state[hb, c % 2, m, :], start=True, stop=True)
                        mm.then_inc(st_full, 1)
                    if c > 2:
                        pe.wait_ge(o_ready, c - 2)
                    if c == 1:
                        pe.wait_ge(x_used, KD + 2)
                        pe.wait_ge(z_used, KD + 1)
                    for m in range(KD):
                        for h in range(2):
                            hb = slice(64 * h, 64 * h + 64)
                            mm = nc.tensor.matmul(bank[1 + c % 2][hb, m * CH:(m + 1) * CH], state[hb, c % 2, m, :],
                                                  rhop[hb, m, c, :], start=True, stop=True)
                    mm.then_inc(os_full, 1)

        @block.scalar
        def _(act):
            act.sem_inc(y_ready, 1)
            act.sem_inc(tw_act, 1)
            act.sem_inc(z_used, 1)
            act.wait_ge(zeroed, 4)
            with act.Fori(0, KD // 2) as i:
                for k in range(2):
                    m = i * 2 + k
                    act.wait_ge(y_full, m + 2)
                    nc.scalar.activation(tok_s[:, k, 4, :], bank[0][:, :], ACT.Copy).then_inc(y_ready, 1)
                    act.wait_ge(tw_full, m + 1)
                    act.wait_ge(xz_full, m * 2 + 2)
                    solved = bank[1][:, :].rearrange("p (q n t) -> p q n t", n=2, t=CH)
                    nc.scalar.activation(ta_s[:, k, 0], solved[:, :, 0], ACT.Copy)
                    nc.scalar.activation(w1_s[:, k, 0], solved[:, :, 1], ACT.Copy)
                    for par in range(2):
                        rows = slice(par * CH, (par + 1) * CH)
                        ins = nc.scalar.activation(w1_b[rows, k, 0, :, par, :], solved[rows, :, 1], ACT.Copy)
                    ins.then_inc(tw_act, 1)
                    act.wait_ge(xz_full, m * 2 + 6)
                    for b, dst in ((5, psi), (6, o_all)):
                        ins = nc.scalar.activation(one(dst, m).rearrange("p m c t -> p (m c t)"), bank[b][:, :], ACT.Copy)
                    ins.then_inc(z_used, 1)

        @block.vector
        def _(dve):
            dve.sem_inc(tw_dve, 1)
            dve.sem_inc(x_used, 2)
            for t in (mats_s[:, 0], mats_s[:, 1]):
                nc.vector.memset(t, 0.0).then_inc(zeroed, 1)
            nc.vector.tensor_tensor(two_id[:, :], ident[:, 0:CH], ident[:, CH:2 * CH], ALU.add).then_inc(id_ready, 1)
            dve.wait_ge(id_ready, 1)
            dve.wait_ge(zeroed, 4)
            with dve.Fori(0, KD // 2) as i:
                for k in range(2):
                    m = i * 2 + k
                    nc.vector.tensor_tensor(diag[:, k, :, :], two_id[:, :].rearrange("p (a t) -> p a t", a=1).broadcast_to([P, NCH, CH]),
                                            one(decay_end, m).rearrange("p a (c t) -> p (a c) t", t=1).broadcast_to([P, NCH, CH]),
                                            ALU.mult).then_inc(diag_ready, 1)
                    dve.wait_ge(diag_ready, m + 1)
                    dve.wait_ge(tw_full, m + 1)
                    dve.wait_ge(xz_full, m * 2 + 2)
                    solved = bank[2][:, :].rearrange("p (q n t) -> p q n t", n=2, t=CH)
                    nc.vector.tensor_copy(ta_s[:, k, 1], solved[:, :, 0])
                    nc.vector.tensor_copy(w1_s[:, k, 1], solved[:, :, 1])
                    for par in range(2):
                        rows = slice(par * CH, (par + 1) * CH)
                        ins = nc.vector.tensor_copy(w1_b[rows, k, 1, :, par, :], solved[rows, :, 1])
                    ins.then_inc(tw_dve, 1)
                    dve.wait_ge(xz_full, m * 2 + 5)
                    nc.vector.tensor_tensor(one(rhop, m).rearrange("p m c t -> p (m c t)"), bank[3][:, :], rho_s[:, k, :], ALU.add)
                    nc.vector.tensor_tensor(one(phi, m).rearrange("p m c t -> p (m c t)"), bank[4][:, :],
                                            diag[:, k, :, :].rearrange("p c t -> p (c t)"), ALU.add).then_inc(x_used, 1)

            dve.wait_ge(x_used, KD + 2)
            dve.wait_ge(z_used, KD + 1)
            nc.vector.tensor_copy(state[:, 1, :, :], psi[:, :, 0, :]).then_inc(state_ready, 1)
            for c in range(1, NCH):
                if c < NCH - 1:
                    dve.wait_ge(st_full, c)
                    if c > 1:
                        dve.wait_ge(os_full, c - 1)
                    nc.vector.tensor_tensor(state[:, (c + 1) % 2, :, :], bank[0][:, :].rearrange("p (m t) -> p m t", t=CH),
                                            psi[:, :, c, :], ALU.add).then_inc(state_ready, 1)
                dve.wait_ge(os_full, c)
                nc.vector.tensor_tensor(o_all[:, :, c, :], bank[1 + c % 2][:, :].rearrange("p (m t) -> p m t", t=CH),
                                        o_all[:, :, c, :], ALU.add).then_inc(o_ready, 1)

    (g2_in, gn_mean, gn_cen, gn_sq, gn_var, gn_std, gn_g, gn_used, gn_chain, gn_on, gn_done) = (sem(n) for n in (
        "g2_in", "gn_mean", "gn_cen", "gn_sq", "gn_var", "gn_std", "gn_g", "gn_used", "gn_chain", "gn_on", "gn_done"))
    g2_s = tok_s[:, 1, 0:2, :].rearrange("p a s -> p (a s)")
    mem_sq, mem_ms, mem_rt, mem_rs = (small[:, 8 * i:8 * i + MEM // P] for i in range(4))
    m_squared, m_scaled, m_rooted, m_normed, m_turned, m_evac, kv_full, kv_evac, hres_in, wo1_in, gn_mixed, gn_pool = (
        sem(n) for n in ("m_squared", "m_scaled", "m_rooted", "m_normed", "m_turned", "m_evac", "kv_full", "kv_evac",
                         "hres_in", "wo1_in", "gn_mixed", "gn_pool"))
    bonus_in = [sem("bonus_in0"), sem("bonus_in1")]
    cen, bns = rho_s, tok_s[:, 0, 0:2, :]
    sq = diag[:, :, :, :].rearrange("p i c t -> p i (c t)")
    std, on = (t[:, :, :, :, :].rearrange("p i h q t -> p i (h q t)") for t in (ta_s, w1_s))
    eps_gn = a3("eps_gn", [P, 1])
    with nc.Block() as block:
        @block.sync
        def _(sp):
            sp.dma_start(g2_s[:, :], rwkv_g2[0]).then_inc(g2_in, 16)
            for m in range(KD):
                if m >= 2:
                    sp.wait_ge(gn_done, m - 1)
                sp.dma_start(bns[:, m % 2, :], bonus_dram[m]).then_inc(bonus_in[m % 2], 16)
                sp.dma_start(w_o1[:, m, :], w_out[0, m * P:(m + 1) * P, :]).then_inc(wo1_in, 16)
                if m < TT:
                    sp.dma_start(hres[:, m, :], x_tok[:, m, :]).then_inc(hres_in, 16)
            sp.wait_ge(wo1_in, 16 * KD)
            sp.wait_ge(hres_in, 16 * TT)

        @block.tensor
        def _(pe):
            def mean(m):
                if m >= 2:
                    pe.wait_ge(gn_cen, m - 1)
                nc.tensor.matmul(bank[m % 2][:, :], bones, o_all[:, m].rearrange("p c t -> p (c t)"), start=True, stop=True).then_inc(gn_mean, 1)
            mean(0)
            pe.wait_ge(g2_in, 16)
            for m in range(KD):
                if m + 1 < KD:
                    mean(m + 1)
                if m >= 2:
                    pe.wait_ge(gn_used, m - 1)
                nc.tensor.matmul(bank[4 + m % 2][:, :], g2_s[:, m * P:(m + 1) * P], sdg[:, :], start=True, stop=True).then_inc(gn_g, 1)
                pe.wait_ge(gn_sq, m + 1)
                if m >= 2:
                    pe.wait_ge(gn_std, m - 1)
                nc.tensor.matmul(bank[2 + m % 2][:, :], bones, sq[:, m % 2, :], start=True, stop=True).then_inc(gn_var, 1)
                if m in (2, 3):
                    for d in range(4 * (m - 2), 4 * (m - 1)):
                        pe.wait_ge(m_normed, MEM // P)
                        if d >= 2:
                            pe.wait_ge(m_evac, d - 1)
                        for t in range(MEM // P):
                            mm = nc.tensor.transpose(bank[6 + d % 2][:, t * P:(t + 1) * P], mem_n[:, t, d * P:(d + 1) * P], ident)
                        mm.then_inc(m_turned, 1)
                for n in {4: (0,), 5: (1,), 6: (2,), 7: (3, 4, 5)}.get(m, ()):
                    pe.wait_ge(kv_in, 16)
                    pe.wait_ge(m_evac, KD)
                    if n >= 2:
                        pe.wait_ge(kv_evac, n - 1)
                    for d in range(KD):
                        st = dict(start=(d == 0), stop=(d == KD - 1))
                        if n < CROSS_H:
                            mm = nc.tensor.matmul(bank[6 + n % 2][:, 0:MEM], w_kv[:, d, n * P:(n + 1) * P], memT[:, d, :], **st)
                        else:
                            t = n - CROSS_H
                            mm = nc.tensor.matmul(bank[6 + n % 2][:, :], memT[:, d, t * P:(t + 1) * P], w_kv[:, d, CROSS_W:], **st)
                    mm.then_inc(kv_full, 1)

        @block.scalar
        def _(act):
            act.wait_ge(mem_in, 16)
            for t in range(MEM // P):
                nc.scalar.activation(mem_n[:, t], mem_s[:, t], ACT.Square, accum_out=mem_sq[:, t:t + 1]).then_inc(m_squared, 1)
            for m in range(KD):
                i = m % 2
                act.wait_ge(gn_cen, m + 1)
                if m >= 2:
                    act.wait_ge(gn_var, m - 1)
                nc.scalar.activation(sq[:, i, :], cen[:, i, :], ACT.Square).then_inc(gn_sq, 1)
                act.wait_ge(gn_var, m + 1)
                if m >= 2:
                    act.wait_ge(gn_on, m - 1)
                nc.scalar.activation(std[:, i, :], bank[2 + i][:, :], ACT.Sqrt, scale=1.0 / HEAD, bias=eps_gn[:, :]).then_inc(gn_std, 1)
                if m == 0:
                    act.wait_ge(m_scaled, 1)
                    nc.scalar.activation(mem_rt, mem_ms, ACT.Sqrt).then_inc(m_rooted, 1)
                if m == 1:
                    act.wait_ge(m_scaled, 2)
                    for t in range(MEM // P):
                        nc.scalar.activation(mem_n[:, t], mem_s[:, t], ACT.Copy, scale=mem_rs[:, t:t + 1]).then_inc(m_normed, 1)
                if m in (2, 3):
                    for d in range(4 * (m - 2), 4 * (m - 1)):
                        act.wait_ge(m_turned, d + 1)
                        nc.scalar.activation(memT[:, d, :], bank[6 + d % 2][:, 0:MEM], ACT.Copy, scale=col(R_GMEM, d)).then_inc(m_evac, 1)
                for n in {4: (0,), 5: (1,), 6: (2,), 7: (3, 4, 5)}.get(m, ()):
                    act.wait_ge(kv_full, n + 1)
                    if n < CROSS_H:
                        ins = nc.scalar.activation(kc[:, n, :], bank[6 + n % 2][:, 0:MEM], ACT.Copy)
                    else:
                        ins = nc.scalar.activation(vc[:, n - CROSS_H, :], bank[6 + n % 2][:, :], ACT.Copy)
                    ins.then_inc(kv_evac, 1)

        @block.vector
        def _(dve):
            n = [0]

            def link(ins):
                n[0] += 1
                ins.then_inc(gn_chain, 1)
                dve.wait_ge(gn_chain, n[0])

            link(nc.vector.memset(eps_gn[:, :], GN_EPS))

            def centre(m):
                i = m % 2
                dve.wait_ge(gn_mean, m + 1)
                if m >= 2:
                    dve.wait_ge(gn_sq, m - 1)
                nc.vector.scalar_tensor_tensor(out=cen[:, i, :], in0=bank[i][:, :], scalar=-1.0 / HEAD,
                                               in1=o_all[:, m].rearrange("p c t -> p (c t)"), op0=ALU.mult, op1=ALU.add).then_inc(gn_cen, 1)
                dve.wait_ge(gn_cen, m + 1)
            centre(0)
            dve.wait_ge(m_squared, MEM // P)
            nc.vector.tensor_scalar(mem_ms, mem_sq, 1.0 / D, EPS, ALU.mult, ALU.add).then_inc(m_scaled, 1)
            for m in range(KD):
                i = m % 2
                if m + 1 < KD:
                    centre(m + 1)
                dve.wait_ge(gn_std, m + 1)
                link(nc.vector.reciprocal(std[:, i, :], std[:, i, :]))
                if m >= 2:
                    dve.wait_ge(gn_mixed, m - 1)
                link(nc.vector.tensor_tensor(on[:, i, :], cen[:, i, :], std[:, i, :], ALU.mult))
                dve.sem_inc(gn_on, 1)
                dve.wait_ge(bonus_in[i], 16 * (m // 2 + 1))
                link(nc.vector.scalar_tensor_tensor(out=on[:, i, :], in0=on[:, i, :], scalar=col(R_LNW, m), in1=bns[:, i, :],
                                                    op0=ALU.mult, op1=ALU.add))
                dve.sem_inc(gn_done, 1)
                dve.wait_ge(gn_g, m + 1)
                nc.vector.scalar_tensor_tensor(out=on[:, i, :], in0=on[:, i, :], scalar=col(R_LNB, m), in1=bank[4 + i][:, :],
                                               op0=ALU.add, op1=ALU.mult).then_inc(gn_used, 1)
                if m == 0:
                    dve.wait_ge(m_rooted, 1)
                    nc.vector.reciprocal(mem_rs, mem_rt).then_inc(m_scaled, 1)

        @block.gpsimd
        def _(pool):
            for m in range(KD):
                pool.wait_ge(gn_used, m + 1)
                nc.gpsimd.tensor_tensor(on[:, m % 2, :], on[:, m % 2, :], gate_b[:, m], ALU.mult).then_inc(gn_pool, 1)
                pool.wait_ge(gn_pool, m + 1)
                nc.gpsimd.tensor_tensor(mix[:, m], mix[:, m], on[:, m % 2, :], ALU.add).then_inc(gn_mixed, 1)
    a3.free()
    end_stage()
    peek("mixed", mix[:, :, :])
    if last < 4:
        return

    a5 = Arena()
    xn5 = a5("xn5", [P, TT, D])
    w_qc = a5("w_qc", [P, KD, CROSS_W])
    w_oc = a5("w_oc", [P, CROSS_H, D])
    cpr = a5("cpr", [P, 2, 2, MEM])
    cprT = a5("cprT", [P, 2, 512])
    cmx, csum, crec = (a5(n, [P, 2, 2]) for n in ("cmx", "csum", "crec"))
    qc = gate_b[:, 0:CROSS_H, :]
    oc = gate_b[:, CROSS_H:2 * CROSS_H, :]
    wpq_first = [sem("wpq_first0"), sem("wpq_first1")]
    (wqc_in, woc_in, op_full, h_ready, qc_full, qc_evac, cs_full, cmx_ready, cp_ready, cpn_ready, ct_full,
     ct_evac, co_full, co_evac, c_chain, oo_full) = (sem(n) for n in (
         "wqc_in", "woc_in", "op_full", "h_ready", "qc_full", "qc_evac", "cs_full", "cmx_ready", "cp_ready",
         "cpn_ready", "ct_full", "ct_evac", "co_full", "co_evac", "c_chain", "oo_full"))
    SC = P ** -0.5
    cunits = [(t, hp) for t in range(TT) for hp in range(2)]
    NC_ = len(cunits)
    with nc.Block() as block:
        @block.sync
        def _(sp):
            sp.dma_start(w_qc[:, :, :], w_q_cross[0].rearrange("(k p) c -> p k c", p=P)).then_inc(wqc_in, 16)
            sp.dma_start(w_oc[:, :, :], w_o_cross[0].rearrange("(k p) c -> p k c", p=P)).then_inc(woc_in, 16)
            sp.wait_ge(op_full, 2 * TT)
            for b in range(2):
                sp.dma_start(w_pq[:, b], peer_w_q[0].rearrange("(k p) c -> p k c", p=P)[:, :, b * 512:(b + 1) * 512]).then_inc(wpq_first[b], 16)

        @block.tensor
        def _(pe):
            for n in range(2 * TT):
                if n >= 2:
                    pe.wait_ge(h_ready, n - 1)
                t, f = n // 2, n % 2
                for d in range(KD):
                    mm = nc.tensor.matmul(bank[2 + n % 2][:, :], mix[:, d, t * P:(t + 1) * P], w_o1[:, d, f * 512:(f + 1) * 512],
                                          start=(d == 0), stop=(d == KD - 1))
                mm.then_inc(op_full, 1)

        @block.vector
        def _(dve):
            for n in range(2 * TT):
                dve.wait_ge(op_full, n + 1)
                v = hres[:, n // 2, n % 2 * 512:n % 2 * 512 + 512]
                nc.vector.tensor_tensor(v, bank[2 + n % 2][:, :], v, ALU.add).then_inc(h_ready, 1)
        xc_ready, xc_at = norm_transpose(block, "nc", hres, TT, R_GCROSS, xn5, xnT, h_ready, 2 * TT, bank[0:2])

        @block.tensor
        def _(pe):
            pe.wait_ge(wqc_in, 16)
            pe.wait_ge(xc_ready, xc_at)
            for n in range(CROSS_H):
                if n >= 2:
                    pe.wait_ge(qc_evac, n - 1)
                for d in range(KD):
                    mm = nc.tensor.matmul(bank[4 + n % 2][:, :], w_qc[:, d, n * P:(n + 1) * P], xnT[:, d, :],
                                          start=(d == 0), stop=(d == KD - 1))
                mm.then_inc(qc_full, 1)

            def scores(u):
                t, hp = cunits[u]
                if u >= 2:
                    pe.wait_ge(cp_ready, u - 1)
                for h in range(2):
                    mm = nc.tensor.matmul(bank[u % 2][:, h * MEM:(h + 1) * MEM], qc[:, 2 * hp + h, t * P:(t + 1) * P],
                                          kc[:, 2 * hp + h, :], start=True, stop=True)
                mm.then_inc(cs_full, 1)

            def turn(u):
                pe.wait_ge(cpn_ready, u + 1)
                if u >= 2:
                    pe.wait_ge(ct_evac, u - 1)
                for h in range(2):
                    for s in range(2):
                        mm = nc.tensor.transpose(bank[2 + u % 2][:, (2 * h + s) * P:(2 * h + s + 1) * P],
                                                 cpr[:, u % 2, h, s * P:(s + 1) * P], ident)
                mm.then_inc(ct_full, 1)

            def weigh(u):
                t, hp = cunits[u]
                pe.wait_ge(ct_evac, u + 1)
                if u >= 2:
                    pe.wait_ge(co_evac, u - 1)
                for h in range(2):
                    for s in range(2):
                        mm = nc.tensor.matmul(bank[4 + u % 2][:, h * P:(h + 1) * P], vc[:, s, (2 * hp + h) * P:(2 * hp + h + 1) * P],
                                              cprT[:, u % 2, (2 * h + s) * P:(2 * h + s + 1) * P], start=(s == 0), stop=(s == 1))
                mm.then_inc(co_full, 1)

            pe.wait_ge(qc_evac, CROSS_H)
            for u in range(NC_ + 2):
                if u < NC_:
                    scores(u)
                if 1 <= u <= NC_:
                    turn(u - 1)
                if u >= 2:
                    weigh(u - 2)
            pe.wait_ge(woc_in, 16)
            pe.wait_ge(co_evac, NC_)
            for b in range(2):
                pe.wait_ge(wpq_first[b], 16)
            for n in range(2 * TT):
                if n >= 2:
                    pe.wait_ge(h_ready, 2 * TT + n - 1)
                t, f = n // 2, n % 2
                for d in range(CROSS_H):
                    mm = nc.tensor.matmul(bank[6 + n % 2][:, :], oc[:, d, t * P:(t + 1) * P], w_oc[:, d, f * 512:(f + 1) * 512],
                                          start=(d == 0), stop=(d == CROSS_H - 1))
                mm.then_inc(oo_full, 1)

        @block.scalar
        def _(act):
            for n in range(CROSS_H):
                act.wait_ge(qc_full, n + 1)
                nc.scalar.activation(qc[:, n, :], bank[4 + n % 2][:, :], ACT.Copy).then_inc(qc_evac, 1)

            def exps(u):
                act.wait_ge(cmx_ready, u + 1)
                for h in range(2):
                    ins = nc.scalar.activation(cpr[:, u % 2, h, :], bank[u % 2][:, h * MEM:(h + 1) * MEM], ACT.Exp, scale=SC,
                                               bias=cmx[:, u % 2, h:h + 1], accum_out=csum[:, u % 2, h:h + 1])
                ins.then_inc(cp_ready, 1)

            def evac(u):
                act.wait_ge(ct_full, u + 1)
                if u >= 2:
                    act.wait_ge(co_full, u - 1)
                nc.scalar.activation(cprT[:, u % 2, :], bank[2 + u % 2][:, :], ACT.Copy).then_inc(ct_evac, 1)

            for u in range(NC_ + 1):
                if u < NC_:
                    exps(u)
                if u >= 1:
                    evac(u - 1)

        @block.vector
        def _(dve):
            n_links = [0]

            def link(ins):
                n_links[0] += 1
                ins.then_inc(c_chain, 1)
                dve.wait_ge(c_chain, n_links[0])

            def maxes(u):
                dve.wait_ge(cs_full, u + 1)
                if u >= 2:
                    dve.wait_ge(cp_ready, u - 1)
                link(nc.vector.tensor_reduce(cmx[:, u % 2, :], bank[u % 2][:, :].rearrange("p (h m) -> p h m", h=2), AX, ALU.max))
                nc.vector.tensor_scalar(cmx[:, u % 2, :], cmx[:, u % 2, :], -SC, None, ALU.mult).then_inc(cmx_ready, 1)

            def normalise(u):
                dve.wait_ge(cp_ready, u + 1)
                link(nc.vector.reciprocal(crec[:, u % 2, :], csum[:, u % 2, :]))
                for h in range(2):
                    ins = nc.vector.tensor_scalar(cpr[:, u % 2, h, :], cpr[:, u % 2, h, :], crec[:, u % 2, h:h + 1], None, ALU.mult)
                ins.then_inc(cpn_ready, 1)

            def collect(u):
                t, hp = cunits[u]
                dve.wait_ge(co_full, u + 1)
                nc.vector.tensor_copy(oc[:, 2 * hp:2 * hp + 2, t * P:(t + 1) * P],
                                      bank[4 + u % 2][:, 0:256].rearrange("p (h q) -> p h q", h=2)).then_inc(co_evac, 1)

            for u in range(NC_ + 2):
                if u < NC_:
                    maxes(u)
                if 1 <= u <= NC_:
                    normalise(u - 1)
                if u >= 2:
                    collect(u - 2)
            for n in range(2 * TT):
                dve.wait_ge(oo_full, n + 1)
                v = hres[:, n // 2, n % 2 * 512:n % 2 * 512 + 512]
                nc.vector.tensor_tensor(v, bank[6 + n % 2][:, :], v, ALU.add).then_inc(h_ready, 1)
    a5.free()
    end_stage()
    peek("h2", hres[:, :, :])
    if last < 5:
        return

    xf = mix[:, :, :].rearrange("p k s -> p (k s)").rearrange("p (t d) -> p t d", d=D)
    HK = PH * TOPK
    expert = sb("expert", [P, TT * HK], U32)
    gate = sb("gate", [P, TT, HK])
    a6 = Arena()
    scores_s = a6("scores_s", [P, TT, 2 * PH, NKEYS])
    sc_in = a6("sc_in", [P, 2, NKEYS])
    rest = a6("rest", [P, 2, NKEYS])
    top = a6("top", [P, 2, TOPK])
    topi = a6("topi", [P, 2, TOPK], U32)
    topf = a6("topf", [P, 2, TOPK])
    cand = a6("cand", [P, TOPK * TOPK])
    cand2 = a6("cand2", [P, TOPK * TOPK])
    ctop = a6("ctop", [P, TOPK])
    ci = a6("ci", [P, TOPK], U32)
    cj = a6("cj", [P, 2, TOPK], U32)
    cf = a6("cf", [P, 2, TOPK])
    pick = a6("pick", [P, 2, TOPK, TOPK])
    pick2 = a6("pick2", [P, 2, TOPK, TOPK])
    ef = a6("ef", [P, 2, TOPK])
    en = a6("en", [P, TOPK])
    shifted, expd = a6("shifted", [P, TOPK]), a6("expd", [P, TOPK])
    gsum = a6("gsum", [P, 1])
    TOP_LINKS = 23

    def top_head(dve, t, h, before, chain, shift, exped):
        n_links = [0]

        def link(ins, apart=False):
            n_links[0] += 1
            ins.then_inc(chain, 1)
            dve.wait_ge(chain, before * TOP_LINKS + n_links[0])
            if apart:
                dve.sem_inc(gone_on, 1)

        def top16(src, spare, vals, idx):
            link(nc.vector.max(vals[:, 0:8], src), apart=True)
            nc.vector.max_index(idx[:, 0:8], vals[:, 0:8], src)
            link(nc.vector.match_replace(spare, vals[:, 0:8], src, -3.0e38), apart=True)
            link(nc.vector.max(vals[:, 8:16], spare), apart=True)
            link(nc.vector.max_index(idx[:, 8:16], vals[:, 8:16], spare), apart=True)

        link(nc.vector.tensor_copy(sc_in[:, :, :], scores_s[:, t, bass.ds(h * 2, 2), :]), apart=True)
        for s in range(2):
            top16(sc_in[:, s, :], rest[:, s, :], top[:, s, :], topi[:, s, :])
        link(nc.vector.tensor_tensor(cand[:, :].rearrange("p (a b) -> p a b", a=TOPK),
                                     top[:, 0, :].rearrange("p (a b) -> p a b", b=1).broadcast_to([P, TOPK, TOPK]),
                                     top[:, 1:2, :].broadcast_to([P, TOPK, TOPK]), ALU.add), apart=True)
        top16(cand[:, :], cand2[:, :], ctop[:, :], ci[:, :])
        nc.vector.tensor_scalar(shifted[:, :], ctop[:, :], ctop[:, 0:1], None, ALU.subtract).then_inc(shift, 1)
        nc.vector.tensor_copy(topf[:, :, :], topi[:, :, :])
        nc.vector.tensor_scalar(cj[:, 0, :], ci[:, :], 4, None, ALU.logical_shift_right)
        link(nc.vector.tensor_scalar(cj[:, 1, :], ci[:, :], 15, None, ALU.bitwise_and))
        link(nc.vector.tensor_copy(cf[:, :, :], cj[:, :, :]))
        places = cst[:, C_IOTA:C_IOTA + TOPK].rearrange("p (a j) -> p a j", a=1).broadcast_to([P, 2 * TOPK, TOPK])
        link(nc.vector.tensor_tensor(pick[:, :, :, :].rearrange("p s k j -> p (s k) j"),
                                     cf[:, :, :].rearrange("p s (k j) -> p (s k) j", j=1).broadcast_to([P, 2 * TOPK, TOPK]),
                                     places, ALU.is_equal))
        for s in range(2):
            ins = nc.vector.tensor_tensor(pick2[:, s, :, :], pick[:, s, :, :], topf[:, s:s + 1, :].broadcast_to([P, TOPK, TOPK]), ALU.mult)
        link(ins)
        link(nc.vector.tensor_reduce(ef[:, :, :], pick2[:, :, :, :], AX, ALU.add))
        link(nc.vector.scalar_tensor_tensor(out=en[:, :], in0=ef[:, 0, :], scalar=float(NKEYS), in1=ef[:, 1, :],
                                            op0=ALU.mult, op1=ALU.add))
        link(nc.vector.tensor_copy(expert[:, bass.ds(h * TOPK + t * HK, TOPK)], en[:, :]))
        dve.wait_ge(exped, before + 1)
        link(nc.vector.reciprocal(gsum[:, :], gsum[:, :]))
        link(nc.vector.tensor_scalar(gate[:, t, bass.ds(h * TOPK, TOPK)], expd[:, :], gsum[:, 0:1], None, ALU.mult))
        assert n_links[0] == TOP_LINKS, n_links

    def top_exp(act, before, shift, exped):
        act.wait_ge(shift, before + 1)
        nc.scalar.activation(expd[:, :], shifted[:, :], ACT.Exp, accum_out=gsum[:, 0:1]).then_inc(exped, 1)

    k_chain, k_shift, k_exp = (sem(n) for n in ("k_chain", "k_shift", "k_exp"))
    a7 = Arena()
    xn7 = a7("xn7", [P, TT, D])
    gf = a7("gf", [P, D])
    qp = a7("qp", [P, 2, SEQ])
    keys = a7("keys", [P, 2, P])
    keysT = a7("keysT", [P, 2, P])
    (gf_in, keys_in, keys_full, keys_ready, pq_full, pq_evac, ps_full, ps_evac, xf_ready) = (sem(n) for n in (
        "gf_in", "keys_in", "keys_full", "keys_ready", "pq_full", "pq_evac", "ps_full", "ps_evac", "xf_ready"))
    wpq_in = [sem("wpq_in0"), sem("wpq_in1")]
    with nc.Block() as block:
        @block.sync
        def _(sp):
            sp.dma_start(keys[:, 0, :], peer_sub_keys_1[0]).then_inc(keys_in, 16)
            sp.dma_start(keys[:, 1, :], peer_sub_keys_2[0]).then_inc(keys_in, 16)
            sp.dma_start(gf[:, :], g_ffn.partition_broadcast(P)).then_inc(gf_in, 16)
            for b in range(2, 4):
                sp.wait_ge(pq_full, 4 * (b - 1))
                sp.dma_start(w_pq[:, b % 2, :, :], peer_w_q[0].rearrange("(k p) c -> p k c", p=P)[:, :, b * 512:(b + 1) * 512]).then_inc(wpq_in[b % 2], 16)
        xp_ready, xp_at = norm_transpose(block, "np", hres, TT, R_GFFN, xn7, xnT, None, 0, bank[0:2])

        @block.vector
        def _(dve):
            dve.wait_ge(gf_in, 16)
            dve.wait_ge(xp_ready, xp_at)
            for t in range(TT):
                nc.vector.tensor_tensor(xf[:, t], xn7[:, t], gf[:, :], ALU.mult).then_inc(xf_ready, 1)
            with dve.Fori(0, PH) as h:
                dve.wait_ge(ps_evac, h * 2 + 2)
                top_head(dve, 0, h, h, k_chain, k_shift, k_exp)

        @block.tensor
        def _(pe):
            pe.wait_ge(keys_in, 32)
            for s in range(2):
                mm = nc.tensor.transpose(bank[2][:, s * P:(s + 1) * P], keys[:, s, :], ident)
            mm.then_inc(keys_full, 1)
            pe.wait_ge(xp_ready, xp_at)

            def score(n):
                pe.wait_ge(pq_evac, n + 1)
                if n >= 2:
                    pe.wait_ge(ps_evac, n - 1)
                for t in range(TT):
                    mm = nc.tensor.matmul(bank[4 + n % 2][:, t * P:(t + 1) * P], qp[:, n % 2, t * P:(t + 1) * P],
                                          keysT[:, n % 2, :], start=True, stop=True)
                mm.then_inc(ps_full, 1)

            pe.wait_ge(keys_ready, 1)
            for n in range(2 * PH):
                if n >= 8:
                    pe.wait_ge(wpq_in[n // 4 % 2], 16)
                if n >= 2:
                    pe.wait_ge(pq_evac, n - 1)
                for d in range(KD):
                    mm = nc.tensor.matmul(bank[2 + n % 2][:, :], w_pq[:, n // 4 % 2, d, n % 4 * P:(n % 4 + 1) * P], xnT[:, d, :],
                                          start=(d == 0), stop=(d == KD - 1))
                mm.then_inc(pq_full, 1)
                if n >= 1:
                    score(n - 1)
            score(2 * PH - 1)

        @block.scalar
        def _(act):
            act.wait_ge(keys_full, 1)
            nc.scalar.activation(keysT[:, :, :], bank[2][:, 0:2 * P].rearrange("p (s n) -> p s n", s=2), ACT.Copy).then_inc(keys_ready, 1)

            def evac_scores(n):
                act.wait_ge(ps_full, n + 1)
                nc.scalar.activation(scores_s[:, :, n, :], bank[4 + n % 2][:, :].rearrange("p (t n) -> p t n", t=TT), ACT.Copy).then_inc(ps_evac, 1)

            for n in range(2 * PH):
                act.wait_ge(pq_full, n + 1)
                if n >= 2:
                    act.wait_ge(ps_full, n - 1)
                nc.scalar.activation(qp[:, n % 2, :], bank[2 + n % 2][:, :], ACT.Copy).then_inc(pq_evac, 1)
                if n >= 1:
                    evac_scores(n - 1)
                if n >= 3 and n % 2 == 1:
                    top_exp(act, n // 2 - 1, k_shift, k_exp)
            evac_scores(2 * PH - 1)
            top_exp(act, PH - 1, k_shift, k_exp)
    a7.free()
    end_stage()

    G = 8
    a9 = Arena()
    stage_i = a9("stage_i", [P, 2, G], U32)
    u_rows = w_big[:, :].rearrange("p (j d) -> p j d", j=G)
    v_rows = a9("v_rows", [P, G, D])
    dots = a9("dots", [P, 2, G])
    gel = a9("gel", [P, 2, G])
    wgt = a9("wgt", [P, 2, G])
    wdiag = gate_b[:, 0:4, :].rearrange("p a s -> p (a s)").rearrange("p (k j q) -> p k j q", k=2, j=G)
    zeros = a9("zeros", [P, P])
    gfin = a9("gfin", [P, D])
    out_s = gate_b[:, 4:8, :].rearrange("p a s -> p (a s)").rearrange("p (k d) -> p k d", k=2)
    sq9 = xnT[:, 0:2, :].rearrange("p a s -> p (a s)")
    fs = a9("fs", [P, TT, 4])
    eps_col = a9("eps_col", [P, 1])
    u_in = [sem(f"u_in{j}") for j in range(G)]
    v_in = [sem(f"v_in{j}") for j in range(G)]
    (staged, dot_done, gel_done, w_done, diag_done, acc_done, fin_full, z_ready, gfin_in, f_sq, f_ms, f_rt, f_chain,
     f_out, v_used) = (sem(n) for n in (
         "staged", "dot_done", "gel_done", "w_done", "diag_done", "acc_done", "fin_full", "z_ready", "gfin_in", "f_sq",
         "f_ms", "f_rt", "f_chain", "f_out", "v_used"))
    top_link, top_shift, top_exped = (sem(n) for n in ("top_link", "top_shift", "top_exped"))
    out_stored = [sem("out_stored0"), sem("out_stored1")]
    NG = HK // G
    with nc.Block() as block:
        @block.sync
        def _(sp):
            sp.dma_start(gfin[:, :], g_final.rearrange("(a d) -> a d", a=1).partition_broadcast(P)).then_inc(gfin_in, 16)
            for t in range(TT):
                sp.wait_ge(f_out, t + 1)
                sp.dma_start(out[0, t * P:(t + 1) * P, :], out_s[:, t % 2, :]).then_inc(out_stored[t % 2], 16)
            for s in out_stored:
                sp.wait_ge(s, 16 * TT // 2)

        @block.gpsimd
        def _(pool):
            for t in range(TT):
                if t >= 1:
                    pool.wait_ge(top_link, t * PH * TOP_LINKS)
                with pool.Fori(0, NG // 2) as i:
                    for k in range(2):
                        g = i * 2 + (k + t * NG)
                        nc.gpsimd.tensor_copy(stage_i[:, k, :], expert[:, bass.ds(g * G, G)]).then_inc(staged, 1)
                        pool.wait_ge(staged, g + 1)
                        for rows_, table, done, used, ahead in ((u_rows, peer_u, u_in, dot_done, 1), (v_rows, peer_v, v_in, v_used, G + 1)):
                            for j in range(G):
                                pool.wait_ge(used, g * G + j + ahead)
                                pool.sem_inc(gone_on, 1)
                                pool.indirect_dma_start(rows_[:, j, :], None, table[0],
                                                        bass.IndirectOffsetOnAxis(ap=stage_i[:, k, j:j + 1], axis=0)).then_inc(done[j], 16)

        @block.vector
        def _(dve):
            dve.sem_inc(dot_done, G)
            nc.vector.memset(zeros[:, :], 0.0).then_inc(z_ready, 1)
            nc.vector.memset(eps_col[:, :], EPS).then_inc(z_ready, 1)
            dve.wait_ge(gfin_in, 16)

            def finish(t):
                dve.wait_ge(f_rt, t + 1)
                nc.vector.reciprocal(fs[:, t, 2:3], fs[:, t, 3:4]).then_inc(f_chain, 1)
                dve.wait_ge(f_chain, t + 1)
                if t >= 2:
                    dve.wait_ge(out_stored[t % 2], 16 * (t // 2))
                for f in range(2):
                    half = slice(f * 512, (f + 1) * 512)
                    ins = nc.vector.scalar_tensor_tensor(out=out_s[:, t % 2, half], in0=bank[2 * t + f][:, :], scalar=fs[:, t, 2:3],
                                                         in1=gfin[:, half], op0=ALU.mult, op1=ALU.mult)
                ins.then_inc(f_out, 1)

            for t in range(TT):
                with dve.Fori(0, NG // 2) as i:
                    if t + 1 < TT:
                        top_head(dve, t + 1, i, i + t * PH, top_link, top_shift, top_exped)
                    for k in range(2):
                        g = i * 2 + (k + t * NG)
                        for j in range(G):
                            dve.wait_ge(u_in[j], g * 16 + 16)
                            nc.vector.tensor_tensor_reduce(u_rows[:, j, :], u_rows[:, j, :], xf[:, t, :], 1.0, 0.0, ALU.mult,
                                                           ALU.add, dots[:, k, j:j + 1]).then_inc(dot_done, 1)
                        dve.wait_ge(gel_done, g + 1)
                        nc.vector.tensor_tensor(wgt[:, k, :], gel[:, k, :], gate[:, t, bass.ds(i * 2 * G + k * G, G)], ALU.mult).then_inc(w_done, 1)
                        dve.wait_ge(w_done, g + 1)
                        dve.wait_ge(v_used, g * G + G)
                        nc.vector.tensor_tensor(wdiag[:, k, :, :], ident.rearrange("p (a q) -> p a q", a=1).broadcast_to([P, G, P]),
                                                wgt[:, k, :].rearrange("p (j a) -> p j a", a=1).broadcast_to([P, G, P]), ALU.mult).then_inc(diag_done, 1)
                if t >= 1:
                    finish(t - 1)
            finish(TT - 1)

        @block.scalar
        def _(act):
            def gelu(g, k):
                act.wait_ge(dot_done, g * G + 2 * G)
                nc.scalar.activation(gel[:, k, :], dots[:, k, :], ACT.Gelu).then_inc(gel_done, 1)
            def finish(t):
                act.wait_ge(fin_full, t + 1)
                for f in range(2):
                    nc.scalar.activation(sq9[:, f * 512:(f + 1) * 512], bank[2 * t + f][:, :], ACT.Square,
                                         accum_out=fs[:, t, f:f + 1]).then_inc(f_sq, 1)
                act.wait_ge(f_sq, 2 * t + 2)
                nc.scalar.activation(fs[:, t, 2:3], fs[:, t, 0:1], ACT.Identity, bias=fs[:, t, 1:2]).then_inc(f_ms, 1)
                act.wait_ge(f_ms, t + 1)
                nc.scalar.activation(fs[:, t, 3:4], fs[:, t, 2:3], ACT.Sqrt, scale=1.0 / D, bias=eps_col[:, :]).then_inc(f_rt, 1)

            act.wait_ge(z_ready, 2)
            for t in range(TT):
                with act.Fori(0, NG // 2) as i:
                    if t + 1 < TT:
                        top_exp(act, i + t * PH, top_shift, top_exped)
                    for k in range(2):
                        gelu(i * 2 + (k + t * NG), k)
                if t >= 1:
                    finish(t - 1)
            finish(TT - 1)

        @block.tensor
        def _(pe):
            pe.sem_inc(v_used, 2 * G)
            pe.wait_ge(z_ready, 1)
            for t in range(TT):
                for f in range(2):
                    nc.tensor.matmul(bank[2 * t + f][:, :], ident, hres[:, t, f * 512:(f + 1) * 512], start=True, stop=False,
                                     skip_group_check=True)
                with pe.Fori(0, NG // 2) as i:
                    for k in range(2):
                        g = i * 2 + (k + t * NG)
                        pe.wait_ge(diag_done, g + 1)
                        for j in range(G):
                            pe.wait_ge(v_in[j], g * 16 + 16)
                            for f in range(2):
                                mm = nc.tensor.matmul(bank[2 * t + f][:, :], wdiag[:, k, j, :], v_rows[:, j, f * 512:(f + 1) * 512],
                                                      start=False, stop=False, skip_group_check=True)
                            mm.then_inc(v_used, 1)
                for f in range(2):
                    mm = nc.tensor.matmul(bank[2 * t + f][:, :], zeros[:, :], hres[:, t, f * 512:(f + 1) * 512], start=False, stop=True,
                                          skip_group_check=True)
                mm.then_inc(fin_full, 1)


NAMES = ["x", "mem", "positions", "g_mix", "w_in", "attn_sinks", "rwkv_mu", "rwkv_w0", "rwkv_w2", "rwkv_a0", "rwkv_a2",
         "rwkv_g2", "rwkv_k_k", "rwkv_k_a", "rwkv_r_k", "rwkv_ln_w", "rwkv_ln_b", "w_out", "g_cross", "g_mem",
         "w_q_cross", "w_kv_cross", "w_o_cross", "g_ffn", "peer_w_q", "peer_sub_keys_1", "peer_sub_keys_2", "peer_u",
         "peer_v", "g_final"]



def kernel(**inputs):
    import numpy as _np
    import concourse.bacc as _bacc
    from concourse import mybir as _mybir
    from concourse.bass_utils import run_bass_kernel_spmd as _run

    nc = _bacc.Bacc("TRN2", target_bir_lowering=False, num_devices=1)
    arrays, args = {}, []
    for name in NAMES:
        a = _np.ascontiguousarray(inputs[name])
        arrays[f"in_{name}"] = a
        args.append(nc.dram_tensor(f"in_{name}", a.shape, _mybir.dt.from_np(a.dtype), kind="ExternalInput").ap())
    c = constants()
    arrays["const"] = c
    args.append(nc.dram_tensor("const", c.shape, F32, kind="ExternalInput").ap())
    args.append(nc.dram_tensor("out", (1, SEQ, D), F32, kind="ExternalOutput").ap())
    build(nc, *args)
    r = _run(nc, [arrays], core_ids=[0])
    return r.results[0]["out"]
```

```python
from contextlib import ExitStack

import numpy as np

import concourse.bass as bass
from concourse import mybir

F32 = mybir.dt.float32
BF16 = mybir.dt.bfloat16
I32 = mybir.dt.int32
U32 = mybir.dt.uint32
ALU = mybir.AluOpType
ACT = mybir.ActivationFunctionType
AX = mybir.AxisListType.X

P = 128
D = 1024
SEQ = 512
TT = SEQ // P
KD = D // P
HEAD = 64
HEADS = 16
KV = 4
CH = 64
NCH = SEQ // CH
MEM = 256
CROSS_W = 512
CROSS_H = 4
PH = 8
TOPK = 16
NKEYS = 128
EPS = 1e-5
GN_EPS = 64e-5
SQE = float(np.exp(-0.5))
TWO_PI = 2.0 * np.pi
OFF_K = 1024
OFF_RWKV = 1536
OFF_LOW = OFF_RWKV + 3 * D
OFF_GATE = OFF_LOW + 256
IN_W = OFF_GATE + 2 * D
NEG = -1e30

C_ID, C_BONES, C_ROT, C_MASK, C_BAND, C_RESET, C_IOTA, C_INVF, C_END = 0, 128, 256, 384, 640, 896, 1408, 1664, 1672

R_MU, R_W0, R_A0, R_KK, R_KA, R_RK, R_LNW, R_LNB, R_GMIX, R_GCROSS, R_GFFN, R_GMEM, R_MULOW = (
    0, 24, 32, 40, 48, 56, 64, 72, 80, 88, 96, 104, 112)
R_END = 114


def constants():
    c = np.zeros((P, C_END), np.float32)
    p = np.arange(P)
    c[:, C_ID:C_ID + P] = np.eye(P)
    c[:, C_BONES:C_BONES + P] = (p[:, None] // HEAD == p[None, :] // HEAD)
    for m in range(P):
        d = m % HEAD
        if d < 8:
            c[m + 8, C_ROT + m] = -1.0
        elif d < 16:
            c[m - 8, C_ROT + m] = 1.0
    s, t = (p % CH)[:, None], np.arange(CH)[None, :]
    for n, m in enumerate([s < t, -1.0 * (s <= t), s < t, s <= t]):
        c[:, C_MASK + n * CH:C_MASK + (n + 1) * CH] = m
    j = np.arange(2 * P)[None, :]
    c[:, C_BAND:C_BAND + 2 * P] = np.where((j > p[:, None]) & (j <= p[:, None] + P), 0.0, NEG)
    c[:, C_RESET:C_RESET + SEQ] = (np.arange(SEQ) % CH != 0)
    c[:, C_IOTA:C_IOTA + 256] = np.arange(256)
    inv = (1.0 / (np.float32(500000.0) ** (np.arange(0, 16, 2, dtype=np.float32) / np.float32(16)))).astype(np.float32)
    d = p % HEAD
    c[:, C_INVF] = np.where(d < 16, inv[d % 8], 0.0)
    return c


def build(nc, x, mem, positions, g_mix, w_in, attn_sinks, rwkv_mu, rwkv_w0, rwkv_w2, rwkv_a0, rwkv_a2, rwkv_g2,
          rwkv_k_k, rwkv_k_a, rwkv_r_k, rwkv_ln_w, rwkv_ln_b, w_out, g_cross, g_mem, w_q_cross, w_kv_cross,
          w_o_cross, g_ffn, peer_w_q, peer_sub_keys_1, peer_sub_keys_2, peer_u, peer_v, g_final, const, out):
    stage_sems = []

    def sem(name):
        stage_sems.append(nc.alloc_semaphore(name))
        return stage_sems[-1]

    gone_on = nc.alloc_semaphore("gone_on")

    def end_stage():
        nc.clear_and_free_semaphores(list(stage_sems))
        stage_sems.clear()
        nc.all_engine_barrier()

    def sb(name, shape, dt=F32):
        return nc.alloc_sbuf_tensor(name, shape, dt)

    def dram(name, shape):
        return nc.dram_tensor(name, shape, F32, kind="Internal").ap()

    bank = [nc.alloc_psum_tensor(f"bank{i}", [P, 512], F32) for i in range(8)]

    tok_dram = dram("tok_dram", [KD, P, 4 * SEQ])
    mats_dram = dram("mats_dram", [KD, P, 2 * 4 * 4 * CH])
    rho_dram = dram("rho_dram", [KD, P, SEQ])
    bonus_dram = dram("bonus_dram", [KD, P, SEQ])
    low_dram = dram("low_dram", [HEADS, 4, 2, CH, CH])
    inv_dram = dram("inv_dram", [HEADS, 4, 2, CH, CH])

    cst = sb("cst", [P, C_END])
    prm = sb("prm", [P, P])
    xnT = sb("xnT", [P, KD, SEQ])
    sdg = sb("sdg", [P, SEQ])
    decay_end = sb("decay_end", [P, KD, NCH])
    ident = cst[:, C_ID:C_ID + P]
    bones = cst[:, C_BONES:C_BONES + P]

    def col(row, m):
        if isinstance(m, int):
            return prm[:, row + m:row + m + 1]
        return prm[:, bass.ds(m + row, 1)]

    class Arena:

        def __init__(self):
            self.stack = ExitStack()

        def __call__(self, name, shape, dt=F32):
            return self.stack.enter_context(nc.sbuf_tensor(name, shape, dt))

        def free(self):
            self.stack.close()

    def norm_transpose(block, tag, src, n, gain_row, xn, dstT, banks, src_ready=None, make_pe=None, make_dve=None, before_gain=None):
        ss, ms, rt, rs = (small[:, 8 * i:8 * i + n] for i in range(4))
        squared, scaled, rooted, normed, turned, evac = (sem(f"{tag}_{s}") for s in (
            "squared", "scaled", "rooted", "normed", "turned", "evac"))

        @block.scalar
        def _(act):
            for t in range(n):
                if src_ready is not None:
                    act.wait_ge(*src_ready(t))
                nc.scalar.activation(xn[:, t], src[:, t], ACT.Square, accum_out=ss[:, t:t + 1]).then_inc(squared, 1)
                act.wait_ge(scaled, 2 * t + 1)
                nc.scalar.activation(rt[:, t:t + 1], ms[:, t:t + 1], ACT.Sqrt).then_inc(rooted, 1)

        @block.vector
        def _(dve):
            def gain(t):
                dve.wait_ge(turned, t + 1)
                for b in range(2):
                    ins = nc.vector.tensor_tensor(
                        dstT[:, 4 * b:4 * b + 4, t * P:(t + 1) * P], banks[b][:, :].rearrange("p (k q) -> p k q", k=4),
                        prm[:, gain_row + 4 * b:gain_row + 4 * b + 4].rearrange("p (k q) -> p k q", q=1).broadcast_to([P, 4, P]), ALU.mult)
                ins.then_inc(evac, 1)

            for t in range(n):
                if make_dve is not None:
                    make_dve(t)
                dve.wait_ge(squared, t + 1)
                nc.vector.tensor_scalar(ms[:, t:t + 1], ss[:, t:t + 1], 1.0 / D, EPS, ALU.mult, ALU.add).then_inc(scaled, 1)
                dve.wait_ge(rooted, t + 1)
                nc.vector.reciprocal(rs[:, t:t + 1], rt[:, t:t + 1]).then_inc(scaled, 1)
                dve.wait_ge(scaled, 2 * t + 2)
                nc.vector.tensor_scalar(xn[:, t], src[:, t], rs[:, t:t + 1], None, ALU.mult).then_inc(normed, 1)
                if t == 1 and before_gain is not None:
                    before_gain()
                if t >= 1:
                    gain(t - 1)
            gain(n - 1)

        @block.tensor
        def _(pe):
            for t in range(n + 1):
                if t < n and make_pe is not None:
                    make_pe(t)
                if t >= 1:
                    pe.wait_ge(normed, t)
                    if t >= 2:
                        pe.wait_ge(evac, t - 1)
                    for k in range(KD):
                        mm = nc.tensor.transpose(banks[k // 4][:, k % 4 * P:(k % 4 + 1) * P], xn[:, t - 1, k * P:(k + 1) * P], ident)
                    mm.then_inc(turned, 1)
        return evac, n

    small = sb("small", [P, 64])

    a_low = Arena()
    w_low = a_low("w_low", [P, KD, 256])
    w_cols = w_in[0].rearrange("(k p) c -> p k c", p=P)
    low_w_in = nc.alloc_semaphore("low_w_in")
    a0 = Arena()
    xt = a0("xt", [P, TT, D])
    xn0 = a0("xn0", [P, TT, D])
    rows = a0("rows", [P, P])
    params_in, rows_turned, prm_ready, cst_in = sem("params_in"), sem("rows_turned"), sem("prm_ready"), sem("cst_in")
    x_in = [sem(f"x_in{t}") for t in range(TT)]
    x_tok = x.rearrange("b (t p) d -> p (b t) d", p=P)
    with nc.Block() as block:
        @block.vector
        def _(dve):
            nc.vector.memset(rows[:, :], 0.0).then_inc(prm_ready, 1)

        @block.sync
        def _(sp):
            sp.wait_ge(prm_ready, 1)
            sp.dma_start(xt[:, 0, :], x_tok[:, 0, :]).then_inc(x_in[0], 16)
            sp.dma_start(cst[:, :], const).then_inc(cst_in, 16)
            for t in range(1, TT):
                sp.dma_start(xt[:, t, :], x_tok[:, t, :]).then_inc(x_in[t], 16)
            params = [(R_MU, rwkv_mu[0, 0:3 * D]), (R_W0, rwkv_w0[0]), (R_A0, rwkv_a0[0]), (R_KK, rwkv_k_k[0]),
                      (R_KA, rwkv_k_a[0]), (R_RK, rwkv_r_k[0].rearrange("h n -> (h n)")), (R_LNW, rwkv_ln_w[0]),
                      (R_LNB, rwkv_ln_b[0]), (R_GMIX, g_mix[0]), (R_GCROSS, g_cross[0]), (R_GFFN, g_ffn[0]),
                      (R_GMEM, g_mem[0]), (R_MULOW, rwkv_mu[0, 3 * D:3 * D + 256])]
            for row, vec in params:
                v = vec.rearrange("(m p) -> m p", p=P)
                sp.dma_start(rows[row:row + v.shape[0], :], v).then_inc(params_in, 16)
            sp.dma_start(w_low[:, :, :], w_cols[:, :, OFF_LOW:OFF_LOW + 256]).then_inc(low_w_in, 16)

        def turn_params(t):
            if t == 1:
                nc.tensor.wait_ge(params_in, 16 * 13)
                nc.tensor.transpose(bank[7][:, 0:P], rows[:, :], ident).then_inc(rows_turned, 1)
            elif t == 0:
                nc.tensor.wait_ge(cst_in, 16)

        def keep_params():
            nc.vector.wait_ge(rows_turned, 1)
            nc.vector.tensor_copy(prm[:, :], bank[7][:, 0:P]).then_inc(prm_ready, 1)
            nc.vector.wait_ge(prm_ready, 2)

        norm_transpose(block, "nx", xt, TT, R_GMIX, xn0, xnT, bank[0:2], src_ready=lambda t: (x_in[t], 16), make_pe=turn_params,
                       before_gain=keep_params)
    a0.free()

    a1 = Arena()
    lowT = a1("lowT", [P, SEQ])
    w3 = a1("w3", [P, 2, 3, KD, P])
    w_up = a1("w_up", [P, 2, P])
    raw = a1("raw", [P, 2, 3, SEQ + 1])
    sh = a1("sh", [P, 2, 3, SEQ])
    dlt = a1("dlt", [P, 3, SEQ])
    sgw, sga, cum, csub, pe_, pi_, pp_, kk, kk2, nrm, bonin, kap, bet, kh, bh, k2, bv = (
        a1(n, [P, 2, SEQ]) for n in ("sgw", "sga", "cum", "csub", "p_end", "p_inv", "p_prev", "kk", "kk2", "nrm",
                                     "bonin", "kap", "bet", "kh", "bh", "k2", "bv"))
    ar = a1("ar", [P, 2, 2, SEQ])
    ar_b = a1("ar_b", [P, 2, 2, SEQ])
    tok = a1("tok", [P, 2, 4, SEQ])
    mats = a1("mats", [P, 2, 2, 4, 4 * CH])

    low_mm, low_raw, low_chain, low_done = (sem(s) for s in (
        "low_mm", "low_raw", "low_chain", "low_done"))
    w3_in = [sem("w3_in0"), sem("w3_in1")]
    (pj_full, pj_free, za_full, za_free, sb_full, sb_free, g_full, g_free, t_full, t_free, raw_zero,
     dve_done, act_done, out_free, cum_ready, exps_ready, kk_ready, kk2_ready, nrm_ready, bon_ready,
     ops_ready, turn_ready, gates_ready, raw_ready, mats_ready, tok_ready, bv_ready, chain) = (sem(s) for s in (
         "pj_full", "pj_free", "za_full", "za_free", "sb_full", "sb_free", "g_full", "g_free", "t_full",
         "t_free", "raw_zero", "dve_done", "act_done", "out_free", "cum_ready", "exps_ready", "kk_ready",
         "kk2_ready", "nrm_ready", "bon_ready", "ops_ready", "turn_ready", "gates_ready", "raw_ready",
         "mats_ready", "tok_ready", "bv_ready", "chain"))
    ar_ready, arb_zero, arb_ready = (sem(s) for s in ("ar_ready", "arb_zero", "arb_ready"))
    store = [sem("store0"), sem("store1")]
    with nc.Block() as block:
        @block.sync
        def _(sp):
            with sp.Fori(0, KD // 2) as i:
                for k in range(2):
                    m = i * 2 + k
                    sp.wait_ge(ops_ready, m + 1)
                    sp.dma_start(rho_dram[bass.ds(m, 1)].rearrange("a p s -> (a p) s"), ar[:, k, 1, :]).then_inc(store[k], 16)
                    sp.wait_ge(bv_ready, m + 1)
                    sp.dma_start(bonus_dram[bass.ds(m, 1)].rearrange("a p s -> (a p) s"), bv[:, k, :]).then_inc(store[k], 16)
                    sp.wait_ge(mats_ready, m * 4 + 4)
                    sp.dma_start(mats_dram[bass.ds(m, 1)].rearrange("a p s -> (a p) s"),
                                 mats[:, k, :, :, :].rearrange("p h c n -> p (h c n)")).then_inc(store[k], 16)
                    for par in range(2):
                        sp.dma_start(
                            low_dram[bass.ds(m * 2, 2), :, par].rearrange("h c s t -> s (h c) t"),
                            mats[par * CH:(par + 1) * CH, k, :, :, 0:CH].rearrange("p h c n -> p (h c) n")).then_inc(store[k], 16)
                    sp.wait_ge(tok_ready, m * 4 + 4)
                    sp.dma_start(tok_dram[bass.ds(m, 1)].rearrange("a p s -> (a p) s"),
                                 tok[:, k, :, :].rearrange("p a s -> p (a s)")).then_inc(store[k], 16)
                    sp.wait_ge(store[k], i * 96 + 96)
                    sp.sem_inc(out_free, 1)

        @block.gpsimd
        def _(pool):
            def loads(m, k):
                for t in range(3):
                    pool.wait_ge(pj_full, m * 3 + t + 1)
                    pool.sem_inc(gone_on, 1)
                    pool.dma_start(w3[:, k, t, :, :], w_cols[:, :, bass.ds(m * P + (OFF_RWKV + t * D), P)]).then_inc(w3_in[k], 16)
                pool.wait_ge(za_full, m * 2 + 2)
                pool.sem_inc(gone_on, 1)
                pool.dma_start(w_up[0:64, k, :], rwkv_w2[0][:, bass.ds(m * P, P)]).then_inc(w3_in[k], 16)
                pool.dma_start(w_up[64:128, k, :], rwkv_a2[0][:, bass.ds(m * P, P)]).then_inc(w3_in[k], 16)

            with pool.Fori(0, KD // 2) as i:
                for k in range(2):
                    loads(i * 2 + k, k)

        @block.tensor
        def _(pe):
            pe.sem_inc(pj_full, 6)
            pe.sem_inc(za_full, 4)
            pe.sem_inc(t_full, 8)
            pe.wait_ge(low_w_in, 16)
            for t in range(2):
                for k in range(KD):
                    mm = nc.tensor.matmul(bank[2 + t][:, :], w_low[:, k, t * P:(t + 1) * P], xnT[:, k, :],
                                          start=(k == 0), stop=(k == KD - 1))
                mm.then_inc(low_mm, 1)

            def project(m, i, k, t):
                pe.wait_ge(pj_free, m * 3 + t + 1)
                for d in range(KD):
                    mm = nc.tensor.matmul(bank[(3 * k + t) % 2][:, :], w3[:, k, t, d, :], xnT[:, d, :],
                                          start=(d == 0), stop=(d == KD - 1))
                mm.then_inc(pj_full, 1)

            def up(m, k, which=(0, 1)):
                for t in which:
                    pe.wait_ge(za_free, m * 2 + t + 1)
                    r = slice(64 * t, 64 * t + 64)
                    nc.tensor.matmul(bank[2][:, :], w_up[r, k, :], lowT[r, :], start=True, stop=True).then_inc(za_full, 1)

            def head_sums(m, k):
                pe.wait_ge(kk2_ready, m + 1)
                pe.wait_ge(sb_free, m * 2 + 1)
                nc.tensor.matmul(bank[3][:, :], bones, kk2[:, k, :], start=True, stop=True).then_inc(sb_full, 1)
                pe.wait_ge(bon_ready, m + 1)
                pe.wait_ge(sb_free, m * 2 + 2)
                nc.tensor.matmul(bank[3][:, :], bones, bonin[:, k, :], start=True, stop=True).then_inc(sb_full, 1)

            def chunk_products(m, k):
                pe.wait_ge(arb_ready, m + 1)
                for qq in range(2):
                    for j in range(2):
                        pe.wait_ge(g_free, m * 4 + 2 * qq + j + 1)
                        pe.sem_inc(gone_on, 1)
                        for c in range(4 * qq + 2 * j, 4 * qq + 2 * j + 2):
                            cb = slice(64 * (c % 2), 64 * (c % 2) + 64)
                            t = slice(c * CH, (c + 1) * CH)
                            dst = bank[4 + j][cb, :].rearrange("p (h n a t) -> p h n a t", h=2, n=2, a=2)
                            for n, left in enumerate((bet, kap)):
                                mm = nc.tensor.matmul(dst[:, :, n], left[:, k, t], ar_b[:, :, :, t].rearrange("p a h t -> p h a t"),
                                                      start=True, stop=True)
                        mm.then_inc(g_full, 1)

            def turns(m, k):
                pe.wait_ge(turn_ready, m + 1)
                for a, src in enumerate((ar[:, k, 0, :], sh[:, k, 2, :], kh[:, k, :], bh[:, k, :])):
                    pe.wait_ge(t_free, m * 4 + a + 1)
                    for t in range(TT):
                        mm = nc.tensor.transpose(bank[6 + a % 2][:, t * P:(t + 1) * P], src[:, t * P:(t + 1) * P], ident)
                    mm.then_inc(t_full, 1)

            def step(m, i, k, nxt, i2, k2_):
                pe.wait_ge(w3_in[k2_], i2 * 80 + 80)
                project(nxt, i2, k2_, 0)
                head_sums(m, k)
                project(nxt, i2, k2_, 1)
                project(nxt, i2, k2_, 2)
                turns(m, k)
                up(nxt, k2_, (0,))
                chunk_products(m, k)
                up(nxt, k2_, (1,))

            pe.wait_ge(w3_in[0], 80)
            for t in range(3):
                project(0, 0, 0, t)
            pe.wait_ge(low_done, 3)
            up(0, 0)
            with pe.Fori(0, KD // 2 - 1) as i:
                step(i * 2, i, 0, i * 2 + 1, i, 1)
                step(i * 2 + 1, i, 1, i * 2 + 2, i + 1, 0)
            step(KD - 2, 0, 0, KD - 1, KD // 2 - 1, 1)
            head_sums(KD - 1, 1)
            turns(KD - 1, 1)
            chunk_products(KD - 1, 1)

        @block.scalar
        def _(act):
            act.sem_inc(pj_free, 2)
            act.sem_inc(za_free, 1)
            act.sem_inc(t_free, 2)
            act.sem_inc(act_done, 2)
            act.wait_ge(raw_zero, 1)
            for t in range(2):
                act.wait_ge(low_mm, t + 1)
                nc.scalar.activation(raw[:, 0, t, 1:SEQ + 1], bank[2 + t][:, :], ACT.Copy).then_inc(low_raw, 1)
            act.wait_ge(low_chain, 4)
            nc.scalar.activation(lowT[0:64, :], sh[0:64, 0, 0, :], ACT.Tanh).then_inc(low_done, 1)
            nc.scalar.activation(lowT[64:128, :], sh[64:128, 0, 0, :], ACT.Copy).then_inc(low_done, 1)
            nc.scalar.activation(sdg[:, :], sh[:, 0, 1, :], ACT.Sigmoid).then_inc(low_done, 1)
            act.wait_ge(low_done, 3)
            def evac_raw(m, k, t):
                act.wait_ge(pj_full, m * 3 + t + 7)
                nc.scalar.activation(raw[:, k, t, 1:SEQ + 1], bank[(3 * k + t) % 2][:, :], ACT.Copy).then_inc(raw_ready, 1)
                act.wait_ge(raw_ready, m * 3 + t + 1)
                act.sem_inc(pj_free, 1)

            def gates(m, k):
                for t, (dst, bias) in enumerate(((sgw, R_W0), (sga, R_A0))):
                    act.wait_ge(za_full, m * 2 + t + 5)
                    nc.scalar.activation(dst[:, k, :], bank[2][:, :], ACT.Sigmoid, bias=col(bias, m)).then_inc(gates_ready, 1)
                    act.wait_ge(gates_ready, m * 2 + t + 1)
                    act.sem_inc(za_free, 1)

            def exps(m, k):
                act.wait_ge(kk_ready, m + 1)
                nc.scalar.activation(kk2[:, k, :], kk[:, k, :], ACT.Square).then_inc(kk2_ready, 1)
                act.wait_ge(cum_ready, m + 1)
                nc.scalar.activation(pe_[:, k, :], cum[:, k, :], ACT.Exp, scale=-SQE).then_inc(exps_ready, 1)
                nc.scalar.activation(pi_[:, k, :], cum[:, k, :], ACT.Exp, scale=SQE).then_inc(exps_ready, 1)
                nc.scalar.activation(pp_[:, k, :], csub[:, k, :], ACT.Exp, scale=-SQE).then_inc(exps_ready, 1)

            def norm_root(m, k):
                act.wait_ge(sb_full, m * 2 + 1)
                nc.scalar.activation(nrm[:, k, :], bank[3][:, :], ACT.Sqrt).then_inc(nrm_ready, 1)

            def evac_turns(m, k):
                act.wait_ge(out_free, m + 1)
                for a in range(4):
                    act.wait_ge(t_full, m * 4 + a + 9)
                    nc.scalar.activation(tok[:, k, a, :], bank[6 + a % 2][:, :], ACT.Copy).then_inc(tok_ready, 1)
                    act.wait_ge(tok_ready, m * 4 + a + 1)
                    act.sem_inc(t_free, 1)
                act.sem_inc(act_done, 1)

            def blocks(m, k):
                act.wait_ge(ar_ready, m + 1)
                act.wait_ge(g_free, m * 4 + 2)
                for n in range(2):
                    for h in range(2):
                        hb = slice(64 * h, 64 * h + 64)
                        ins = nc.scalar.activation(ar_b[hb, n, h, :], ar[hb, k, n, :], ACT.Copy)
                ins.then_inc(arb_ready, 1)

            act.wait_ge(arb_zero, 1)

            def front(m, k, m_before=None, k_before=None):
                act.wait_ge(dve_done, m + 1)
                evac_raw(m, k, 0)
                if m_before is not None:
                    norm_root(m_before, k_before)
                evac_raw(m, k, 1)
                if m_before is not None:
                    blocks(m_before, k_before)
                evac_raw(m, k, 2)
                if m_before is not None:
                    evac_turns(m_before, k_before)
                gates(m, k)
                act.wait_ge(t_full, m * 4 + 4)
                exps(m, k)

            front(0, 0)
            with act.Fori(0, KD // 2 - 1) as i:
                front(i * 2 + 1, 1, i * 2, 0)
                front(i * 2 + 2, 0, i * 2 + 1, 1)
            front(KD - 1, 1, KD - 2, 0)
            norm_root(KD - 1, 1)
            blocks(KD - 1, 1)
            evac_turns(KD - 1, 1)

        LINKS = 19

        @block.vector
        def _(dve):
            dve.sem_inc(dve_done, 2)
            dve.sem_inc(sb_free, 1)
            dve.sem_inc(g_free, 2)
            dve.sem_inc(out_free, 2)
            nc.vector.memset(raw[:, :, :, 0:1], 0.0).then_inc(raw_zero, 1)
            dve.wait_ge(raw_zero, 1)
            nc.vector.memset(ar_b[:, :, :, :], 0.0).then_inc(arb_zero, 1)
            for t in range(2):
                dve.wait_ge(low_raw, t + 1)
                nc.vector.tensor_tensor(dlt[:, t, :], raw[:, 0, t, 0:SEQ], raw[:, 0, t, 1:SEQ + 1], ALU.subtract).then_inc(low_chain, 1)
                dve.wait_ge(low_chain, 2 * t + 1)
                nc.vector.scalar_tensor_tensor(out=sh[:, 0, t, :], in0=dlt[:, t, :], scalar=col(R_MULOW, t),
                                               in1=raw[:, 0, t, 1:SEQ + 1], op0=ALU.mult, op1=ALU.add).then_inc(low_chain, 1)
            dve.wait_ge(low_done, 3)
            with dve.Fori(0, KD // 2) as i:
                for k in range(2):
                    m = i * 2 + k
                    count = [0]

                    def link(ins):
                        count[0] += 1
                        ins.then_inc(chain, 1)
                        dve.wait_ge(chain, m * LINKS + count[0])

                    dve.wait_ge(t_full, m * 4 + 4)
                    dve.wait_ge(act_done, m + 1)
                    dve.wait_ge(out_free, m + 1)
                    r_, k_, v_ = (sh[:, k, t, :] for t in range(3))
                    alpha, rho = ar[:, k, 0, :], ar[:, k, 1, :]
                    for t in (1, 0, 2):
                        dve.wait_ge(raw_ready, m * 3 + t + 1)
                        link(nc.vector.tensor_tensor(dlt[:, t, :], raw[:, k, t, 0:SEQ], raw[:, k, t, 1:SEQ + 1], ALU.subtract))
                        link(nc.vector.scalar_tensor_tensor(out=sh[:, k, t, :], in0=dlt[:, t, :], scalar=col(R_MU + 8 * t, m),
                                                            in1=raw[:, k, t, 1:SEQ + 1], op0=ALU.mult, op1=ALU.add))
                        if t == 1:
                            link(nc.vector.tensor_scalar(kk[:, k, :], k_, col(R_KK, m), None, ALU.mult))
                            dve.sem_inc(kk_ready, 1)
                    dve.wait_ge(gates_ready, m * 2 + 1)
                    link(nc.vector.tensor_tensor_scan(cum[:, k, :], cst[:, C_RESET:C_RESET + SEQ], sgw[:, k, :], 0.0, ALU.mult, ALU.add))
                    link(nc.vector.tensor_tensor(csub[:, k, :], cum[:, k, :], sgw[:, k, :], ALU.subtract))
                    dve.sem_inc(cum_ready, 1)
                    dve.wait_ge(gates_ready, m * 2 + 2)
                    link(nc.vector.tensor_scalar(k2[:, k, :], sga[:, k, :], 1.0, col(R_KA, m), ALU.subtract, ALU.mult))
                    link(nc.vector.scalar_tensor_tensor(out=k2[:, k, :], in0=k2[:, k, :], scalar=1.0, in1=k_, op0=ALU.add, op1=ALU.mult))
                    link(nc.vector.scalar_tensor_tensor(out=bonin[:, k, :], in0=r_, scalar=col(R_RK, m), in1=k2[:, k, :],
                                                        op0=ALU.mult, op1=ALU.mult))
                    dve.sem_inc(bon_ready, 1)
                    dve.wait_ge(nrm_ready, m + 1)
                    dve.sem_inc(sb_free, 1)
                    link(nc.vector.tensor_scalar(nrm[:, k, :], nrm[:, k, :], 1e-12, None, ALU.max))
                    link(nc.vector.reciprocal(nrm[:, k, :], nrm[:, k, :]))
                    link(nc.vector.tensor_tensor(kk[:, k, :], kk[:, k, :], nrm[:, k, :], ALU.mult))
                    dve.wait_ge(exps_ready, m * 3 + 3)
                    nc.vector.tensor_copy(decay_end[:, bass.ds(m, 1), :].rearrange("p a c -> p (a c)"), pe_[:, k, CH - 1::CH])
                    nc.vector.tensor_tensor(alpha, kk[:, k, :], pp_[:, k, :], ALU.mult)
                    nc.vector.tensor_tensor(rho, r_, pe_[:, k, :], ALU.mult)
                    link(nc.vector.tensor_tensor(bet[:, k, :], kk[:, k, :], sga[:, k, :], ALU.mult))
                    dve.sem_inc(ar_ready, 1)
                    nc.vector.tensor_tensor(kap[:, k, :], k2[:, k, :], pi_[:, k, :], ALU.mult)
                    link(nc.vector.tensor_tensor(bet[:, k, :], bet[:, k, :], pi_[:, k, :], ALU.mult))
                    dve.sem_inc(ops_ready, 1)
                    chunks = lambda t: t[:, k, :].rearrange("p (c t) -> p c t", t=CH)
                    last_decay = chunks(pe_)[:, :, CH - 1:CH].broadcast_to([P, NCH, CH])
                    nc.vector.tensor_tensor(chunks(kh), chunks(kap), last_decay, ALU.mult)
                    link(nc.vector.scalar_tensor_tensor(out=chunks(bh), in0=chunks(bet), scalar=-1.0, in1=last_decay,
                                                        op0=ALU.mult, op1=ALU.mult))
                    dve.sem_inc(turn_ready, 1)
                    dve.wait_ge(sb_full, m * 2 + 2)
                    link(nc.vector.tensor_tensor(bv[:, k, :], bank[3][:, :], v_, ALU.mult))
                    dve.sem_inc(sb_free, 1)
                    dve.sem_inc(bv_ready, 1)
                    mask = cst[:, C_MASK:C_MASK + 256].rearrange("p (a n) -> p a n", a=1).broadcast_to([P, 2, 256])
                    for f in range(4):
                        dve.wait_ge(g_full, m * 4 + f + 1)
                        nc.vector.tensor_tensor(mats[:, k, :, f, :], bank[4 + f % 2][:, :].rearrange("p (h n) -> p h n", h=2),
                                                mask, ALU.mult).then_inc(mats_ready, 1)
                        dve.wait_ge(mats_ready, m * 4 + f + 1)
                        dve.sem_inc(g_free, 1)
                    dve.sem_inc(dve_done, 1)
                    assert count[0] == LINKS, count
    a1.free()
    a_low.free()
    end_stage()

    mix = sb("mix", [P, KD, SEQ])
    gate_b = sb("gate_b", [P, KD, SEQ])
    a2 = Arena()
    lo = a2("lo", [P, CH, CH])
    ti = a2("ti", [P, CH, CH])
    upd = a2("upd", [P, CH * CH // 4])
    wr = a2("wr", [P, 3, KD, 512])
    qk = a2("qk", [P, 10, SEQ])
    vt = a2("vt", [P, TT, KV * HEAD])
    rope_tmp = a2("rope_tmp", [P, 2, SEQ])
    rope_sin_x = a2("rope_sin_x", [P, 2, SEQ])
    cos_t, sin_t, ang, turn = (a2(n, [P, SEQ]) for n in ("cos_t", "sin_t", "ang", "turn"))
    pos_i = a2("pos_i", [P, SEQ], positions.tensor.dtype)
    sink = a2("sink", [P, HEADS])
    kp = a2("kp", [P, 2, 2, SEQ])
    nsink = a2("nsink", [P, HEADS])
    band = a2("band", [P, 2, 2 * P], BF16)
    ident_b = a2("ident_b", [P, P], BF16)
    pr = a2("pr", [P, 4, 2, 2 * P])
    prT = a2("prT", [P, 2, 512])
    inv_sum = upd[:, :].rearrange("p (i h q) -> p i h q", i=4, h=2)
    mx, nmx, sums, es, sd, rec = (a2(n, [P, 4, 2]) for n in ("mx", "nmx", "sums", "es", "sd", "rec"))

    lo_in, tab_in, sink_in, lo_chain, ti_ready, ti_stored, pos_ready = (sem(n) for n in (
        "lo_in", "tab_in", "sink_in", "lo_chain", "ti_ready", "ti_stored", "pos_ready"))
    wr_in = [sem(f"wr_in{n}") for n in range(3)]
    first_in = [sem(f"first_in{d}") for d in range(KD)]
    f_full, f_evac, tab_done, rot_full, rope_x, rope_s, roped = (sem(n) for n in (
        "f_full", "f_evac", "tab_done", "rot_full", "rope_x", "rope_s", "roped"))
    s_full, mx_ready, p_ready, rec_ready, inv_ready, pt_full, pt_ready, o_full, o_used, att_chain, kp_zero, band_ready = (
        sem(n) for n in ("s_full", "mx_ready", "p_ready", "rec_ready", "inv_ready", "pt_full", "pt_ready", "o_full",
                         "o_used", "att_chain", "kp_zero", "band_ready"))
    w_blocks = [0, 512, 1024] + [OFF_GATE + 512 * n for n in range(4)]
    fills = ([("q", b, g) for b in range(2) for g in range(4)] + [("k", 2, g) for g in range(2)]
             + [("v", 2, t) for t in range(TT)] + [("a", 3 + b, g) for b in range(2) for g in range(4)]
             + [("b", 5 + b, g) for b in range(2) for g in range(4)])
    units = [(pp, n, g) for pp in range(2) for n in range(TT) for g in range(4)]

    def load_q(engine, n, c, d):
        for a in range(2):
            engine.dma_start(wr[:, n, d, :].rearrange("p (g a j) -> p g a j", a=2, g=4)[:, :, a, :],
                             w_cols[:, d, c + 256 * a:c + 256 * a + 256].rearrange("p (g j) -> p g j", g=4))\
                .then_inc(first_in[d] if n == 0 else wr_in[n], 16)

    NU = len(units)
    with nc.Block() as block:
        @block.sync
        def _(sp):
            for n, c in enumerate(w_blocks):
                if n >= 3:
                    sp.wait_ge(f_full, 1 + max(i for i, f in enumerate(fills) if f[1] == n - 3))
                if n < 2:
                    for d in range(KD):
                        load_q(sp, n, c, d)
                    if n == 0:
                        sp.dma_start(lo[:, :, :], low_dram.rearrange("h q c s t -> (h q c) s t")).then_inc(lo_in, 16)
                else:
                    sp.dma_start(wr[:, n % 3, :, :], w_cols[:, :, c:c + 512]).then_inc(wr_in[n % 3], 16)
            sp.wait_ge(ti_ready, 1)
            sp.dma_start(inv_dram.rearrange("h q c s t -> (h q c) s t"), ti[:, :, :]).then_inc(ti_stored, 16)
            sp.wait_ge(ti_stored, 16)

        @block.vector
        def _(dve):
            n = [0]

            def link(ins):
                n[0] += 1
                ins.then_inc(pos_ready, 1)
                dve.wait_ge(pos_ready, n[0])

            dve.wait_ge(tab_in, 16)
            link(nc.vector.tensor_copy(ang[:, :], pos_i[:, :]))
            link(nc.vector.tensor_scalar(ang[:, :], ang[:, :], cst[:, C_INVF:C_INVF + 1], None, ALU.mult))
            magic = 1.5 * 2 ** 23
            for dst, quarter in ((sin_t, 0.0), (cos_t, 0.25)):
                link(nc.vector.tensor_scalar(turn[:, :], ang[:, :], 1.0 / TWO_PI, quarter, ALU.mult, ALU.add))
                link(nc.vector.tensor_scalar(turn[:, :], turn[:, :], magic, magic, ALU.add, ALU.subtract))
                hi = 6.28125
                mid = float(np.float32(TWO_PI - hi).view(np.uint32) & np.uint32(0xFFFFF000))
                mid = float(np.uint32(np.float32(TWO_PI - hi).view(np.uint32) & np.uint32(0xFFFFF000)).view(np.float32))
                low = float(TWO_PI - hi - mid)
                link(nc.vector.scalar_tensor_tensor(out=dst[:, :], in0=turn[:, :], scalar=-hi, in1=ang[:, :], op0=ALU.mult, op1=ALU.add))
                link(nc.vector.scalar_tensor_tensor(out=dst[:, :], in0=turn[:, :], scalar=-mid, in1=dst[:, :], op0=ALU.mult, op1=ALU.add))
                link(nc.vector.scalar_tensor_tensor(out=dst[:, :], in0=turn[:, :], scalar=-low, in1=dst[:, :], op0=ALU.mult, op1=ALU.add))
                if quarter:
                    link(nc.vector.tensor_scalar(dst[:, :], dst[:, :], float(np.pi / 2), None, ALU.add))
                link(nc.vector.tensor_scalar(dst[:, :], dst[:, :], 3.1415925, -3.1415925, ALU.min, ALU.max))
            dve.sem_inc(tab_done, 1)
            nc.vector.tensor_copy(ident_b[:, :], ident).then_inc(band_ready, 1)
            for h in range(2):
                nc.vector.tensor_copy(band[:, h, :], cst[:, C_BAND:C_BAND + 2 * P]).then_inc(band_ready, 1)
            dve.wait_ge(sink_in, 16)
            nc.vector.tensor_scalar(nsink[:, :], sink[:, :], -1.0, None, ALU.mult).then_inc(band_ready, 1)

            def rope(i):
                if i == 0:
                    dve.wait_ge(tab_done, 3)
                dve.wait_ge(rot_full, i + 1)
                nc.vector.tensor_tensor(rope_sin_x[:, i % 2, :], bank[2 + i % 6][:, :], sin_t[:, :], ALU.mult).then_inc(rope_s, 1)
                dve.wait_ge(rope_s, i + 1)
                dve.wait_ge(rope_x, i + 1)
                if i < 8:
                    ins = nc.vector.tensor_tensor(qk[:, i, :], rope_tmp[:, i % 2, :], rope_sin_x[:, i % 2, :], ALU.add)
                else:
                    dve.wait_ge(kp_zero, 1)
                    for h in range(2):
                        hb = slice(64 * h, 64 * h + 64)
                        ins = nc.vector.tensor_tensor(kp[hb, i - 8, h, :], rope_tmp[hb, i % 2, :], rope_sin_x[hb, i % 2, :], ALU.add)
                ins.then_inc(roped, 1)

            n[0] = 0

            def follow(ins):
                n[0] += 1
                ins.then_inc(lo_chain, 1)
                dve.wait_ge(lo_chain, n[0])

            follow(nc.vector.memset(ti[:, :, :], 0.0))
            follow(nc.vector.memset(ti[:, :, :].rearrange("p s t -> p (s t)")[:, ::CH + 1], 1.0))
            dve.wait_ge(lo_in, 16)
            for j in range(CH - 1):
                r, c = j + 1, CH - 1 - j
                u = upd[:, 0:r * c].rearrange("p (r c) -> p r c", c=c)
                follow(nc.vector.tensor_tensor(u, ti[:, 0:r, j:j + 1].broadcast_to([P, r, c]),
                                               lo[:, j:j + 1, j + 1:].broadcast_to([P, r, c]), ALU.mult))
                follow(nc.vector.tensor_tensor(ti[:, 0:r, j + 1:], ti[:, 0:r, j + 1:], u, ALU.subtract))
                if j % 5 == 4 and j // 5 < 10 + 2 and j // 5 >= 2:
                    rope(j // 5 - 2)
            dve.sem_inc(ti_ready, 1)

        @block.tensor
        def _(pe):
            def rot(i):
                pe.wait_ge(f_evac, i + 1)
                if i >= 6:
                    pe.wait_ge(rope_s, i - 5)
                nc.tensor.matmul(bank[2 + i % 6][:, :], cst[:, C_ROT:C_ROT + P], qk[:, i, :], start=True, stop=True).then_inc(rot_full, 1)

            for i, (kind, b, g) in enumerate(fills):
                if b > 0:
                    pe.wait_ge(wr_in[b % 3], 16 * (b // 3 + {0: 0, 1: 16, 2: 1}[b % 3]))
                if i >= 2:
                    pe.wait_ge(f_evac, i - 1)
                w = wr[:, b % 3, :, :]
                for d in range(KD):
                    if i == 0:
                        pe.wait_ge(first_in[d], 32)
                    st = dict(start=(d == 0), stop=(d == KD - 1))
                    if kind == "v":
                        mm = nc.tensor.matmul(bank[i % 2][:, 0:256], xnT[:, d, g * P:(g + 1) * P], w[:, d, 256:512], **st)
                    else:
                        mm = nc.tensor.matmul(bank[i % 2][:, :], w[:, d, g * P:(g + 1) * P], xnT[:, d, :], **st)
                mm.then_inc(f_full, 1)
                if 2 <= i <= 20 and i % 2 == 0:
                    rot(i // 2 - 1)

            def scores(u):
                pp, n, g = units[u]
                if u >= 4:
                    pe.wait_ge(p_ready, u - 3)
                k0, width = (0, P) if n == 0 else ((n - 1) * P, 2 * P)
                first = P if n == 0 else 0
                dst = bank[u % 4][:, :].rearrange("p (h k) -> p h k", h=2)[:, :, 0:width]
                nc.tensor.matmul(dst, qk[:, 4 * pp + g, n * P:(n + 1) * P], kp[:, pp, :, k0:k0 + width], start=True, stop=False)
                nc.tensor.matmul(dst, ident_b[:, :], band[:, :, first:2 * P], start=False, stop=True).then_inc(s_full, 1)

            def turn_p(u):
                n = units[u][1]
                pe.wait_ge(inv_ready, u + 1)
                if u >= 2:
                    pe.wait_ge(pt_ready, u - 1)
                for h in range(2):
                    for s in range(1 if n == 0 else 2):
                        mm = nc.tensor.matmul(bank[4 + u % 2][:, (2 * h + s) * P:(2 * h + s + 1) * P],
                                              pr[:, u % 4, h, s * P:(s + 1) * P], inv_sum[:, u % 4, h, :], start=True, stop=True)
                mm.then_inc(pt_full, 1)

            def weigh(u):
                pp, n, g = units[u]
                pe.wait_ge(pt_ready, u + 1)
                if u >= 2:
                    pe.wait_ge(o_used, u - 1)
                ob = slice(64 * (g % 2), 64 * (g % 2) + 64)
                tiles = [0] if n == 0 else [n - 1, n]
                for h in range(2):
                    kv = 2 * pp + h
                    for s, t in enumerate(tiles):
                        mm = nc.tensor.matmul(bank[6 + u % 2][ob, h * P:(h + 1) * P], vt[:, t, kv * HEAD:(kv + 1) * HEAD],
                                              prT[:, u % 2, (2 * h + s) * P:(2 * h + s + 1) * P],
                                              start=(s == 0), stop=(s == len(tiles) - 1))
                mm.then_inc(o_full, 1)

            pe.wait_ge(roped, 10)
            pe.wait_ge(band_ready, 4)
            pe.wait_ge(f_evac, len(fills))
            for u in range(NU + 4):
                if u < NU:
                    scores(u)
                if 3 <= u < NU + 3:
                    turn_p(u - 3)
                if u >= 4:
                    weigh(u - 4)

        @block.scalar
        def _(act):
            act.dma_start(pos_i[:, :], positions.partition_broadcast(P)).then_inc(tab_in, 16)
            act.dma_start(sink[:, :], attn_sinks.partition_broadcast(P)).then_inc(sink_in, 16)
            act.wait_ge(tab_done, 1)
            nc.scalar.activation(sin_t[:, :], sin_t[:, :], ACT.Sin).then_inc(tab_done, 1)
            nc.scalar.activation(cos_t[:, :], cos_t[:, :], ACT.Sin).then_inc(tab_done, 1)
            for i, (kind, b, g) in enumerate(fills):
                act.wait_ge(f_full, i + 1)
                src = bank[i % 2][:, :]
                if kind == "q":
                    nc.scalar.activation(qk[:, 4 * b + g, :], src, ACT.Copy, scale=HEAD ** -0.5).then_inc(f_evac, 1)
                elif kind == "k":
                    nc.scalar.activation(qk[:, 8 + g, :], src, ACT.Copy).then_inc(f_evac, 1)
                elif kind == "v":
                    nc.scalar.activation(vt[:, g, :], src[:, 0:256], ACT.Copy).then_inc(f_evac, 1)
                elif kind == "a":
                    nc.scalar.activation(mix[:, 4 * (b - 3) + g, :], src, ACT.Sigmoid).then_inc(f_evac, 1)
                else:
                    nc.scalar.activation(gate_b[:, 4 * (b - 5) + g, :], src, ACT.Sigmoid).then_inc(f_evac, 1)

            def exps(u):
                width = P if units[u][1] == 0 else 2 * P
                act.wait_ge(mx_ready, u + 1)
                if u >= 4:
                    act.wait_ge(pt_full, u - 3)
                for h in range(2):
                    nc.scalar.activation(pr[:, u % 4, h, 0:width], bank[u % 4][:, h * 2 * P:h * 2 * P + width], ACT.Exp,
                                         bias=nmx[:, u % 4, h:h + 1], accum_out=sums[:, u % 4, h:h + 1])
                nc.scalar.activation(es[:, u % 4, :], sd[:, u % 4, :], ACT.Exp).then_inc(p_ready, 1)

            def evac_p(u):
                act.wait_ge(pt_full, u + 1)
                if u >= 2:
                    act.wait_ge(o_full, u - 1)
                n = units[u][1]
                if n == 0:
                    v = prT[:, u % 2, :].rearrange("p (h s q) -> p h s q", h=2, s=2)[:, :, 0, :]
                    w = bank[4 + u % 2][:, :].rearrange("p (h s q) -> p h s q", h=2, s=2)[:, :, 0, :]
                else:
                    v, w = prT[:, u % 2, :], bank[4 + u % 2][:, :]
                nc.scalar.activation(v, w, ACT.Copy).then_inc(pt_ready, 1)

            for u in range(NU + 3):
                if u < NU:
                    exps(u)
                if u >= 3:
                    evac_p(u - 3)

        @block.gpsimd
        def _(pool):
            nc.gpsimd.memset(kp[:, :, :, :], 0.0).then_inc(kp_zero, 1)
            pool.wait_ge(tab_done, 3)
            for i in range(10):
                pool.wait_ge(f_evac, i + 1)
                if i >= 2:
                    pool.wait_ge(roped, i - 1)
                nc.gpsimd.tensor_tensor(rope_tmp[:, i % 2, :], qk[:, i, :], cos_t[:, :], ALU.mult).then_inc(rope_x, 1)
            for u in range(NU):
                pool.wait_ge(rec_ready, u + 1)
                if u >= 4:
                    pool.wait_ge(pt_full, u - 3)
                nc.gpsimd.tensor_tensor(inv_sum[:, u % 4, :, :], ident.rearrange("p (a q) -> p a q", a=1).broadcast_to([P, 2, P]),
                                        rec[:, u % 4, :].rearrange("p (h a) -> p h a", a=1).broadcast_to([P, 2, P]), ALU.mult)\
                    .then_inc(inv_ready, 1)

        @block.vector
        def _(dve):
            n_links = [0]

            def link(ins):
                n_links[0] += 1
                ins.then_inc(att_chain, 1)
                dve.wait_ge(att_chain, n_links[0])

            def maxes(u):
                pp, n, g = units[u]
                i, width = u % 4, (P if n == 0 else 2 * P)
                dve.wait_ge(s_full, u + 1)
                link(nc.vector.tensor_reduce(mx[:, i, :], bank[i][:, :].rearrange("p (h k) -> p h k", h=2)[:, :, 0:width], AX, ALU.max))
                of_pair = slice(8 * pp + g, 8 * pp + g + 5, 4)
                link(nc.vector.scalar_tensor_tensor(out=nmx[:, i, :], in0=mx[:, i, :], scalar=-1.0, in1=nsink[:, of_pair],
                                                    op0=ALU.mult, op1=ALU.min))
                nc.vector.tensor_tensor(sd[:, i, :], sink[:, of_pair], nmx[:, i, :], ALU.add).then_inc(mx_ready, 1)

            def over_sum(u):
                i = u % 4
                dve.wait_ge(p_ready, u + 1)
                link(nc.vector.tensor_tensor(rec[:, i, :], sums[:, i, :], es[:, i, :], ALU.add))
                nc.vector.reciprocal(rec[:, i, :], rec[:, i, :]).then_inc(rec_ready, 1)

            def gated(u):
                pp, n, g = units[u]
                dve.wait_ge(o_full, u + 1)
                ob = slice(64 * (g % 2), 64 * (g % 2) + 64)
                m0 = 4 * pp + g // 2
                for h in range(2):
                    v = mix[ob, m0 + 2 * h, n * P:(n + 1) * P]
                    ins = nc.vector.tensor_tensor(v, bank[6 + u % 2][ob, h * P:(h + 1) * P], v, ALU.mult)
                ins.then_inc(o_used, 1)

            for u in range(NU + 5):
                if u < NU:
                    maxes(u)
                if 1 <= u <= NU:
                    over_sum(u - 1)
                if u >= 5:
                    gated(u - 5)
    a2.free()
    end_stage()

    hres = sb("hres", [P, TT, D])
    kv_keep = sb("kv_keep", [P, 2 * CROSS_H * MEM])
    kc = kv_keep[:, 0:CROSS_H * MEM].rearrange("p (n s) -> p n s", n=CROSS_H)
    vc = kv_keep[:, CROSS_H * MEM:].rearrange("p (t c) -> p t c", t=MEM // P)
    w_big = sb("w_big", [P, KD * D])
    w_o1 = w_big[:, :].rearrange("p (k c) -> p k c", k=KD)
    a3 = Arena()
    tok_s = a3("tok_s", [P, 2, 5, SEQ])
    for_kv = a3("for_kv", [P, 2 * CROSS_W * KD])
    w_kv = for_kv[:, :].rearrange("p (d c) -> p d c", d=KD)
    mats_s = for_kv[:, 0:8 * SEQ].rearrange("p (k n h q a t) -> p k n h q a t", k=2, n=2, h=2, q=4, a=2)
    y_in = for_kv[:, 8 * SEQ:12 * SEQ].rearrange("p (k n s) -> p k n s", k=2, n=2)
    rho_s = a3("rho_s", [P, 2, SEQ])
    vb_s = a3("vb_s", [P, 2, 2, NCH, 2, CH])
    ta_s = a3("ta_s", [P, 2, 2, 4, CH])
    w1_s = a3("w1_s", [P, 2, 2, 4, CH])
    w1_b = a3("w1_b", [P, 2, 2, 4, 2, CH])
    diag = a3("diag", [P, 2, NCH, CH])
    two_id = a3("two_id", [P, CH])
    ti_s = kv_keep[:, :].rearrange("p (k h q a t) -> p k h q a t", k=2, h=2, q=4, a=2)
    phi = w_big[:, 0:KD * SEQ].rearrange("p (m c t) -> p m c t", m=KD, t=CH)
    psi = w_big[:, KD * SEQ:].rearrange("p (m c t) -> p m c t", m=KD, t=CH)
    rhop = hres[:, :, :].rearrange("p a (b c t) -> p (a b) c t", b=2, t=CH)
    o_all = xnT[:, :, :].rearrange("p m (c t) -> p m c t", t=CH)
    state = rho_s[:, :, :].rearrange("p i (m t) -> p i m t", t=CH)

    in_s = [sem("chunk_in0"), sem("chunk_in1")]
    IN_ALL = 16 * 8
    y_loaded = [sem("y_loaded0"), sem("y_loaded1")]
    (y_full, y_ready, tw_full, tw_act, tw_dve, vb_ready, zeroed, xz_full, x_used, z_used, id_ready, diag_ready, state_ready, st_full,
     os_full, o_ready) = (sem(n) for n in (
         "y_full", "y_ready", "tw_full", "tw_act", "tw_dve", "vb_ready", "zeroed", "xz_full", "x_used", "z_used", "id_ready",
         "diag_ready", "state_ready", "st_full", "os_full", "o_ready"))

    vb_flat = vb_s[:, :, :, :, :, :].rearrange("p k n u a t -> p (k n u a t)")
    mem_s, mem_n = (vb_flat[:, i * 2 * D:(i + 1) * 2 * D].rearrange("p (t d) -> p t d", d=D) for i in range(2))
    memT = w1_b[:, :, :, :, :, :].rearrange("p k h q a t -> p (k h q a t)").rearrange("p (d s) -> p d s", s=MEM)
    mem_in, kv_in = sem("mem_in"), sem("kv_in")

    def halves(c):
        return slice(64 * (c % 2), 64 * (c % 2) + 64)

    def one(t, m):
        return t[:, bass.ds(m, 1)] if not isinstance(m, int) else t[:, m:m + 1]

    with nc.Block() as block:
        @block.sync
        def _(sp):
            def y_loads(m, k):
                sp.dma_start(y_in[:, k, 0, :].rearrange("p (n t) -> p n t", t=CH),
                             mats_dram[bass.ds(m, 1)].rearrange("a p (n j t) -> (a p) n j t", j=4, t=CH)[:, :, 2, :]).then_inc(y_loaded[k], 16)
                sp.dma_start(y_in[:, k, 1, :], tok_dram[bass.ds(m, 1)].rearrange("a p s -> (a p) s")[:, SEQ:2 * SEQ]).then_inc(y_loaded[k], 16)

            def loads(m, k):
                sp.wait_ge(xz_full, m * 2 + 2)
                sp.sem_inc(gone_on, 1)
                sp.wait_ge(x_used, m + 1)
                sp.sem_inc(gone_on, 1)
                sp.dma_start(tok_s[:, k, 0:4, :].rearrange("p a s -> p (a s)"),
                             tok_dram[bass.ds(m, 1)].rearrange("a p s -> (a p) s")).then_inc(in_s[k], 16)
                sp.wait_ge(zeroed, 4)
                sp.sem_inc(gone_on, 1)
                for par in range(2):
                    rows = slice(par * CH, (par + 1) * CH)
                    sp.dma_start(ti_s[rows, k, :, :, par, :].rearrange("p h c t -> p (h c) t"),
                                 inv_dram[bass.ds(m * 2, 2), :, par].rearrange("h c s t -> s (h c) t")).then_inc(in_s[k], 16)
                    for n, kind in enumerate((1, 3)):
                        sp.dma_start(mats_s[rows, k, n, :, :, par, :].rearrange("p h c t -> p (h c) t"),
                                     mats_dram[bass.ds(m, 1), rows].rearrange("a p (u j t) -> (a p) u j t", j=4, t=CH)[:, :, kind, :])\
                            .then_inc(in_s[k], 16)
                sp.dma_start(rho_s[:, k, :], rho_dram[bass.ds(m, 1)].rearrange("a p s -> (a p) s")).then_inc(in_s[k], 16)

            y_loads(0, 0)
            with sp.Fori(0, KD // 2 - 1) as i:
                for k in range(2):
                    m = i * 2 + k
                    sp.wait_ge(y_full, m + 1)
                    sp.sem_inc(gone_on, 1)
                    y_loads(m + 1, 1 - k)
                    loads(m, k)
            sp.wait_ge(y_full, KD - 1)
            y_loads(KD - 1, 1)
            loads(KD - 2, 0)
            loads(KD - 1, 1)
            sp.wait_ge(xz_full, 2 * KD + 4)
            sp.dma_start(mem_s, mem.rearrange("b (t p) d -> p (b t) d", p=P)).then_inc(mem_in, 16)
            sp.dma_start(w_kv, w_kv_cross[0].rearrange("(k p) c -> p k c", p=P)).then_inc(kv_in, 16)

        @block.gpsimd
        def _(pool):
            nc.gpsimd.memset(kv_keep[:, :], 0.0).then_inc(zeroed, 1)
            nc.gpsimd.memset(w1_b[:, :], 0.0).then_inc(zeroed, 1)
            nc.gpsimd.memset(vb_s[:, :, :, :, :, :], 0.0).then_inc(vb_ready, 1)
            pool.wait_ge(vb_ready, 1)
            with pool.Fori(0, KD // 2) as i:
                for k in range(2):
                    pool.wait_ge(in_s[k], i * IN_ALL + IN_ALL)
                    pool.sem_inc(gone_on, 1)
                    for n, kind in enumerate((1, 3)):
                        for par in range(2):
                            rows = slice(par * CH, (par + 1) * CH)
                            ins = nc.gpsimd.tensor_copy(vb_s[rows, k, n, :, par, :], tok_s[rows, k, kind, :].rearrange("p (u t) -> p u t", t=CH))
                    ins.then_inc(vb_ready, 1)

        @block.tensor
        def _(pe):
            pe.sem_inc(xz_full, 4)
            pe.sem_inc(y_full, 1)

            def y_part(m, i, k):
                pe.wait_ge(y_loaded[k], i * 32 + 32)
                pe.wait_ge(y_ready, m + 1)
                pe.sem_inc(gone_on, 1)
                for c in range(NCH):
                    cb = halves(c)
                    for h in range(2):
                        ch = slice(c // 2 * P + h * 64, c // 2 * P + h * 64 + 64)
                        at = (h * 4 + c // 2) * CH
                        mm = nc.tensor.matmul(bank[0][cb, ch], y_in[cb, k, 0, at:at + CH], y_in[cb, k, 1, ch], start=True, stop=True)
                mm.then_inc(y_full, 1)

            def solve_part(m, i, k):
                pe.wait_ge(in_s[k], i * IN_ALL + IN_ALL)
                pe.wait_ge(y_ready, m + 2)
                pe.wait_ge(tw_act, m + 1)
                pe.wait_ge(tw_dve, m + 1)
                pe.sem_inc(gone_on, 1)
                for h in range(2):
                    for q in range(4):
                        mm = nc.tensor.matmul(bank[1 + h][:, q * P:(q + 1) * P], ti_s[:, k, h, q, :, :].rearrange("p a t -> p (a t)"),
                                              tok_s[:, k, 0:5:4, q * P + h * 64:q * P + h * 64 + 64], start=True, stop=True)
                mm.then_inc(tw_full, 1)

            def xz_part(m, k):
                pe.wait_ge(tw_act, m + 2)
                pe.wait_ge(tw_dve, m + 2)
                pe.wait_ge(vb_ready, m + 2)
                pe.wait_ge(x_used, m + 2)
                pe.sem_inc(gone_on, 1)

                def blocks(t):
                    return t.rearrange("p a t -> p (a t)")

                for q in range(4):
                    to = slice(q * P, (q + 1) * P)
                    for h in range(2):
                        hb = slice(64 * h, 64 * h + 64)
                        nc.tensor.matmul(bank[3][hb, to], ta_s[:, k, h, q, :], blocks(mats_s[:, k, 0, h, q]), start=True, stop=True)
                        mm = nc.tensor.matmul(bank[4][hb, to], ta_s[:, k, h, q, :], blocks(vb_s[:, k, 1, 2 * q + h]), start=True, stop=True)
                mm.then_inc(xz_full, 1)
                pe.wait_ge(z_used, m + 1)
                pe.sem_inc(gone_on, 1)
                for q in range(4):
                    to = slice(q * P, (q + 1) * P)
                    for h in range(2):
                        hb = slice(64 * h, 64 * h + 64)
                        ch = slice(q * P + h * 64, q * P + h * 64 + 64)
                        nc.tensor.matmul(bank[6][hb, to], tok_s[:, k, 1, ch], blocks(mats_s[:, k, 1, h, q]), start=True, stop=False)
                        nc.tensor.matmul(bank[6][hb, to], w1_s[:, k, h, q, :], blocks(mats_s[:, k, 0, h, q]), start=False, stop=True)
                        nc.tensor.matmul(bank[5][hb, to], tok_s[:, k, 2, ch], blocks(vb_s[:, k, 0, 2 * q + h]), start=True, stop=False)
                        mm = nc.tensor.matmul(bank[5][hb, to], tok_s[:, k, 3, ch], blocks(w1_b[:, k, h, q]), start=False, stop=True)
                mm.then_inc(xz_full, 1)

            y_part(0, 0, 0)
            with pe.Fori(0, KD // 2 - 1) as i:
                solve_part(i * 2, i, 0)
                y_part(i * 2 + 1, i, 1)
                xz_part(i * 2, 0)
                solve_part(i * 2 + 1, i, 1)
                y_part(i * 2 + 2, i + 1, 0)
                xz_part(i * 2 + 1, 1)
            solve_part(KD - 2, KD // 2 - 1, 0)
            y_part(KD - 1, KD // 2 - 1, 1)
            xz_part(KD - 2, 0)
            solve_part(KD - 1, KD // 2 - 1, 1)
            xz_part(KD - 1, 1)

            for c in range(NCH):
                if c > 0:
                    pe.wait_ge(state_ready, c)
                    if c < NCH - 1:
                        for m in range(KD):
                            for h in range(2):
                                hb = slice(64 * h, 64 * h + 64)
                                mm = nc.tensor.matmul(bank[0][hb, m * CH:(m + 1) * CH], phi[hb, m, c, :],
                                                      state[hb, c % 2, m, :], start=True, stop=True)
                        mm.then_inc(st_full, 1)
                    if c > 2:
                        pe.wait_ge(o_ready, c - 2)
                    if c == 1:
                        pe.wait_ge(x_used, KD + 2)
                        pe.wait_ge(z_used, KD + 1)
                    for m in range(KD):
                        for h in range(2):
                            hb = slice(64 * h, 64 * h + 64)
                            mm = nc.tensor.matmul(bank[1 + c % 2][hb, m * CH:(m + 1) * CH], state[hb, c % 2, m, :],
                                                  rhop[hb, m, c, :], start=True, stop=True)
                    mm.then_inc(os_full, 1)

        @block.scalar
        def _(act):
            act.sem_inc(y_ready, 1)
            act.sem_inc(tw_act, 1)
            act.sem_inc(z_used, 1)
            act.wait_ge(zeroed, 4)
            with act.Fori(0, KD // 2) as i:
                for k in range(2):
                    m = i * 2 + k
                    act.wait_ge(y_full, m + 2)
                    nc.scalar.activation(tok_s[:, k, 4, :], bank[0][:, :], ACT.Copy).then_inc(y_ready, 1)
                    act.wait_ge(tw_full, m + 1)
                    act.wait_ge(xz_full, m * 2 + 2)
                    solved = bank[1][:, :].rearrange("p (q n t) -> p q n t", n=2, t=CH)
                    nc.scalar.activation(ta_s[:, k, 0], solved[:, :, 0], ACT.Copy)
                    nc.scalar.activation(w1_s[:, k, 0], solved[:, :, 1], ACT.Copy)
                    for par in range(2):
                        rows = slice(par * CH, (par + 1) * CH)
                        ins = nc.scalar.activation(w1_b[rows, k, 0, :, par, :], solved[rows, :, 1], ACT.Copy)
                    ins.then_inc(tw_act, 1)
                    act.wait_ge(xz_full, m * 2 + 6)
                    for b, dst in ((5, psi), (6, o_all)):
                        ins = nc.scalar.activation(one(dst, m).rearrange("p m c t -> p (m c t)"), bank[b][:, :], ACT.Copy)
                    ins.then_inc(z_used, 1)

        @block.vector
        def _(dve):
            dve.sem_inc(tw_dve, 1)
            dve.sem_inc(x_used, 2)
            for t in (mats_s[:, 0], mats_s[:, 1]):
                nc.vector.memset(t, 0.0).then_inc(zeroed, 1)
            nc.vector.tensor_tensor(two_id[:, :], ident[:, 0:CH], ident[:, CH:2 * CH], ALU.add).then_inc(id_ready, 1)
            dve.wait_ge(id_ready, 1)
            dve.wait_ge(zeroed, 4)
            with dve.Fori(0, KD // 2) as i:
                for k in range(2):
                    m = i * 2 + k
                    nc.vector.tensor_tensor(diag[:, k, :, :], two_id[:, :].rearrange("p (a t) -> p a t", a=1).broadcast_to([P, NCH, CH]),
                                            one(decay_end, m).rearrange("p a (c t) -> p (a c) t", t=1).broadcast_to([P, NCH, CH]),
                                            ALU.mult).then_inc(diag_ready, 1)
                    dve.wait_ge(diag_ready, m + 1)
                    dve.wait_ge(tw_full, m + 1)
                    dve.wait_ge(xz_full, m * 2 + 2)
                    solved = bank[2][:, :].rearrange("p (q n t) -> p q n t", n=2, t=CH)
                    nc.vector.tensor_copy(ta_s[:, k, 1], solved[:, :, 0])
                    nc.vector.tensor_copy(w1_s[:, k, 1], solved[:, :, 1])
                    for par in range(2):
                        rows = slice(par * CH, (par + 1) * CH)
                        ins = nc.vector.tensor_copy(w1_b[rows, k, 1, :, par, :], solved[rows, :, 1])
                    ins.then_inc(tw_dve, 1)
                    dve.wait_ge(xz_full, m * 2 + 5)
                    nc.vector.tensor_tensor(one(rhop, m).rearrange("p m c t -> p (m c t)"), bank[3][:, :], rho_s[:, k, :], ALU.add)
                    nc.vector.tensor_tensor(one(phi, m).rearrange("p m c t -> p (m c t)"), bank[4][:, :],
                                            diag[:, k, :, :].rearrange("p c t -> p (c t)"), ALU.add).then_inc(x_used, 1)

            dve.wait_ge(x_used, KD + 2)
            dve.wait_ge(z_used, KD + 1)
            nc.vector.tensor_copy(state[:, 1, :, :], psi[:, :, 0, :]).then_inc(state_ready, 1)
            for c in range(1, NCH):
                if c < NCH - 1:
                    dve.wait_ge(st_full, c)
                    if c > 1:
                        dve.wait_ge(os_full, c - 1)
                    nc.vector.tensor_tensor(state[:, (c + 1) % 2, :, :], bank[0][:, :].rearrange("p (m t) -> p m t", t=CH),
                                            psi[:, :, c, :], ALU.add).then_inc(state_ready, 1)
                dve.wait_ge(os_full, c)
                nc.vector.tensor_tensor(o_all[:, :, c, :], bank[1 + c % 2][:, :].rearrange("p (m t) -> p m t", t=CH),
                                        o_all[:, :, c, :], ALU.add).then_inc(o_ready, 1)

    (g2_in, gn_mean, gn_cen, gn_sq, gn_var, gn_std, gn_g, gn_used, gn_chain, gn_on, gn_done) = (sem(n) for n in (
        "g2_in", "gn_mean", "gn_cen", "gn_sq", "gn_var", "gn_std", "gn_g", "gn_used", "gn_chain", "gn_on", "gn_done"))
    g2_s = tok_s[:, 1, 0:2, :].rearrange("p a s -> p (a s)")
    mem_sq, mem_ms, mem_rt, mem_rs = (small[:, 8 * i:8 * i + MEM // P] for i in range(4))
    m_squared, m_scaled, m_rooted, m_normed, m_turned, m_evac, kv_full, kv_evac, hres_in, wo1_in, gn_mixed, gn_pool = (
        sem(n) for n in ("m_squared", "m_scaled", "m_rooted", "m_normed", "m_turned", "m_evac", "kv_full", "kv_evac",
                         "hres_in", "wo1_in", "gn_mixed", "gn_pool"))
    bonus_in = [sem("bonus_in0"), sem("bonus_in1")]
    cen, bns = rho_s, tok_s[:, 0, 0:2, :]
    sq = diag[:, :, :, :].rearrange("p i c t -> p i (c t)")
    std, on = (t[:, :, :, :, :].rearrange("p i h q t -> p i (h q t)") for t in (ta_s, w1_s))
    eps_gn = a3("eps_gn", [P, 1])
    with nc.Block() as block:
        @block.sync
        def _(sp):
            sp.dma_start(g2_s[:, :], rwkv_g2[0]).then_inc(g2_in, 16)
            for m in range(KD):
                if m >= 2:
                    sp.wait_ge(gn_done, m - 1)
                sp.dma_start(bns[:, m % 2, :], bonus_dram[m]).then_inc(bonus_in[m % 2], 16)
                sp.dma_start(w_o1[:, m, :], w_out[0, m * P:(m + 1) * P, :]).then_inc(wo1_in, 16)
                if m < TT:
                    sp.dma_start(hres[:, m, :], x_tok[:, m, :]).then_inc(hres_in, 16)
            sp.wait_ge(wo1_in, 16 * KD)
            sp.wait_ge(hres_in, 16 * TT)

        @block.tensor
        def _(pe):
            def mean(m):
                if m >= 2:
                    pe.wait_ge(gn_cen, m - 1)
                nc.tensor.matmul(bank[m % 2][:, :], bones, o_all[:, m].rearrange("p c t -> p (c t)"), start=True, stop=True).then_inc(gn_mean, 1)
            mean(0)
            pe.wait_ge(g2_in, 16)
            for m in range(KD):
                if m + 1 < KD:
                    mean(m + 1)
                if m >= 2:
                    pe.wait_ge(gn_used, m - 1)
                nc.tensor.matmul(bank[4 + m % 2][:, :], g2_s[:, m * P:(m + 1) * P], sdg[:, :], start=True, stop=True).then_inc(gn_g, 1)
                pe.wait_ge(gn_sq, m + 1)
                if m >= 2:
                    pe.wait_ge(gn_std, m - 1)
                nc.tensor.matmul(bank[2 + m % 2][:, :], bones, sq[:, m % 2, :], start=True, stop=True).then_inc(gn_var, 1)
                if m in (2, 3):
                    for d in range(4 * (m - 2), 4 * (m - 1)):
                        pe.wait_ge(m_normed, MEM // P)
                        if d >= 2:
                            pe.wait_ge(m_evac, d - 1)
                        for t in range(MEM // P):
                            mm = nc.tensor.transpose(bank[6 + d % 2][:, t * P:(t + 1) * P], mem_n[:, t, d * P:(d + 1) * P], ident)
                        mm.then_inc(m_turned, 1)
                for n in {4: (0,), 5: (1,), 6: (2,), 7: (3, 4, 5)}.get(m, ()):
                    pe.wait_ge(kv_in, 16)
                    pe.wait_ge(m_evac, KD)
                    if n >= 2:
                        pe.wait_ge(kv_evac, n - 1)
                    for d in range(KD):
                        st = dict(start=(d == 0), stop=(d == KD - 1))
                        if n < CROSS_H:
                            mm = nc.tensor.matmul(bank[6 + n % 2][:, 0:MEM], w_kv[:, d, n * P:(n + 1) * P], memT[:, d, :], **st)
                        else:
                            t = n - CROSS_H
                            mm = nc.tensor.matmul(bank[6 + n % 2][:, :], memT[:, d, t * P:(t + 1) * P], w_kv[:, d, CROSS_W:], **st)
                    mm.then_inc(kv_full, 1)

        @block.scalar
        def _(act):
            act.wait_ge(mem_in, 16)
            for t in range(MEM // P):
                nc.scalar.activation(mem_n[:, t], mem_s[:, t], ACT.Square, accum_out=mem_sq[:, t:t + 1]).then_inc(m_squared, 1)
            for m in range(KD):
                i = m % 2
                act.wait_ge(gn_cen, m + 1)
                if m >= 2:
                    act.wait_ge(gn_var, m - 1)
                nc.scalar.activation(sq[:, i, :], cen[:, i, :], ACT.Square).then_inc(gn_sq, 1)
                act.wait_ge(gn_var, m + 1)
                if m >= 2:
                    act.wait_ge(gn_on, m - 1)
                nc.scalar.activation(std[:, i, :], bank[2 + i][:, :], ACT.Sqrt, scale=1.0 / HEAD, bias=eps_gn[:, :]).then_inc(gn_std, 1)
                if m == 0:
                    act.wait_ge(m_scaled, 1)
                    nc.scalar.activation(mem_rt, mem_ms, ACT.Sqrt).then_inc(m_rooted, 1)
                if m == 1:
                    act.wait_ge(m_scaled, 2)
                    for t in range(MEM // P):
                        nc.scalar.activation(mem_n[:, t], mem_s[:, t], ACT.Copy, scale=mem_rs[:, t:t + 1]).then_inc(m_normed, 1)
                if m in (2, 3):
                    for d in range(4 * (m - 2), 4 * (m - 1)):
                        act.wait_ge(m_turned, d + 1)
                        nc.scalar.activation(memT[:, d, :], bank[6 + d % 2][:, 0:MEM], ACT.Copy, scale=col(R_GMEM, d)).then_inc(m_evac, 1)
                for n in {4: (0,), 5: (1,), 6: (2,), 7: (3, 4, 5)}.get(m, ()):
                    act.wait_ge(kv_full, n + 1)
                    if n < CROSS_H:
                        ins = nc.scalar.activation(kc[:, n, :], bank[6 + n % 2][:, 0:MEM], ACT.Copy)
                    else:
                        ins = nc.scalar.activation(vc[:, n - CROSS_H, :], bank[6 + n % 2][:, :], ACT.Copy)
                    ins.then_inc(kv_evac, 1)

        @block.vector
        def _(dve):
            n = [0]

            def link(ins):
                n[0] += 1
                ins.then_inc(gn_chain, 1)
                dve.wait_ge(gn_chain, n[0])

            link(nc.vector.memset(eps_gn[:, :], GN_EPS))

            def centre(m):
                i = m % 2
                dve.wait_ge(gn_mean, m + 1)
                if m >= 2:
                    dve.wait_ge(gn_sq, m - 1)
                nc.vector.scalar_tensor_tensor(out=cen[:, i, :], in0=bank[i][:, :], scalar=-1.0 / HEAD,
                                               in1=o_all[:, m].rearrange("p c t -> p (c t)"), op0=ALU.mult, op1=ALU.add).then_inc(gn_cen, 1)
                dve.wait_ge(gn_cen, m + 1)
            centre(0)
            dve.wait_ge(m_squared, MEM // P)
            nc.vector.tensor_scalar(mem_ms, mem_sq, 1.0 / D, EPS, ALU.mult, ALU.add).then_inc(m_scaled, 1)
            for m in range(KD):
                i = m % 2
                if m + 1 < KD:
                    centre(m + 1)
                dve.wait_ge(gn_std, m + 1)
                link(nc.vector.reciprocal(std[:, i, :], std[:, i, :]))
                if m >= 2:
                    dve.wait_ge(gn_mixed, m - 1)
                link(nc.vector.tensor_tensor(on[:, i, :], cen[:, i, :], std[:, i, :], ALU.mult))
                dve.sem_inc(gn_on, 1)
                dve.wait_ge(bonus_in[i], 16 * (m // 2 + 1))
                link(nc.vector.scalar_tensor_tensor(out=on[:, i, :], in0=on[:, i, :], scalar=col(R_LNW, m), in1=bns[:, i, :],
                                                    op0=ALU.mult, op1=ALU.add))
                dve.sem_inc(gn_done, 1)
                dve.wait_ge(gn_g, m + 1)
                nc.vector.scalar_tensor_tensor(out=on[:, i, :], in0=on[:, i, :], scalar=col(R_LNB, m), in1=bank[4 + i][:, :],
                                               op0=ALU.add, op1=ALU.mult).then_inc(gn_used, 1)
                if m == 0:
                    dve.wait_ge(m_rooted, 1)
                    nc.vector.reciprocal(mem_rs, mem_rt).then_inc(m_scaled, 1)

        @block.gpsimd
        def _(pool):
            for m in range(KD):
                pool.wait_ge(gn_used, m + 1)
                nc.gpsimd.tensor_tensor(on[:, m % 2, :], on[:, m % 2, :], gate_b[:, m], ALU.mult).then_inc(gn_pool, 1)
                pool.wait_ge(gn_pool, m + 1)
                nc.gpsimd.tensor_tensor(mix[:, m], mix[:, m], on[:, m % 2, :], ALU.add).then_inc(gn_mixed, 1)
    a3.free()
    end_stage()

    w_pq = sb("w_pq", [P, 2, KD, 256])
    a5 = Arena()
    xn5 = a5("xn5", [P, TT, D])
    w_qc = a5("w_qc", [P, KD, CROSS_W])
    w_oc = a5("w_oc", [P, CROSS_H, D])
    cpr = a5("cpr", [P, 2, 2, MEM])
    cprT = a5("cprT", [P, 2, 512])
    cmx, csum, crec = (a5(n, [P, 2, 2]) for n in ("cmx", "csum", "crec"))
    qc = gate_b[:, 0:CROSS_H, :]
    oc = gate_b[:, CROSS_H:2 * CROSS_H, :]
    wpq_first = [sem("wpq_first0"), sem("wpq_first1")]
    (wqc_in, woc_in, op_full, h_ready, qc_full, qc_evac, cs_full, cmx_ready, cp_ready, cpn_ready, ct_full,
     ct_evac, co_full, co_evac, c_chain, oo_full) = (sem(n) for n in (
         "wqc_in", "woc_in", "op_full", "h_ready", "qc_full", "qc_evac", "cs_full", "cmx_ready", "cp_ready",
         "cpn_ready", "ct_full", "ct_evac", "co_full", "co_evac", "c_chain", "oo_full"))
    SC = P ** -0.5
    cunits = [(t, hp) for t in range(TT) for hp in range(2)]
    NC_ = len(cunits)
    with nc.Block() as block:
        @block.sync
        def _(sp):
            sp.dma_start(w_qc[:, :, :], w_q_cross[0].rearrange("(k p) c -> p k c", p=P)).then_inc(wqc_in, 16)
            sp.dma_start(w_oc[:, :, :], w_o_cross[0].rearrange("(k p) c -> p k c", p=P)).then_inc(woc_in, 16)
            for b in range(2):
                sp.dma_start(w_pq[:, b], peer_w_q[0].rearrange("(k p) c -> p k c", p=P)[:, :, b * 256:(b + 1) * 256]).then_inc(wpq_first[b], 16)

        def project_out(t):
            for f in range(2):
                if t >= 1:
                    nc.tensor.wait_ge(h_ready, 2 * t + f - 1)
                for d in range(KD):
                    mm = nc.tensor.matmul(bank[2 + f][:, :], mix[:, d, t * P:(t + 1) * P], w_o1[:, d, f * 512:(f + 1) * 512],
                                          start=(d == 0), stop=(d == KD - 1))
                mm.then_inc(op_full, 1)

        def add_residual(t):
            for f in range(2):
                nc.vector.wait_ge(op_full, 2 * t + f + 1)
                v = hres[:, t, f * 512:(f + 1) * 512]
                nc.vector.tensor_tensor(v, bank[2 + f][:, :], v, ALU.add).then_inc(h_ready, 1)
            nc.vector.wait_ge(h_ready, 2 * t + 2)

        xc_ready, xc_at = norm_transpose(block, "nc", hres, TT, R_GCROSS, xn5, xnT, bank[0:2],
                                         src_ready=lambda t: (h_ready, 2 * t + 2), make_pe=project_out, make_dve=add_residual)

        @block.tensor
        def _(pe):
            pe.wait_ge(wqc_in, 16)
            pe.wait_ge(xc_ready, xc_at)
            for n in range(CROSS_H):
                if n >= 2:
                    pe.wait_ge(qc_evac, n - 1)
                for d in range(KD):
                    mm = nc.tensor.matmul(bank[4 + n % 2][:, :], w_qc[:, d, n * P:(n + 1) * P], xnT[:, d, :],
                                          start=(d == 0), stop=(d == KD - 1))
                mm.then_inc(qc_full, 1)

            def scores(u):
                t, hp = cunits[u]
                if u >= 2:
                    pe.wait_ge(cp_ready, u - 1)
                for h in range(2):
                    mm = nc.tensor.matmul(bank[u % 2][:, h * MEM:(h + 1) * MEM], qc[:, 2 * hp + h, t * P:(t + 1) * P],
                                          kc[:, 2 * hp + h, :], start=True, stop=True)
                mm.then_inc(cs_full, 1)

            def turn(u):
                pe.wait_ge(cpn_ready, u + 1)
                if u >= 2:
                    pe.wait_ge(ct_evac, u - 1)
                for h in range(2):
                    for s in range(2):
                        mm = nc.tensor.transpose(bank[2 + u % 2][:, (2 * h + s) * P:(2 * h + s + 1) * P],
                                                 cpr[:, u % 2, h, s * P:(s + 1) * P], ident)
                mm.then_inc(ct_full, 1)

            def weigh(u):
                t, hp = cunits[u]
                pe.wait_ge(ct_evac, u + 1)
                if u >= 2:
                    pe.wait_ge(co_evac, u - 1)
                for h in range(2):
                    for s in range(2):
                        mm = nc.tensor.matmul(bank[4 + u % 2][:, h * P:(h + 1) * P], vc[:, s, (2 * hp + h) * P:(2 * hp + h + 1) * P],
                                              cprT[:, u % 2, (2 * h + s) * P:(2 * h + s + 1) * P], start=(s == 0), stop=(s == 1))
                mm.then_inc(co_full, 1)

            pe.wait_ge(qc_evac, CROSS_H)
            for u in range(NC_ + 2):
                if u < NC_:
                    scores(u)
                if 1 <= u <= NC_:
                    turn(u - 1)
                if u >= 2:
                    weigh(u - 2)
            pe.wait_ge(woc_in, 16)
            pe.wait_ge(co_evac, NC_)
            for b in range(2):
                pe.wait_ge(wpq_first[b], 16)
            for n in range(2 * TT):
                if n >= 2:
                    pe.wait_ge(h_ready, 2 * TT + n - 1)
                t, f = n // 2, n % 2
                for d in range(CROSS_H):
                    mm = nc.tensor.matmul(bank[6 + n % 2][:, :], oc[:, d, t * P:(t + 1) * P], w_oc[:, d, f * 512:(f + 1) * 512],
                                          start=(d == 0), stop=(d == CROSS_H - 1))
                mm.then_inc(oo_full, 1)

        @block.scalar
        def _(act):
            for n in range(CROSS_H):
                act.wait_ge(qc_full, n + 1)
                nc.scalar.activation(qc[:, n, :], bank[4 + n % 2][:, :], ACT.Copy).then_inc(qc_evac, 1)

            def exps(u):
                act.wait_ge(cmx_ready, u + 1)
                for h in range(2):
                    ins = nc.scalar.activation(cpr[:, u % 2, h, :], bank[u % 2][:, h * MEM:(h + 1) * MEM], ACT.Exp, scale=SC,
                                               bias=cmx[:, u % 2, h:h + 1], accum_out=csum[:, u % 2, h:h + 1])
                ins.then_inc(cp_ready, 1)

            def evac(u):
                act.wait_ge(ct_full, u + 1)
                if u >= 2:
                    act.wait_ge(co_full, u - 1)
                nc.scalar.activation(cprT[:, u % 2, :], bank[2 + u % 2][:, :], ACT.Copy).then_inc(ct_evac, 1)

            for u in range(NC_ + 1):
                if u < NC_:
                    exps(u)
                if u >= 1:
                    evac(u - 1)

        @block.vector
        def _(dve):
            n_links = [0]

            def link(ins):
                n_links[0] += 1
                ins.then_inc(c_chain, 1)
                dve.wait_ge(c_chain, n_links[0])

            def maxes(u):
                dve.wait_ge(cs_full, u + 1)
                if u >= 2:
                    dve.wait_ge(cp_ready, u - 1)
                link(nc.vector.tensor_reduce(cmx[:, u % 2, :], bank[u % 2][:, :].rearrange("p (h m) -> p h m", h=2), AX, ALU.max))
                nc.vector.tensor_scalar(cmx[:, u % 2, :], cmx[:, u % 2, :], -SC, None, ALU.mult).then_inc(cmx_ready, 1)

            def normalise(u):
                dve.wait_ge(cp_ready, u + 1)
                link(nc.vector.reciprocal(crec[:, u % 2, :], csum[:, u % 2, :]))
                for h in range(2):
                    ins = nc.vector.tensor_scalar(cpr[:, u % 2, h, :], cpr[:, u % 2, h, :], crec[:, u % 2, h:h + 1], None, ALU.mult)
                ins.then_inc(cpn_ready, 1)

            def collect(u):
                t, hp = cunits[u]
                dve.wait_ge(co_full, u + 1)
                nc.vector.tensor_copy(oc[:, 2 * hp:2 * hp + 2, t * P:(t + 1) * P],
                                      bank[4 + u % 2][:, 0:256].rearrange("p (h q) -> p h q", h=2)).then_inc(co_evac, 1)

            for u in range(NC_ + 2):
                if u < NC_:
                    maxes(u)
                if 1 <= u <= NC_:
                    normalise(u - 1)
                if u >= 2:
                    collect(u - 2)
            for n in range(2 * TT):
                dve.wait_ge(oo_full, n + 1)
                v = hres[:, n // 2, n % 2 * 512:n % 2 * 512 + 512]
                nc.vector.tensor_tensor(v, bank[6 + n % 2][:, :], v, ALU.add).then_inc(h_ready, 1)
    a5.free()
    end_stage()

    xf = mix[:, :, :].rearrange("p k s -> p (k s)").rearrange("p (t d) -> p t d", d=D)
    HK = PH * TOPK
    expert = sb("expert", [P, TT * HK], U32)
    gate = sb("gate", [P, TT, HK])
    a6 = Arena()
    scores_s = a6("scores_s", [P, TT, 2 * PH, NKEYS])
    sc_in = a6("sc_in", [P, 2, NKEYS])
    rest = a6("rest", [P, 2, NKEYS])
    top = a6("top", [P, 2, TOPK])
    topi = a6("topi", [P, 2, TOPK], U32)
    topf = a6("topf", [P, 2, TOPK])
    cand, cand2 = sdg[:, 0:TOPK * TOPK], sdg[:, TOPK * TOPK:2 * TOPK * TOPK]
    ctop = a6("ctop", [P, TOPK])
    ci = a6("ci", [P, TOPK], U32)
    cj = a6("cj", [P, 2, TOPK], U32)
    cf = a6("cf", [P, 2, TOPK])
    pick = a6("pick", [P, 2, TOPK, TOPK])
    pick2 = a6("pick2", [P, 2, TOPK, TOPK])
    ef = a6("ef", [P, 2, TOPK])
    en = a6("en", [P, TOPK])
    shifted, expd = a6("shifted", [P, TOPK]), a6("expd", [P, TOPK])
    gsum = a6("gsum", [P, 1])
    TOP_LINKS = 23

    def top_head(dve, t, h, before, chain, shift, exped):
        n_links = [0]

        def link(ins, apart=False):
            n_links[0] += 1
            ins.then_inc(chain, 1)
            dve.wait_ge(chain, before * TOP_LINKS + n_links[0])
            if apart:
                dve.sem_inc(gone_on, 1)

        def top16(src, spare, vals, idx):
            link(nc.vector.max(vals[:, 0:8], src), apart=True)
            nc.vector.max_index(idx[:, 0:8], vals[:, 0:8], src)
            link(nc.vector.match_replace(spare, vals[:, 0:8], src, -3.0e38), apart=True)
            link(nc.vector.max(vals[:, 8:16], spare), apart=True)
            link(nc.vector.max_index(idx[:, 8:16], vals[:, 8:16], spare), apart=True)

        link(nc.vector.tensor_copy(sc_in[:, :, :], scores_s[:, t, bass.ds(h * 2, 2), :]), apart=True)
        for s in range(2):
            top16(sc_in[:, s, :], rest[:, s, :], top[:, s, :], topi[:, s, :])
        link(nc.vector.tensor_tensor(cand[:, :].rearrange("p (a b) -> p a b", a=TOPK),
                                     top[:, 0, :].rearrange("p (a b) -> p a b", b=1).broadcast_to([P, TOPK, TOPK]),
                                     top[:, 1:2, :].broadcast_to([P, TOPK, TOPK]), ALU.add), apart=True)
        top16(cand[:, :], cand2[:, :], ctop[:, :], ci[:, :])
        nc.vector.tensor_scalar(shifted[:, :], ctop[:, :], ctop[:, 0:1], None, ALU.subtract).then_inc(shift, 1)
        nc.vector.tensor_copy(topf[:, :, :], topi[:, :, :])
        nc.vector.tensor_scalar(cj[:, 0, :], ci[:, :], 4, None, ALU.logical_shift_right)
        link(nc.vector.tensor_scalar(cj[:, 1, :], ci[:, :], 15, None, ALU.bitwise_and))
        link(nc.vector.tensor_copy(cf[:, :, :], cj[:, :, :]))
        places = cst[:, C_IOTA:C_IOTA + TOPK].rearrange("p (a j) -> p a j", a=1).broadcast_to([P, 2 * TOPK, TOPK])
        link(nc.vector.tensor_tensor(pick[:, :, :, :].rearrange("p s k j -> p (s k) j"),
                                     cf[:, :, :].rearrange("p s (k j) -> p (s k) j", j=1).broadcast_to([P, 2 * TOPK, TOPK]),
                                     places, ALU.is_equal))
        for s in range(2):
            ins = nc.vector.tensor_tensor(pick2[:, s, :, :], pick[:, s, :, :], topf[:, s:s + 1, :].broadcast_to([P, TOPK, TOPK]), ALU.mult)
        link(ins)
        link(nc.vector.tensor_reduce(ef[:, :, :], pick2[:, :, :, :], AX, ALU.add))
        link(nc.vector.scalar_tensor_tensor(out=en[:, :], in0=ef[:, 0, :], scalar=float(NKEYS), in1=ef[:, 1, :],
                                            op0=ALU.mult, op1=ALU.add))
        link(nc.vector.tensor_copy(expert[:, bass.ds(h * TOPK + t * HK, TOPK)], en[:, :]))
        dve.wait_ge(exped, before + 1)
        link(nc.vector.reciprocal(gsum[:, :], gsum[:, :]))
        link(nc.vector.tensor_scalar(gate[:, t, bass.ds(h * TOPK, TOPK)], expd[:, :], gsum[:, 0:1], None, ALU.mult))
        assert n_links[0] == TOP_LINKS, n_links

    def top_exp(act, before, shift, exped):
        act.wait_ge(shift, before + 1)
        nc.scalar.activation(expd[:, :], shifted[:, :], ACT.Exp, accum_out=gsum[:, 0:1]).then_inc(exped, 1)

    G = 8
    a9 = Arena()
    stage_i = a9("stage_i", [P, 2, G], U32)
    u_rows = w_big[:, :].rearrange("p (j d) -> p j d", j=G)
    v_rows = a9("v_rows", [P, G, D])
    xn7 = v_rows[:, 0:TT, :]
    dots = a9("dots", [P, 2, G])
    gel = a9("gel", [P, 2, G])
    wgt = a9("wgt", [P, 2, G])
    wdiag = gate_b[:, 0:4, :].rearrange("p a s -> p (a s)").rearrange("p (k j q) -> p k j q", k=2, j=G)
    zeros = a9("zeros", [P, P])
    out_s = gate_b[:, 4:8, :].rearrange("p a s -> p (a s)").rearrange("p (k d) -> p k d", k=2)
    gf = out_s[:, 0, :]
    gfin = w_pq[:, 0, 0:4, :].rearrange("p k c -> p (k c)")
    qp = kv_keep[:, 0:2 * SEQ].rearrange("p (k s) -> p k s", k=2)
    keys, keysT = (kv_keep[:, 2 * SEQ + i * 2 * P:2 * SEQ + (i + 1) * 2 * P].rearrange("p (s n) -> p s n", s=2) for i in range(2))
    sq9 = xnT[:, 0:2, :].rearrange("p a s -> p (a s)")
    fs = a9("fs", [P, TT, 4])
    eps_col = a9("eps_col", [P, 1])
    (gf_in, keys_in, keys_full, keys_ready, pq_full, pq_evac, ps_full, ps_evac, xf_ready) = (sem(n) for n in (
        "gf_in", "keys_in", "keys_full", "keys_ready", "pq_full", "pq_evac", "ps_full", "ps_evac", "xf_ready"))
    wpq_in = [sem("wpq_in0"), sem("wpq_in1")]
    u_in = [sem(f"u_in{j}") for j in range(G)]
    v_in = [sem(f"v_in{j}") for j in range(G)]
    (staged, dot_done, gel_done, w_done, diag_done, fin_full, z_ready, gfin_in, f_sq, f_ms, f_rt, f_chain,
     f_out, v_used) = (sem(n) for n in (
         "staged", "dot_done", "gel_done", "w_done", "diag_done", "fin_full", "z_ready", "gfin_in", "f_sq",
         "f_ms", "f_rt", "f_chain", "f_out", "v_used"))
    top_link, top_shift, top_exped = (sem(n) for n in ("top_link", "top_shift", "top_exped"))
    out_stored = [sem("out_stored0"), sem("out_stored1")]
    HALVES = 2 * PH
    first = [("p", 0), ("p", 1), ("s", 0), ("p", 2), ("s", 1), ("p", 3), ("s", 2), ("s", 3)]

    def of_head(h):
        return [("p", 2 * h)], [("p", 2 * h + 1), ("s", 2 * h), ("s", 2 * h + 1)]

    def heads_before(t, i):
        return {0: i * 2 - 1, 1: i * 2 + 2}[t] if t < 2 else i + (t * PH)

    NG = HK // G
    with nc.Block() as block:
        @block.sync
        def _(sp):
            sp.dma_start(keys[:, 0, :], peer_sub_keys_1[0]).then_inc(keys_in, 16)
            sp.dma_start(keys[:, 1, :], peer_sub_keys_2[0]).then_inc(keys_in, 16)
            sp.dma_start(gf, g_ffn.partition_broadcast(P)).then_inc(gf_in, 16)
            for b in range(2, 8):
                sp.wait_ge(pq_full, 2 * (b - 1))
                sp.dma_start(w_pq[:, b % 2, :, :], peer_w_q[0].rearrange("(k p) c -> p k c", p=P)[:, :, b * 256:(b + 1) * 256]).then_inc(wpq_in[b % 2], 16)
            sp.wait_ge(pq_full, HALVES)
            sp.dma_start(gfin, g_final.rearrange("(a d) -> a d", a=1).partition_broadcast(P)).then_inc(gfin_in, 16)
            for t in range(TT):
                sp.wait_ge(f_out, t + 1)
                sp.dma_start(out[0, t * P:(t + 1) * P, :], out_s[:, t % 2, :]).then_inc(out_stored[t % 2], 16)
            for s in out_stored:
                sp.wait_ge(s, 16 * TT // 2)

        xp_ready, xp_at = norm_transpose(block, "np", hres, TT, R_GFFN, xn7, xnT, bank[0:2])

        @block.gpsimd
        def _(pool):
            def head_rows(i, base):
                for k in range(2):
                    g = i * 2 + (k + base)
                    nc.gpsimd.tensor_copy(stage_i[:, k, :], expert[:, bass.ds(g * G, G)]).then_inc(staged, 1)
                    pool.wait_ge(staged, g + 1)
                    for rows_, table, done, used, ahead in ((u_rows, peer_u, u_in, dot_done, 1), (v_rows, peer_v, v_in, v_used, G + 1)):
                        for j in range(G):
                            pool.wait_ge(used, g * G + j + ahead)
                            pool.sem_inc(gone_on, 1)
                            pool.indirect_dma_start(rows_[:, j, :], None, table[0],
                                                    bass.IndirectOffsetOnAxis(ap=stage_i[:, k, j:j + 1], axis=0)).then_inc(done[j], 16)

            pool.wait_ge(top_link, TOP_LINKS)
            head_rows(0, 0)
            with pool.Fori(0, PH - 1) as i:
                pool.wait_ge(top_link, i * (2 * TOP_LINKS) + 2 * TOP_LINKS)
                pool.sem_inc(gone_on, 1)
                head_rows(i, 2)
            for t in range(1, TT):
                pool.wait_ge(top_link, (t + 1) * PH * TOP_LINKS)
                with pool.Fori(0, PH) as i:
                    head_rows(i, t * NG)

        @block.vector
        def _(dve):
            dve.sem_inc(dot_done, G)
            nc.vector.memset(zeros[:, :], 0.0).then_inc(z_ready, 1)
            nc.vector.memset(eps_col[:, :], EPS).then_inc(z_ready, 1)
            dve.wait_ge(gf_in, 16)
            dve.wait_ge(xp_ready, xp_at)
            for t in range(TT):
                nc.vector.tensor_tensor(xf[:, t], xn7[:, t], gf, ALU.mult).then_inc(xf_ready, 1)
            dve.wait_ge(xf_ready, TT)

            def finish(t):
                dve.wait_ge(f_rt, t + 1)
                nc.vector.reciprocal(fs[:, t, 2:3], fs[:, t, 3:4]).then_inc(f_chain, 1)
                dve.wait_ge(f_chain, t + 1)
                if t >= 2:
                    dve.wait_ge(out_stored[t % 2], 16 * (t // 2))
                for f in range(2):
                    half = slice(f * 512, (f + 1) * 512)
                    ins = nc.vector.scalar_tensor_tensor(out=out_s[:, t % 2, half], in0=bank[2 * t + f][:, :], scalar=fs[:, t, 2:3],
                                                         in1=gfin[:, half], op0=ALU.mult, op1=ALU.mult)
                ins.then_inc(f_out, 1)

            def group(t, i, k):
                g = i * 2 + (k + t * NG)
                for j in range(G):
                    dve.wait_ge(u_in[j], g * 16 + 16)
                    nc.vector.tensor_tensor_reduce(u_rows[:, j, :], u_rows[:, j, :], xf[:, t, :], 1.0, 0.0, ALU.mult,
                                                   ALU.add, dots[:, k, j:j + 1]).then_inc(dot_done, 1)
                dve.wait_ge(gel_done, g + 1)
                nc.vector.tensor_tensor(wgt[:, k, :], gel[:, k, :], gate[:, t, bass.ds(i * 2 * G + k * G, G)], ALU.mult).then_inc(w_done, 1)
                dve.wait_ge(w_done, g + 1)
                dve.wait_ge(v_used, g * G + G)
                nc.vector.tensor_tensor(wdiag[:, k, :, :], ident.rearrange("p (a q) -> p a q", a=1).broadcast_to([P, G, P]),
                                        wgt[:, k, :].rearrange("p (j a) -> p j a", a=1).broadcast_to([P, G, P]), ALU.mult).then_inc(diag_done, 1)

            dve.wait_ge(ps_evac, 2)
            top_head(dve, 0, 0, 0, top_link, top_shift, top_exped)
            with dve.Fori(0, PH - 1) as i:
                group(0, i, 0)
                dve.wait_ge(ps_evac, i * 2 + 4)
                top_head(dve, 0, i + 1, heads_before(0, i + 1), top_link, top_shift, top_exped)
                group(0, i, 1)
                top_head(dve, 1, i, heads_before(1, i), top_link, top_shift, top_exped)
            group(0, PH - 1, 0)
            top_head(dve, 1, PH - 1, 2 * PH - 1, top_link, top_shift, top_exped)
            group(0, PH - 1, 1)
            dve.wait_ge(gfin_in, 16)
            for t in range(1, TT):
                with dve.Fori(0, PH) as i:
                    if t + 1 < TT:
                        top_head(dve, t + 1, i, heads_before(t + 1, i), top_link, top_shift, top_exped)
                    group(t, i, 0)
                    group(t, i, 1)
                finish(t - 1)
            finish(TT - 1)

        @block.scalar
        def _(act):
            act.wait_ge(keys_full, 1)
            nc.scalar.activation(keysT[:, :, :], bank[2][:, 0:2 * P].rearrange("p (s n) -> p s n", s=2), ACT.Copy).then_inc(keys_ready, 1)

            def evac(kind, n):
                if kind == "p":
                    act.wait_ge(pq_full, n + 1)
                    if n >= 2:
                        act.wait_ge(ps_full, n - 1)
                    nc.scalar.activation(qp[:, n % 2, :], bank[2 + n % 2][:, :], ACT.Copy).then_inc(pq_evac, 1)
                else:
                    act.wait_ge(ps_full, n + 1)
                    nc.scalar.activation(scores_s[:, :, n, :], bank[4 + n % 2][:, :].rearrange("p (t n) -> p t n", t=TT), ACT.Copy).then_inc(ps_evac, 1)

            def gelu(t, i, k):
                act.wait_ge(dot_done, (i * 2 + (k + t * NG)) * G + 2 * G)
                nc.scalar.activation(gel[:, k, :], dots[:, k, :], ACT.Gelu).then_inc(gel_done, 1)

            def finish(t):
                act.wait_ge(fin_full, t + 1)
                for f in range(2):
                    nc.scalar.activation(sq9[:, f * 512:(f + 1) * 512], bank[2 * t + f][:, :], ACT.Square,
                                         accum_out=fs[:, t, f:f + 1]).then_inc(f_sq, 1)
                act.wait_ge(f_sq, 2 * t + 2)
                nc.scalar.activation(fs[:, t, 2:3], fs[:, t, 0:1], ACT.Identity, bias=fs[:, t, 1:2]).then_inc(f_ms, 1)
                act.wait_ge(f_ms, t + 1)
                nc.scalar.activation(fs[:, t, 3:4], fs[:, t, 2:3], ACT.Sqrt, scale=1.0 / D, bias=eps_col[:, :]).then_inc(f_rt, 1)

            for n, what in enumerate(first):
                if n == 5:
                    top_exp(act, 0, top_shift, top_exped)
                evac(*what)
            for i in range(PH):
                gelu(0, i, 0)
                if i + 1 < PH:
                    top_exp(act, heads_before(0, i + 1), top_shift, top_exped)
                else:
                    top_exp(act, 2 * PH - 1, top_shift, top_exped)
                if i + 2 < PH:
                    for what in of_head(i + 2)[0]:
                        evac(*what)
                gelu(0, i, 1)
                if i + 1 < PH:
                    top_exp(act, heads_before(1, i), top_shift, top_exped)
                if i + 2 < PH:
                    for what in of_head(i + 2)[1]:
                        evac(*what)
            act.wait_ge(z_ready, 2)
            for t in range(1, TT):
                with act.Fori(0, PH) as i:
                    if t + 1 < TT:
                        top_exp(act, heads_before(t + 1, i), top_shift, top_exped)
                    for k in range(2):
                        gelu(t, i, k)
                finish(t - 1)
            finish(TT - 1)

        @block.tensor
        def _(pe):
            pe.sem_inc(v_used, 2 * G)
            pe.wait_ge(keys_in, 32)
            for s in range(2):
                mm = nc.tensor.transpose(bank[2][:, s * P:(s + 1) * P], keys[:, s, :], ident)
            mm.then_inc(keys_full, 1)
            pe.wait_ge(xp_ready, xp_at)
            pe.wait_ge(keys_ready, 1)
            pe.wait_ge(z_ready, 1)

            def query(kind, n):
                if kind == "p":
                    if n >= 4:
                        pe.wait_ge(wpq_in[n // 2 % 2], 16 * (n // 4))
                    if n >= 2:
                        pe.wait_ge(pq_evac, n - 1)
                    for d in range(KD):
                        mm = nc.tensor.matmul(bank[2 + n % 2][:, :], w_pq[:, n // 2 % 2, d, n % 2 * P:(n % 2 + 1) * P], xnT[:, d, :],
                                              start=(d == 0), stop=(d == KD - 1))
                    mm.then_inc(pq_full, 1)
                else:
                    pe.wait_ge(pq_evac, n + 1)
                    if n >= 2:
                        pe.wait_ge(ps_evac, n - 1)
                    for t in range(TT):
                        mm = nc.tensor.matmul(bank[4 + n % 2][:, t * P:(t + 1) * P], qp[:, n % 2, t * P:(t + 1) * P],
                                              keysT[:, n % 2, :], start=True, stop=True)
                    mm.then_inc(ps_full, 1)

            def residual(t):
                for f in range(2):
                    nc.tensor.matmul(bank[2 * t + f][:, :], ident, hres[:, t, f * 512:(f + 1) * 512], start=True, stop=False,
                                     skip_group_check=True)

            def group(t, i, k):
                g = i * 2 + (k + t * NG)
                pe.wait_ge(diag_done, g + 1)
                for j in range(G):
                    pe.wait_ge(v_in[j], g * 16 + 16)
                    for f in range(2):
                        mm = nc.tensor.matmul(bank[2 * t + f][:, :], wdiag[:, k, j, :], v_rows[:, j, f * 512:(f + 1) * 512],
                                              start=False, stop=False, skip_group_check=True)
                    mm.then_inc(v_used, 1)

            def close(t):
                for f in range(2):
                    mm = nc.tensor.matmul(bank[2 * t + f][:, :], zeros[:, :], hres[:, t, f * 512:(f + 1) * 512], start=False, stop=True,
                                          skip_group_check=True)
                mm.then_inc(fin_full, 1)

            for what in first:
                query(*what)
            residual(0)
            for i in range(PH):
                for k in range(2):
                    group(0, i, k)
                    if i + 2 < PH:
                        for what in of_head(i + 2)[k]:
                            query(*what)
            close(0)
            pe.wait_ge(ps_evac, HALVES)
            for t in range(1, TT):
                residual(t)
                with pe.Fori(0, PH) as i:
                    for k in range(2):
                        group(t, i, k)
                close(t)


NAMES = ["x", "mem", "positions", "g_mix", "w_in", "attn_sinks", "rwkv_mu", "rwkv_w0", "rwkv_w2", "rwkv_a0", "rwkv_a2",
         "rwkv_g2", "rwkv_k_k", "rwkv_k_a", "rwkv_r_k", "rwkv_ln_w", "rwkv_ln_b", "w_out", "g_cross", "g_mem",
         "w_q_cross", "w_kv_cross", "w_o_cross", "g_ffn", "peer_w_q", "peer_sub_keys_1", "peer_sub_keys_2", "peer_u",
         "peer_v", "g_final"]


def kernel(**inputs):
    import numpy as _np
    import concourse.bacc as _bacc
    from concourse import mybir as _mybir
    from concourse.bass_utils import run_bass_kernel_spmd as _run

    nc = _bacc.Bacc("TRN2", target_bir_lowering=False, num_devices=1)
    arrays, args = {}, []
    for name in NAMES:
        a = _np.ascontiguousarray(inputs[name])
        arrays[f"in_{name}"] = a
        args.append(nc.dram_tensor(f"in_{name}", a.shape, _mybir.dt.from_np(a.dtype), kind="ExternalInput").ap())
    c = constants()
    arrays["const"] = c
    args.append(nc.dram_tensor("const", c.shape, F32, kind="ExternalInput").ap())
    args.append(nc.dram_tensor("out", (1, SEQ, D), F32, kind="ExternalOutput").ap())
    build(nc, *args)
    r = _run(nc, [arrays], core_ids=[0])
    return r.results[0]["out"]
```
